# Optimizing a Trainium2 kernel written in Bass

```python
import jax, jax.numpy as jnp
from jax import lax
import numpy as np

D_MODEL = 1024
BATCH = 1
SEQ = 512
DEPTH = 1

N_MIXERS = 3
RMS_EPS = 1e-6
RW_HEAD = 64
RW_HEADS = D_MODEL // RW_HEAD
RW_DECAY_LORA = 64
RW_AAA_LORA = 64
RW_GATE_LORA = 128
RW_LNX_EPS = 64e-5
RW_N_MIX = 6
SC_WIDTH = 3
LRU_WIDTH = D_MODEL
LRU_HEADS = 4
LRU_BLOCK = LRU_WIDTH // LRU_HEADS
LRU_CONV = 4
LRU_C = 8.0
N_EXPERTS = 16
EXPERT_FF = 2 * D_MODEL
CAPACITY_FACTOR = 2
N_LAYERS_A = (DEPTH + N_MIXERS - 1) // N_MIXERS
N_LAYERS_B = (DEPTH + N_MIXERS - 2) // N_MIXERS
N_LAYERS_C = DEPTH // N_MIXERS

kernel_name = "hybrid_rwkv7_shortconv_rglru_ecmoe_encoder"

def rms_norm(x, g):
    xf = x.astype(jnp.float32)
    y = xf * lax.rsqrt(jnp.mean(xf * xf, axis=-1, keepdims=True) + RMS_EPS)
    return (y * g.astype(jnp.float32)).astype(x.dtype)

def centred_shift(x):
    prev = jnp.pad(x[:, :-1], ((0, 0), (1, 0), (0, 0)))
    nxt = jnp.pad(x[:, 1:], ((0, 0), (0, 1), (0, 0)))
    return 0.5 * (prev + nxt)

def depthwise_conv(x, w, pad_left, pad_right):
    return lax.conv_general_dilated(
        x, w.astype(x.dtype)[:, None, :], window_strides=(1,),
        padding=[(pad_left, pad_right)], dimension_numbers=('NWC', 'WIO', 'NWC'),
        feature_group_count=x.shape[-1])

def rwkv7_scan(r, w, k, v, kk, a, reverse):
    bsz, _, nh, n = r.shape

    def step(state, inp):
        r_t, w_t, k_t, v_t, kk_t, a_t = inp
        sa = jnp.einsum('bhvk,bhk->bhv', state, kk_t)
        state = (state * w_t[:, :, None, :]
                 - sa[..., None] * (kk_t * a_t)[:, :, None, :]
                 + v_t[..., None] * k_t[:, :, None, :])
        return state, jnp.einsum('bhvk,bhk->bhv', state, r_t)

    xs = tuple(jnp.moveaxis(t, 1, 0) for t in (r, w, k, v, kk, a))
    s0 = jnp.zeros((bsz, nh, n, n), jnp.float32)
    _, ys = lax.scan(step, s0, xs, reverse=reverse)
    return jnp.moveaxis(ys, 0, 1)

def rwkv7_mixer(h, mu, w_in, w0, w1, w2, a0, a1, a2, g1, g2, k_k, k_a, r_k, lnx_g, lnx_b, w_out):
    bsz, seq, d = h.shape
    f32 = jnp.float32
    xx = centred_shift(h) - h
    xm = h[None] + xx[None] * mu[:, None, None, :]
    r, k, v = jnp.einsum('pbsd,pde->pbse', xm[:3], w_in)
    x_w, x_a, x_g = xm[3], xm[4], xm[5]
    lora_w = jnp.einsum('zbsr,zrd->zbsd', jnp.tanh(jnp.einsum('bsd,zdr->zbsr', x_w, w1)), w2)
    w_log = -jax.nn.softplus(-(w0[:, None, None, :] + lora_w).astype(f32)) - 0.5
    decay = jnp.exp(-jnp.exp(w_log))
    lora_a = jnp.einsum('zbsr,zrd->zbsd', jnp.einsum('bsd,zdr->zbsr', x_a, a1), a2)
    a = jax.nn.sigmoid((a0[:, None, None, :] + lora_a).astype(f32))
    g = jnp.einsum('bsr,rd->bsd', jax.nn.sigmoid(jnp.einsum('bsd,dr->bsr', x_g, g1)), g2)

    def heads(t):
        return t.reshape(t.shape[:-1] + (RW_HEADS, RW_HEAD))

    r_h = heads(r.astype(f32))
    v_h = heads(v.astype(f32))
    kk = heads((k * k_k).astype(f32))
    kk = kk / jnp.maximum(jnp.sqrt(jnp.sum(kk * kk, axis=-1, keepdims=True)), 1e-12)
    k_dir = heads(k.astype(f32)[None] * (1.0 + (a - 1.0) * k_a.astype(f32)))
    a_h = heads(a)
    decay_h = heads(decay)
    y = (rwkv7_scan(r_h, decay_h[0], k_dir[0], v_h, kk, a_h[0], reverse=False)
         + rwkv7_scan(r_h, decay_h[1], k_dir[1], v_h, kk, a_h[1], reverse=True))
    mean = jnp.mean(y, axis=-1, keepdims=True)
    var = jnp.mean(jnp.square(y - mean), axis=-1, keepdims=True)
    y = ((y - mean) * lax.rsqrt(var + RW_LNX_EPS)).reshape(bsz, seq, d)
    y = y * lnx_g.astype(f32) + lnx_b.astype(f32)
    bonus = jnp.sum(r_h[None] * k_dir * r_k.astype(f32), axis=-1, keepdims=True) * v_h[None]
    y = y + jnp.sum(bonus, axis=0).reshape(bsz, seq, d)
    return jnp.einsum('bsd,de->bse', y.astype(h.dtype) * g, w_out)

def short_conv_mixer(h, w_in, conv_w, w_out):
    bcu = jnp.einsum('bsd,de->bse', h, w_in)
    b_gate, c_gate, u = jnp.split(bcu, 3, axis=-1)
    z = depthwise_conv(c_gate * u, conv_w, 1, 1)
    return jnp.einsum('bse,ed->bsd', b_gate * z, w_out)

def linear_scan(a, b):
    def combine(e1, e2):
        a1, b1 = e1
        a2, b2 = e2
        return a1 * a2, a2 * b1 + b2
    _, hs = lax.associative_scan(combine, (a, b), axis=1)
    return hs

def rglru_mixer(h, w_in, conv_w, conv_b, w_a, b_a, w_x, b_x, lam, w_out):
    bsz, seq, _ = h.shape
    f32 = jnp.float32
    gu = jnp.einsum('bsd,de->bse', h, w_in)
    gate, u = jnp.split(gu, 2, axis=-1)
    gate = jax.nn.gelu(gate)
    u = depthwise_conv(u, conv_w, 2, 1) + conv_b
    uh = u.reshape(bsz, seq, LRU_HEADS, LRU_BLOCK)
    r_gate = jax.nn.sigmoid((jnp.einsum('bshi,zhij->zbshj', uh, w_a).reshape(2, bsz, seq, LRU_WIDTH)
                             + b_a[:, None, None, :]).astype(f32))
    i_gate = jax.nn.sigmoid((jnp.einsum('bshi,zhij->zbshj', uh, w_x).reshape(2, bsz, seq, LRU_WIDTH)
                             + b_x[:, None, None, :]).astype(f32))
    log_a = -LRU_C * r_gate * jax.nn.softplus(-lam.astype(f32))[:, None, None, :]
    a = jnp.exp(log_a)
    b = jnp.sqrt(-jnp.expm1(2.0 * log_a)) * (i_gate * u.astype(f32)[None])
    h_fwd = linear_scan(a[0], b[0])
    h_bwd = jnp.flip(linear_scan(jnp.flip(a[1], axis=1), jnp.flip(b[1], axis=1)), axis=1)
    y = (h_fwd + h_bwd).astype(h.dtype) * gate
    return jnp.einsum('bse,ed->bsd', y, w_out)

def expert_choice_moe(h, router_w, w_gate, w_up, w_down):
    bsz, seq, _ = h.shape
    cap = CAPACITY_FACTOR * seq // N_EXPERTS
    logits = jnp.einsum('bsd,de->bse', h, router_w).astype(jnp.float32)
    aff = jax.nn.softmax(logits, axis=-1)
    gates, idx = lax.top_k(jnp.swapaxes(aff, 1, 2), cap)
    bidx = jnp.arange(bsz)[:, None, None]
    xin = h[bidx, idx]
    hid = (jax.nn.silu(jnp.einsum('becd,edf->becf', xin, w_gate))
           * jnp.einsum('becd,edf->becf', xin, w_up))
    yexp = jnp.einsum('becf,efd->becd', hid, w_down) * gates[..., None].astype(h.dtype)
    return jnp.zeros_like(h).at[bidx, idx].add(yexp)

def setup_inputs(seed: int = 0) -> dict:
    key = jax.random.key(seed)
    keys = iter(jax.random.split(key, 48))
    f32 = jnp.float32
    D, E, F = D_MODEL, N_EXPERTS, EXPERT_FF

    def nrm(shape, scale):
        return scale * jax.random.normal(next(keys), shape, f32)

    def uni(shape, lo, hi):
        return jax.random.uniform(next(keys), shape, f32, minval=lo, maxval=hi)

    inp = {}
    inp['x'] = nrm((BATCH, SEQ, D), 1.0)
    inp['norm_mix_g'] = 1.0 + nrm((DEPTH, D), 0.02)
    inp['norm_ffn_g'] = 1.0 + nrm((DEPTH, D), 0.02)
    inp['router_w'] = nrm((DEPTH, D, E), D ** -0.5)
    inp['exp_w_gate'] = nrm((DEPTH, E, D, F), D ** -0.5)
    inp['exp_w_up'] = nrm((DEPTH, E, D, F), D ** -0.5)
    inp['exp_w_down'] = nrm((DEPTH, E, F, D), F ** -0.5)
    inp['final_norm_g'] = 1.0 + nrm((D,), 0.02)
    inp['rw_mu'] = uni((N_LAYERS_A, RW_N_MIX, D), 0.0, 1.0)
    inp['rw_w_in'] = nrm((N_LAYERS_A, 3, D, D), D ** -0.5)
    inp['rw_w0'] = uni((N_LAYERS_A, 2, D), -7.0, 0.0)
    inp['rw_w1'] = nrm((N_LAYERS_A, 2, D, RW_DECAY_LORA), D ** -0.5)
    inp['rw_w2'] = nrm((N_LAYERS_A, 2, RW_DECAY_LORA, D), 0.1 * RW_DECAY_LORA ** -0.5)
    inp['rw_a0'] = nrm((N_LAYERS_A, 2, D), 0.5)
    inp['rw_a1'] = nrm((N_LAYERS_A, 2, D, RW_AAA_LORA), D ** -0.5)
    inp['rw_a2'] = nrm((N_LAYERS_A, 2, RW_AAA_LORA, D), 0.1 * RW_AAA_LORA ** -0.5)
    inp['rw_g1'] = nrm((N_LAYERS_A, D, RW_GATE_LORA), D ** -0.5)
    inp['rw_g2'] = nrm((N_LAYERS_A, RW_GATE_LORA, D), RW_GATE_LORA ** -0.5)
    inp['rw_k_k'] = 0.85 + nrm((N_LAYERS_A, D), 0.02)
    inp['rw_k_a'] = 1.0 + nrm((N_LAYERS_A, D), 0.02)
    inp['rw_r_k'] = nrm((N_LAYERS_A, RW_HEADS, RW_HEAD), 0.1)
    inp['rw_lnx_g'] = 1.0 + nrm((N_LAYERS_A, D), 0.02)
    inp['rw_lnx_b'] = nrm((N_LAYERS_A, D), 0.02)
    inp['rw_w_out'] = nrm((N_LAYERS_A, D, D), D ** -0.5)
    inp['sc_w_in'] = nrm((N_LAYERS_B, D, 3 * D), D ** -0.5)
    inp['sc_conv_w'] = nrm((N_LAYERS_B, SC_WIDTH, D), SC_WIDTH ** -0.5)
    inp['sc_w_out'] = nrm((N_LAYERS_B, D, D), D ** -0.5)
    inp['lru_w_in'] = nrm((N_LAYERS_C, D, 2 * LRU_WIDTH), D ** -0.5)
    inp['lru_conv_w'] = nrm((N_LAYERS_C, LRU_CONV, LRU_WIDTH), LRU_CONV ** -0.5)
    inp['lru_conv_b'] = nrm((N_LAYERS_C, LRU_WIDTH), 0.01)
    inp['lru_w_a'] = nrm((N_LAYERS_C, 2, LRU_HEADS, LRU_BLOCK, LRU_BLOCK), LRU_BLOCK ** -0.5)
    inp['lru_b_a'] = nrm((N_LAYERS_C, 2, LRU_WIDTH), 0.01)
    inp['lru_w_x'] = nrm((N_LAYERS_C, 2, LRU_HEADS, LRU_BLOCK, LRU_BLOCK), LRU_BLOCK ** -0.5)
    inp['lru_b_x'] = nrm((N_LAYERS_C, 2, LRU_WIDTH), 0.01)
    a_c = uni((N_LAYERS_C, 2, LRU_WIDTH), 0.9, 0.999)
    s = a_c ** (1.0 / LRU_C)
    inp['lru_lambda'] = jnp.log(s) - jnp.log1p(-s)
    inp['lru_w_out'] = nrm((N_LAYERS_C, LRU_WIDTH, D), LRU_WIDTH ** -0.5)
    return inp

def reference(x, norm_mix_g, norm_ffn_g, router_w, exp_w_gate, exp_w_up, exp_w_down, final_norm_g,
              rw_mu, rw_w_in, rw_w0, rw_w1, rw_w2, rw_a0, rw_a1, rw_a2, rw_g1, rw_g2,
              rw_k_k, rw_k_a, rw_r_k, rw_lnx_g, rw_lnx_b, rw_w_out,
              sc_w_in, sc_conv_w, sc_w_out,
              lru_w_in, lru_conv_w, lru_conv_b, lru_w_a, lru_b_a, lru_w_x, lru_b_x, lru_lambda, lru_w_out):
    ia, ib, ic = 0, 0, 0
    for i in range(DEPTH):
        h = rms_norm(x, norm_mix_g[i])
        m = i % N_MIXERS
        if m == 0:
            y = rwkv7_mixer(h, rw_mu[ia], rw_w_in[ia], rw_w0[ia], rw_w1[ia], rw_w2[ia],
                            rw_a0[ia], rw_a1[ia], rw_a2[ia], rw_g1[ia], rw_g2[ia],
                            rw_k_k[ia], rw_k_a[ia], rw_r_k[ia], rw_lnx_g[ia], rw_lnx_b[ia], rw_w_out[ia])
            ia += 1
        elif m == 1:
            y = short_conv_mixer(h, sc_w_in[ib], sc_conv_w[ib], sc_w_out[ib])
            ib += 1
        else:
            y = rglru_mixer(h, lru_w_in[ic], lru_conv_w[ic], lru_conv_b[ic], lru_w_a[ic], lru_b_a[ic],
                            lru_w_x[ic], lru_b_x[ic], lru_lambda[ic], lru_w_out[ic])
            ic += 1
        x = x + y
        h = rms_norm(x, norm_ffn_g[i])
        x = x + expert_choice_moe(h, router_w[i], exp_w_gate[i], exp_w_up[i], exp_w_down[i])
    return rms_norm(x, final_norm_g)


_drawn_inputs = setup_inputs


def setup_inputs(seed=0):
    import zlib

    import numpy as np

    out = dict(_drawn_inputs(seed))
    spreads = {}
    factors = {'norm_ffn_g': 4.217,
     'final_norm_g': 2.869,
     'rw_w1': 8.0,
     'rw_w2': 8.0,
     'rw_a1': 2.774,
     'rw_a2': 2.883,
     'rw_k_k': 3.961,
     'rw_k_a': 3.253,
     'rw_lnx_g': 3.988,
     'rw_lnx_b': 5.151}
    for name, (base, spread) in spreads.items():
        noise = np.random.default_rng([zlib.crc32(name.encode()), seed]).standard_normal(out[name].shape)
        drawn = base * np.exp(spread * noise) if base else spread * noise
        out[name] = __import__('jax').numpy.asarray(drawn.astype(out[name].dtype))
    for name, factor in factors.items():
        out[name] = (out[name] * factor).astype(out[name].dtype)
    return out
```

```python
from contextlib import ExitStack

import numpy as np

import concourse.bass as bass
from concourse import mybir

F32 = mybir.dt.float32
ALU = mybir.AluOpType
ACT = mybir.ActivationFunctionType
AX_X = mybir.AxisListType.X

P = 128
D = 1024
SEQ = 512
TILES = SEQ // P
DC = D // P
HEAD = 64
HEADS = D // HEAD
HALF = 512
LORA = 64
EXPERTS = 16
CAP = 2 * SEQ // EXPERTS
FF = 2048
EPS = 1e-6
LNX_EPS = 64e-5
DECAY = float(np.exp(-0.5))
LEVELS = 6
QUADS = HEADS // 4

C_ID, C_CUM, C_SCORE, C_LEVEL, C_TRI, C_ONES, C_HEAD, C_SEL, C_IOTA, C_END = np.cumsum(
    [0, P, 4 * P, 8 * P, 7 * P, P, P, P, 4, CAP]).tolist()
V_NORM, V_MU, V_A0, V_KK, V_KA, V_RK, V_END = np.cumsum([0, 1, 6, 2, 1, 1, 1]).tolist()


def constants():
    s, t = np.arange(P)[:, None], np.arange(P)[None, :]
    low = (s < P // 2) * 1.0
    cum = [(s <= t) - low, (s < t) - low, (s >= t) - (1 - low), (s > t) - (1 - low)]
    score = []
    for strict, incl in ((s < t, s <= t), (s > t, s >= t)):
        score += [-1.0 * strict, 1.0 * incl, 1.0 * strict, 1.0 * incl]
    level = [(s // (2 * m) == t // (2 * m)) & (s // m != t // m) for m in (1, 2, 4, 8, 16, 32, 64)]
    sel = (s // HEAD == np.arange(4)[None, :]) * 1.0
    iota = np.broadcast_to(np.arange(CAP)[None, :], (P, CAP))
    parts = [s == t, *cum, *score, *level, s <= t, np.ones((P, P)), s // HEAD == t // HEAD, sel, iota]
    return np.ascontiguousarray(np.concatenate([np.asarray(a, np.float32) for a in parts], axis=1))


class Chain:

    def __init__(self, eng, sem, base=0):
        self.eng, self.sem, self.base, self.n = eng, sem, base, 0

    def link(self, ins):
        ins.then_inc(self.sem, 1)
        self.n += 1
        self.eng.wait_ge(self.sem, self.base + self.n)


def wait_alone(eng, sem, value, tick):
    eng.wait_ge(sem, value)
    eng.sem_inc(tick, 1)


def build_trunk(nc, io, out):
    scr = {
        name: nc.dram_tensor(f"scratch_{name}", shape, F32, kind="Internal").ap()
        for name, shape in {
            "r": [TILES, P, DC, P], "kk": [TILES, P, DC, P], "bz": [2, TILES, P, DC, P],
            "kd": [2, TILES, P, DC, P], "sw": [2, TILES, P, D], "v": [TILES, P, D],
        }.items()
    }
    with ExitStack() as ctx:
        keep = {
            "con": ctx.enter_context(nc.sbuf_tensor("con", [P, C_END], F32)),
            "vec": ctx.enter_context(nc.sbuf_tensor("vec", [P, V_END, DC], F32)),
            "gate_low": ctx.enter_context(nc.sbuf_tensor("gate_low", [P, SEQ], F32)),
            "bonus": ctx.enter_context(nc.sbuf_tensor("bonus", [P, TILES, HEADS], F32)),
        }
        mix_inputs(nc, io, scr, keep)
        with nc.sbuf_tensor("y", [P, TILES, D], F32) as y:
            keep["y"] = y
            recurrence(nc, scr, keep)
            with ExitStack() as moe:
                for name, shape in (("res", [P, TILES, D]), ("slot", [P, TILES, EXPERTS]), ("aff", [P, TILES, EXPERTS]),
                                    ("ring", [P, 3, 8, D])):
                    keep[name] = moe.enter_context(nc.sbuf_tensor(name, shape, F32))
                keep["landed"] = [moe.enter_context(nc.semaphore(f"weights_landed{k}")) for k in range(3)]
                mix_output(nc, io, scr, keep)
                experts(nc, io, keep)
                final_norm(nc, io, keep, out)


def mix_inputs(nc, io, scr, keep):
    con, vec = keep["con"], keep["vec"]
    ident = con[:, C_ID:C_ID + P]
    with ExitStack() as ctx:
        def sb(name, *shape):
            return ctx.enter_context(nc.sbuf_tensor(name, list(shape), F32))

        def sem(name):
            return ctx.enter_context(nc.semaphore(name))

        x_in = sb("x_in", P, 2, D)
        hT = sb("hT", P, DC, SEQ + 2)
        shift = sb("shift", P, DC, SEQ)
        xm = [sb(f"xm{i}", P, DC, SEQ) for i in range(2)]
        w_ring = sb("w_ring", P, 2, 2, DC, 256)
        low_w = sb("low_w", P, 3, DC, P)
        up_w = sb("up_w", P, 2, D)
        w0_row = sb("w0_row", P, 2, D)
        tw, xa = sb("tw", P, SEQ), sb("xa", P, SEQ)
        tok = sb("tok", P, 2, D)
        kT, rT = sb("kT", P, SEQ), sb("rT", P, SEQ)
        sq, rn, kk = sb("sq", P, SEQ), sb("rn", P, SEQ), sb("kk", P, SEQ)
        aT, kd, bz = sb("aT", P, 2, SEQ), sb("kd", P, 2, SEQ), sb("bz", P, 2, SEQ)
        ts, rk = sb("ts", P, SEQ), sb("rk", P, SEQ)
        stat = sb("stat", P, 3, TILES)
        ps = [ctx.enter_context(nc.psum_tensor(f"mi_ps{i}", [P, HALF], F32)) for i in range(8)]

        x_load = [sem(f"x_load{i}") for i in range(2)]
        con_load, low_load, row_load = sem("con_load"), sem("low_load"), sem("row_load")
        sq_done, root_done, h_done = sem("sq_done"), sem("root_done"), sem("h_done")
        turned, hT_done, xm_done = sem("turned"), sem("hT_done"), sem("xm_done")
        chain_s = sem("mi_chain")
        low_mm, low_ev = sem("low_mm"), sem("low_ev")
        sw_mm, sw_sum, sw_done = sem("sw_mm"), sem("sw_sum"), sem("sw_done")
        sw_out = [sem(f"sw_out{i}") for i in range(2)]
        v_out = [sem(f"v_out{i}") for i in range(2)]
        w_load = [sem(f"w_load{i}") for i in range(2)]
        wv_load = sem("wv_load")
        proj_mm, kr_ev, sq_ev = sem("proj_mm"), sem("kr_ev"), sem("sq_ev")
        norm_mm, norm_max, norm_root, kk_done = sem("norm_mm"), sem("norm_max"), sem("norm_root"), sem("kk_done")
        a_mm, a_ev, keys_done, rk_done = sem("a_mm"), sem("a_ev"), sem("keys_done"), sem("rk_done")
        bonus_mm, bonus_ev, chunk_out = sem("bonus_mm"), sem("bonus_ev"), sem("chunk_out")
        v_mm, v_ev = sem("v_mm"), sem("v_ev")

        x_t = io["x"].rearrange("b (t p) d -> (b t) p d", p=P)
        w_in = io["rw_w_in"].rearrange("a m (c p) e -> (a m) p c e", p=P)
        LOW = (3, 4, 5)

        def bonus_products(pe, c):
            pe.wait_ge(rk_done, c + 1)
            if c:
                pe.wait_ge(bonus_ev, c)
            for t in range(TILES):
                last = pe.matmul(ps[7][:, 4 * t:4 * t + 4], rk[:, P * t:P * t + P], con[:, C_SEL:C_SEL + 4], start=True, stop=True)
            last.then_inc(bonus_mm, 1)

        def bonus_copy(dve, c):
            dve.wait_ge(bonus_mm, c + 1)
            dve.tensor_copy(keep["bonus"][:, :, 2 * c:2 * c + 2],
                            ps[7][:, 0:4 * TILES].rearrange("p (t h) -> p t h", h=4)[:, :, 0:2]).then_inc(bonus_ev, 1)

        block = ctx.enter_context(nc.Block())

        @block.sync
        def _(sp):
            for t in range(TILES):
                if t >= 2:
                    sp.wait_ge(h_done, t - 1)
                    sp.wait_ge(turned, 2 * (t - 1))
                sp.dma_start(x_in[:, t % 2, :], x_t[t]).then_inc(x_load[t % 2], 16)
            for q in range(4):
                if q >= 2:
                    sp.wait_ge(proj_mm, 4 * (q - 1))
                for m, which in enumerate((1, 0)):
                    sp.dma_start(w_ring[:, q % 2, m], w_in[which][:, :, 256 * q:256 * q + 256]).then_inc(w_load[q % 2], 16)
            sp.wait_ge(proj_mm, 16)
            for h in range(2):
                sp.dma_start(w_ring[:, h].rearrange("p m c e -> p (m c e)").rearrange("p (c e) -> p c e", c=DC),
                             w_in[2][:, :, HALF * h:HALF * h + HALF]).then_inc(wv_load, 16)
            for t in range(TILES):
                sp.wait_ge(v_ev, 2 * t + 2)
                sp.dma_start(scr["v"][t], tok[:, t % 2, :]).then_inc(v_out[t % 2], 16)
            for k in range(2):
                sp.wait_ge(sw_out[k], 16 * TILES)
                sp.wait_ge(v_out[k], 16 * TILES // 2)
            sp.wait_ge(chunk_out, 16 * 6 * DC)

        @block.gpsimd
        def _(pool):
            pool.dma_start(con[:, :], io["consts"]).then_inc(con_load, 16)
            pool.dma_start(vec[:, :, :], io["vectors"]).then_inc(con_load, 16)
            for i, name in enumerate(("rw_w1", "rw_a1")):
                for z in range(2):
                    pool.dma_start(low_w[:, i, :, LORA * z:LORA * z + LORA],
                                   io[name][0, z].rearrange("(c p) r -> p c r", p=P)).then_inc(low_load, 16)
            pool.dma_start(low_w[:, 2], io["rw_g1"][0].rearrange("(c p) r -> p c r", p=P)).then_inc(low_load, 16)
            for i, name in enumerate(("rw_w2", "rw_a2")):
                pool.dma_start(up_w[:, i, :], io[name].rearrange("a z r d -> (a z r) d")).then_inc(low_load, 16)
            for z in range(2):
                pool.dma_start(w0_row[:, z, :], io["rw_w0"][0, z].partition_broadcast(P)).then_inc(row_load, 16)
            for u in range(2 * TILES):
                pool.wait_ge(sw_done, u + 1)
                pool.dma_start(scr["sw"][u // TILES, u % TILES], tok[:, u % 2, :]).then_inc(sw_out[u % 2], 16)
            for c in range(DC):
                def spill(name, z, src):
                    dst = scr[name] if z is None else scr[name][z]
                    pool.dma_start(dst[:, :, c, :].rearrange("t p s -> p t s"),
                                   src.rearrange("p (t s) -> p t s", s=P)).then_inc(chunk_out, 16)
                pool.wait_ge(kr_ev, 2 * c + 2)
                spill("r", None, rT[:, :])
                pool.wait_ge(kk_done, c + 1)
                spill("kk", None, kk[:, :])
                pool.wait_ge(keys_done, c + 1)
                for z in range(2):
                    spill("bz", z, bz[:, z, :])
                    spill("kd", z, kd[:, z, :])

        @block.scalar
        def _(act):
            for t in range(TILES):
                act.wait_ge(x_load[t % 2], 16 * (t // 2 + 1))
                act.activation(shift[:, 2 * t:2 * t + 2, :].rearrange("p a b -> p (a b)"), x_in[:, t % 2, :], ACT.Square,
                               accum_out=stat[:, 0, t:t + 1]).then_inc(sq_done, 1)
                act.wait_ge(norm_max, t + 1)
                act.activation(stat[:, 1, t:t + 1], stat[:, 2, t:t + 1], ACT.Sqrt).then_inc(root_done, 1)
            for i, (dst, fn) in enumerate(((tw, ACT.Tanh), (xa, ACT.Copy), (keep["gate_low"], ACT.Sigmoid))):
                act.wait_ge(low_mm, i + 1)
                act.activation(dst[:, :], ps[i % 2][:, :], fn).then_inc(low_ev, 1)
            for u in range(2 * TILES):
                act.wait_ge(sw_sum, 2 * u + 2)
                act.activation(tok[:, u % 2, :], tok[:, u % 2, :], ACT.Sigmoid).then_inc(sw_done, 1)
            for c in range(DC):
                act.wait_ge(proj_mm, 2 * c + 1)
                if c:
                    act.wait_ge(keys_done, c)
                act.activation(kT[:, :], ps[2][:, :], ACT.Copy).then_inc(kr_ev, 1)
                act.activation(sq[:, :], ps[2][:, :], ACT.Square, scale=vec[:, V_KK, c:c + 1]).then_inc(sq_ev, 1)
                for z in range(2):
                    act.wait_ge(a_mm, 2 * c + z + 1)
                    act.activation(aT[:, z, :], ps[4 + z][:, :], ACT.Sigmoid,
                                   bias=vec[:, V_A0 + z, c:c + 1]).then_inc(a_ev, 1)
                act.wait_ge(norm_max, TILES + c + 1)
                act.activation(rn[:, :], sq[:, :], ACT.Sqrt).then_inc(norm_root, 1)
                act.wait_ge(proj_mm, 2 * c + 2)
                if c:
                    act.wait_ge(chunk_out, 16 * 6 * c)
                    act.wait_ge(rk_done, c)
                act.activation(rT[:, :], ps[3][:, :], ACT.Copy).then_inc(kr_ev, 1)
            for t in range(TILES):
                act.wait_ge(sw_out[t % 2], 16 * TILES)
                if t >= 2:
                    act.wait_ge(v_out[t % 2], 16 * (t // 2))
                for h in range(2):
                    act.wait_ge(v_mm, 2 * t + h + 1)
                    act.activation(tok[:, t % 2, HALF * h:HALF * h + HALF], ps[h][:, :], ACT.Copy).then_inc(v_ev, 1)

        @block.tensor
        def _(pe):
            pe.wait_ge(con_load, 32)
            for t in range(TILES):
                pe.wait_ge(h_done, t + 1)
                for g in range(2):
                    if t:
                        pe.wait_ge(hT_done, 2 * t + g - 1)
                    for c in range(4):
                        last = pe.transpose(ps[g][:, P * c:P * c + P], x_in[:, t % 2, P * (4 * g + c):P * (4 * g + c + 1)], ident)
                    last.then_inc(turned, 1)
            pe.wait_ge(low_load, 16 * 7)
            for i in range(3):
                pe.wait_ge(xm_done, i + 1)
                if i < 2:
                    pe.wait_ge(hT_done, 2 * TILES)
                else:
                    pe.wait_ge(low_ev, 1)
                for c in range(DC):
                    last = pe.matmul(ps[i % 2][:, :], low_w[:, i, c, :], xm[i % 2][:, c, :], start=c == 0, stop=c == DC - 1)
                last.then_inc(low_mm, 1)
            for u in range(2 * TILES):
                z, t = u // TILES, u % TILES
                for h in range(2):
                    pe.wait_ge(low_ev, 3)
                    if u:
                        pe.wait_ge(sw_sum, 2 * u + h - 1)
                    pe.matmul(ps[h][:, :], tw[LORA * z:LORA * z + LORA, P * t:P * t + P],
                              up_w[LORA * z:LORA * z + LORA, 0, HALF * h:HALF * h + HALF], start=True, stop=True).then_inc(sw_mm, 1)
            for c in range(DC):
                q = c // 2
                pe.wait_ge(w_load[q % 2], 32 * (q // 2 + 1))
                pe.wait_ge(xm_done, 5)
                for m in range(2):
                    if c:
                        pe.wait_ge(kr_ev, 2 * (c - 1) + m + 1)
                        pe.wait_ge(sq_ev, c)
                    for k in range(DC):
                        last = pe.matmul(ps[2 + m][:, :], w_ring[:, q % 2, m, k, P * (c % 2):P * (c % 2) + P],
                                         xm[(3 + m) % 2][:, k, :], start=k == 0, stop=k == DC - 1)
                    last.then_inc(proj_mm, 1)
                    if m == 0:
                        for z in range(2):
                            if c:
                                pe.wait_ge(a_ev, 2 * (c - 1) + z + 1)
                            pe.matmul(ps[4 + z][:, :], up_w[LORA * z:LORA * z + LORA, 1, P * c:P * c + P],
                                      xa[LORA * z:LORA * z + LORA, :], start=True, stop=True).then_inc(a_mm, 1)
                pe.wait_ge(sq_ev, c + 1)
                if c:
                    pe.wait_ge(norm_max, TILES + c)
                pe.matmul(ps[6][:, :], con[:, C_HEAD:C_HEAD + P], sq[:, :], start=True, stop=True).then_inc(norm_mm, 1)
                if c:
                    bonus_products(pe, c - 1)
            pe.wait_ge(wv_load, 32)
            pe.wait_ge(xm_done, 6)
            for t in range(TILES):
                for h in range(2):
                    if t:
                        pe.wait_ge(v_ev, 2 * t + h - 1)
                    wv = w_ring[:, h].rearrange("p m c e -> p (m c e)").rearrange("p (c e) -> p c e", c=DC)
                    for k in range(DC):
                        last = pe.matmul(ps[h][:, :], xm[1][:, k, P * t:P * t + P], wv[:, k, :], start=k == 0, stop=k == DC - 1)
                    last.then_inc(v_mm, 1)
                if t == 0:
                    bonus_products(pe, DC - 1)

        @block.vector
        def _(dve):
            chain = Chain(dve, chain_s)
            dve.memset(hT[:, :, 0:1], 0.0)
            dve.memset(hT[:, :, SEQ + 1:SEQ + 2], 0.0)
            for t in range(TILES):
                dve.wait_ge(sq_done, t + 1)
                dve.tensor_scalar(stat[:, 2, t:t + 1], stat[:, 0, t:t + 1], 1.0 / D, EPS, ALU.mult, ALU.add).then_inc(norm_max, 1)
                dve.wait_ge(root_done, t + 1)
                chain.link(dve.reciprocal(stat[:, 1, t:t + 1], stat[:, 1, t:t + 1]))
                dve.tensor_scalar(x_in[:, t % 2, :], x_in[:, t % 2, :], stat[:, 1, t:t + 1], None, ALU.mult).then_inc(h_done, 1)
                if t == 0:
                    dve.wait_ge(con_load, 32)
                for g in range(2):
                    dve.wait_ge(turned, 2 * t + g + 1)
                    dve.tensor_tensor(hT[:, 4 * g:4 * g + 4, 1 + P * t:1 + P * t + P], ps[g][:, :].rearrange("p (c s) -> p c s", s=P),
                                      vec[:, V_NORM, 4 * g:4 * g + 4].unsqueeze(2).to_broadcast([P, 4, P]), ALU.mult).then_inc(hT_done, 1)
            dve.wait_ge(hT_done, 2 * TILES)
            for c in range(DC):
                chain.link(dve.tensor_tensor(shift[:, c, :], hT[:, c, 0:SEQ], hT[:, c, 2:SEQ + 2], ALU.add))
                chain.link(dve.scalar_tensor_tensor(out=shift[:, c, :], in0=shift[:, c, :], scalar=0.5, in1=hT[:, c, 1:SEQ + 1],
                                                    op0=ALU.mult, op1=ALU.subtract))

            def mix(i, which):
                for c in range(DC):
                    last = dve.scalar_tensor_tensor(out=xm[i % 2][:, c, :], in0=shift[:, c, :], scalar=vec[:, V_MU + which, c:c + 1],
                                                    in1=hT[:, c, 1:SEQ + 1], op0=ALU.mult, op1=ALU.add)
                last.then_inc(xm_done, 1)

            mix(0, 3)
            mix(1, 4)
            dve.wait_ge(low_mm, 1)
            mix(2, 5)
            dve.wait_ge(low_mm, 2)
            mix(3, 1)
            dve.wait_ge(low_mm, 3)
            mix(4, 0)
            dve.wait_ge(row_load, 32)
            for u in range(2 * TILES):
                for h in range(2):
                    dve.wait_ge(sw_mm, 2 * u + h + 1)
                    if u >= 2:
                        dve.wait_ge(sw_out[u % 2], 16 * (u // 2))
                    cols = slice(HALF * h, HALF * h + HALF)
                    dve.tensor_tensor(tok[:, u % 2, cols], ps[h][:, :], w0_row[:, u // TILES, cols], ALU.add).then_inc(sw_sum, 1)
            for c in range(DC):
                dve.wait_ge(norm_mm, c + 1)
                dve.tensor_scalar(sq[:, :], ps[6][:, :], 1e-24, None, ALU.max).then_inc(norm_max, 1)
                dve.wait_ge(norm_root, c + 1)
                chain.link(dve.reciprocal(rn[:, :], rn[:, :]))
                if c:
                    dve.wait_ge(chunk_out, 16 * 6 * c)
                dve.scalar_tensor_tensor(out=kk[:, :], in0=kT[:, :], scalar=vec[:, V_KK, c:c + 1], in1=rn[:, :],
                                         op0=ALU.mult, op1=ALU.mult).then_inc(kk_done, 1)
                dve.wait_ge(kk_done, c + 1)
                for z in range(2):
                    dve.wait_ge(a_ev, 2 * c + z + 1)
                    chain.link(dve.tensor_scalar(ts[:, :], aT[:, z, :], -1.0, vec[:, V_KA, c:c + 1], ALU.add, ALU.mult))
                    chain.link(dve.scalar_tensor_tensor(out=kd[:, z, :], in0=ts[:, :], scalar=1.0, in1=kT[:, :],
                                                        op0=ALU.add, op1=ALU.mult))
                    last = dve.tensor_tensor(bz[:, z, :], kk[:, :], aT[:, z, :], ALU.mult)
                last.then_inc(keys_done, 1)
                chain.link(dve.tensor_tensor(ts[:, :], kd[:, 0, :], kd[:, 1, :], ALU.add))
                dve.wait_ge(kr_ev, 2 * c + 2)
                if c:
                    dve.wait_ge(bonus_mm, c)
                dve.scalar_tensor_tensor(out=rk[:, :], in0=rT[:, :], scalar=vec[:, V_RK, c:c + 1], in1=ts[:, :],
                                         op0=ALU.mult, op1=ALU.mult).then_inc(rk_done, 1)
                if c == DC - 1:
                    dve.wait_ge(proj_mm, 2 * DC)
                    mix(5, 2)
                if c:
                    bonus_copy(dve, c - 1)
            bonus_copy(dve, DC - 1)


def recurrence(nc, scr, keep):
    con, y = keep["con"], keep["y"]
    with ExitStack() as ctx:
        def sb(name, *shape):
            return ctx.enter_context(nc.sbuf_tensor(name, list(shape), F32))

        def sem(name):
            return ctx.enter_context(nc.semaphore(name))

        STREAMS = 6
        IN = [sb(f"streams{b}", P, STREAMS, D) for b in range(2)]
        R_, KK_, BZ_, KD_, SW_, V_ = range(STREAMS)
        decay = sb("decay", P, DC, 2, P)
        grow = sb("grow", P, DC, P)
        QR = [sb(f"QR{b}", P, DC, 2, P) for b in range(2)]
        B = [sb(f"B{b}", P, DC, P) for b in range(2)]
        KH = [sb(f"KH{b}", P, DC, P) for b in range(2)]
        AM = sb("AM", P, HEADS, 4, P)
        X, XT, W = (sb(n, P, HEADS, P) for n in ("X", "XT", "W"))
        TK = sb("TK", P, DC, 2, P)
        RN, UN = sb("RN", P, 2, HALF), sb("UN", P, 2, HALF)
        carry = [sb(f"carry{b}", P, DC, HEAD) for b in range(2)]
        state = sb("state", P, DC, HEAD)
        p_mid = [sb(f"p_mid{b}", P, DC) for b in range(2)]
        p_end = [sb(f"p_end{b}", P, DC) for b in range(2)]
        pS = [ctx.enter_context(nc.psum_tensor(f"pS{i}", [P, HALF], F32)) for i in range(2)]
        pI = [ctx.enter_context(nc.psum_tensor(f"pI{i}", [P, HALF], F32)) for i in range(QUADS)]
        pT = [ctx.enter_context(nc.psum_tensor(f"pT{i}", [P, HALF], F32)) for i in range(2)]

        loaded = [sem(f"loaded{b}") for b in range(2)]
        cleared = sem("cleared")
        cum_mm, exp_done = sem("cum_mm"), sem("exp_done")
        prep_dve, prep_pool = sem("prep_dve"), sem("prep_pool")
        score_mm, score_ev = sem("score_mm"), sem("score_ev")
        inv_mm = [sem(f"inv_mm{q}") for q in range(QUADS)]
        inv_ev = [sem(f"inv_ev{q}") for q in range(QUADS)]
        half_done = sem("half_done")
        pt_full = [sem(f"pt_full{k}") for k in range(2)]
        pt_free = [sem(f"pt_free{k}") for k in range(2)]
        state_ready, carried = sem("state_ready"), sem("carried")
        sp_tick, dve_tick = sem("sp_tick"), sem("dve_tick")
        USES = (6, 5)
        EV, MM = 3 * LEVELS + 1, 3 * LEVELS
        BATCHES = 2 * TILES

        def chunk(i, b):
            return (TILES - 1) - i if b else i

        def rolled(eng, body):
            with eng.Fori(0, TILES - 1) as i:
                for b in range(2):
                    body(i, b, False)
            for b in range(2):
                body(TILES - 1, b, b == 1)

        block = ctx.enter_context(nc.Block())

        @block.sync
        def _(sp):
            def load(c, b):
                for s, src in ((SW_, scr["sw"][b, c]), (R_, scr["r"][c]), (KK_, scr["kk"][c]), (BZ_, scr["bz"][b, c]),
                               (KD_, scr["kd"][b, c]), (V_, scr["v"][c])):
                    if len(src.shape) == 3:
                        src = src.rearrange("p c s -> p (c s)")
                    sp.dma_start(IN[b][:, s, :], src).then_inc(loaded[b], 16)

            load(0, 0)

            def body(i, b, last):
                if last:
                    return
                n = 2 * i + b
                wait_alone(sp, pt_full[0], USES[0] * n, sp_tick)
                load(chunk(i + b, 1 - b), 1 - b)

            rolled(sp, body)

        @block.gpsimd
        def _(pool):
            for b in range(2):
                last = pool.memset(carry[b][:, :, :], 0.0)
            last.then_inc(cleared, 1)
            pool.memset(y[:, :, :], 0.0).then_inc(cleared, 1)

            def prep(i, b):
                n = 2 * i + b
                pool.wait_ge(exp_done, 4 * n + 4)
                pool.wait_ge(loaded[b], 16 * STREAMS * (i + 1))
                pool.tensor_tensor(B[b][:, :, :], IN[b][:, BZ_, :].rearrange("p (c s) -> p c s", s=P), grow[:, :, :], ALU.mult)
                pool.tensor_tensor(KH[b][:, :, :], IN[b][:, KD_, :].rearrange("p (c s) -> p c s", s=P), grow[:, :, :],
                                   ALU.mult).then_inc(prep_pool, 1)

            prep(0, 0)

            def body(i, b, last):
                if not last:
                    pool.wait_ge(pt_full[0], USES[0] * (2 * i + b))
                    prep(i + b, 1 - b)

            rolled(pool, body)

        @block.scalar
        def _(act):
            def decays(i, b):
                n = 2 * i + b
                first = P - 1 if b else 0
                for u in range(4):
                    act.wait_ge(cum_mm, 4 * n + u + 1)
                    if u == 0:
                        act.wait_ge(prep_dve, n)
                        act.wait_ge(prep_pool, n)
                    two = pS[u % 2][:, :].rearrange("p (c e s) -> p c e s", e=2, s=P)
                    cs = slice(2 * u, 2 * u + 2)
                    act.activation(decay[:, cs].rearrange("p c e s -> p (c e s)"), pS[u % 2][:, :], ACT.Exp, scale=-DECAY)
                    act.activation(grow[:, cs, :], two[:, :, 0, :], ACT.Exp, scale=DECAY)
                    act.activation(p_mid[b][:, cs], two[:, :, 1, first], ACT.Exp, scale=DECAY).then_inc(exp_done, 1)

            decays(0, 0)

            def body(i, b, last):
                n = 2 * i + b
                for u in range(4):
                    act.wait_ge(pt_full[u % 2], USES[u % 2] * n + u // 2 + 1)
                    act.activation(TK[:, 2 * u:2 * u + 2].rearrange("p c e s -> p (c e s)"), pT[u % 2][:, :],
                                   ACT.Copy).then_inc(pt_free[u % 2], 1)
                if not last:
                    decays(i + b, 1 - b)
                for lev in range(LEVELS):
                    for q in range(QUADS):
                        act.wait_ge(inv_mm[q], MM * n + 3 * lev + 1)
                        dst = X if lev == 0 else XT
                        act.activation(dst[:, 4 * q:4 * q + 4, :].rearrange("p h s -> p (h s)"), pI[q][:, :],
                                       ACT.Copy).then_inc(inv_ev[q], 1)
                for h in range(2):
                    act.wait_ge(pt_full[h], USES[h] * n + 3)
                    act.activation(RN[:, h, :], pT[h][:, :], ACT.Copy, scale=-1.0).then_inc(pt_free[h], 1)
                for h in range(2):
                    act.wait_ge(pt_full[h], USES[h] * n + 4)
                    act.activation(UN[:, h, :], pT[h][:, :], ACT.Copy).then_inc(pt_free[h], 1)

            rolled(act, body)

        @block.tensor
        def _(pe):
            def cumulate(i, b):
                n = 2 * i + b
                pe.wait_ge(loaded[b], 16 * STREAMS * (i + 1))
                for u in range(4):
                    if u >= 2:
                        pe.wait_ge(exp_done, 4 * n + u - 1)
                    for c in range(2):
                        last = pe.matmul(pS[u % 2][:, 2 * P * c:2 * P * c + 2 * P], IN[b][:, SW_, P * (2 * u + c):P * (2 * u + c + 1)],
                                         con[:, C_CUM + 2 * P * b:C_CUM + 2 * P * (b + 1)], start=True, stop=True)
                    last.then_inc(cum_mm, 1)

            cumulate(0, 0)

            def body(i, b, last):
                n = 2 * i + b
                v = IN[b][:, V_, :]
                pe.wait_ge(prep_dve, n + 1)
                pe.wait_ge(prep_pool, n + 1)
                for j in range(HEADS):
                    c, lo = j // 2, HEAD * (j % 2)
                    if j >= 2:
                        pe.wait_ge(score_ev, HEADS * n + j - 1)
                    qr = QR[b][lo:lo + HEAD, c].rearrange("k e s -> k (e s)")
                    pe.matmul(pS[j % 2][:, 0:2 * P], B[b][lo:lo + HEAD, c, :], qr, start=True, stop=True)
                    pe.matmul(pS[j % 2][:, 2 * P:4 * P], KH[b][lo:lo + HEAD, c, :], qr, start=True, stop=True).then_inc(score_mm, 1)
                for u in range(4):
                    pe.wait_ge(pt_free[u % 2], USES[u % 2] * n + u // 2)
                    for c in range(2):
                        for e, src in enumerate((B[b], KH[b])):
                            at = P * (2 * c + e)
                            tr = pe.transpose(pT[u % 2][:, at:at + P], src[:, 2 * u + c, :], con[:, C_ID:C_ID + P])
                    tr.then_inc(pt_full[u % 2], 1)
                if not last:
                    pe.wait_ge(score_ev, HEADS * (n + 1))
                    cumulate(i + b, 1 - b)

                def per_head(q, step, lhsT, rhs, turn=False):
                    pe.wait_ge(inv_ev[q], EV * n + step)
                    for k in range(4):
                        j = 4 * q + k
                        dst = pI[q][:, P * k:P * k + P]
                        if turn:
                            mm = pe.transpose(dst, lhsT[:, j, :], con[:, C_ID:C_ID + P])
                        else:
                            mm = pe.matmul(dst, lhsT[:, j, :], rhs[:, j, :], start=True, stop=True)
                    mm.then_inc(inv_mm[q], 1)

                for q in range(QUADS):
                    per_head(q, 1, XT, None, turn=True)
                for lev in range(1, LEVELS + 1):
                    base = 3 * lev - 1
                    for q in range(QUADS):
                        per_head(q, base, AM[:, :, 0, :], X)
                    for q in range(QUADS):
                        if lev < LEVELS:
                            per_head(q, base + 1, XT, W)
                        else:
                            per_head(q, base + 1, W, XT)
                    if lev < LEVELS:
                        for q in range(QUADS):
                            per_head(q, base + 2, X, None, turn=True)
                pe.wait_ge(state_ready, n + 1)
                for h in range(2):
                    pe.wait_ge(pt_free[h], USES[h] * n + 2)
                    for c in range(DC):
                        j, lo, at = 2 * c + h, HEAD * h, HEAD * c
                        pe.matmul(pT[h][:, at:at + HEAD], QR[b][lo:lo + HEAD, c, 0, :], state[lo:lo + HEAD, c, :], start=True, stop=False)
                        mm = pe.matmul(pT[h][:, at:at + HEAD], AM[:, j, 2, :], v[:, HEAD * j:HEAD * j + HEAD], start=False, stop=True)
                    mm.then_inc(pt_full[h], 1)
                for h in range(2):
                    pe.wait_ge(pt_free[h], USES[h] * n + 3)
                    for q in range(QUADS):
                        pe.wait_ge(inv_ev[q], EV * (n + 1))
                    for c in range(DC):
                        mm = pe.matmul(pT[h][:, HEAD * c:HEAD * c + HEAD], XT[:, 2 * c + h, :], RN[:, h, HEAD * c:HEAD * c + HEAD],
                                       start=True, stop=True)
                    mm.then_inc(pt_full[h], 1)
                for h in range(2):
                    pe.wait_ge(pt_free[h], USES[h] * n + 4)
                    for c in range(DC):
                        j, lo, at = 2 * c + h, HEAD * h, HEAD * c
                        dst = pT[h][:, at:at + HEAD]
                        pe.matmul(dst, QR[b][lo:lo + HEAD, c, 1, :], state[lo:lo + HEAD, c, :], start=True, stop=False)
                        pe.matmul(dst, AM[:, j, 3, :], v[:, HEAD * j:HEAD * j + HEAD], start=False, stop=False)
                        mm = pe.matmul(dst, AM[:, j, 1, :], UN[:, h, at:at + HEAD], start=False, stop=True)
                    mm.then_inc(pt_full[h], 1)
                pe.wait_ge(pt_free[0], USES[0] * n + 5)
                for j in range(HEADS):
                    c, lo = j // 2, HEAD * (j % 2)
                    dst = pT[0][lo:lo + HEAD, HEAD * c:HEAD * c + HEAD]
                    pe.matmul(dst, TK[:, c, 1, lo:lo + HEAD], v[:, HEAD * j:HEAD * j + HEAD], start=True, stop=False)
                    mm = pe.matmul(dst, TK[:, c, 0, lo:lo + HEAD], UN[:, j % 2, HEAD * c:HEAD * c + HEAD], start=False, stop=True)
                mm.then_inc(pt_full[0], 1)

            rolled(pe, body)

        @block.vector
        def _(dve):
            def prep(i, b):
                n = 2 * i + b
                last_col = 0 if b else P - 1
                dve.wait_ge(exp_done, 4 * n + 4)
                dve.wait_ge(loaded[b], 16 * STREAMS * (i + 1))
                dve.tensor_tensor(QR[b][:, :, 0, :], IN[b][:, KK_, :].rearrange("p (c s) -> p c s", s=P), decay[:, :, 1, :], ALU.mult)
                dve.tensor_tensor(QR[b][:, :, 1, :], IN[b][:, R_, :].rearrange("p (c s) -> p c s", s=P), decay[:, :, 0, :], ALU.mult)
                dve.tensor_copy(p_end[b][:, :], decay[:, :, 0, last_col]).then_inc(prep_dve, 1)

            prep(0, 0)
            dve.wait_ge(cleared, 2)

            def body(i, b, last):
                n = 2 * i + b
                dve.wait_ge(carried, n)
                dve.tensor_tensor(state[:, :, :], carry[b][:, :, :], p_mid[b][:, :].unsqueeze(2).to_broadcast([P, DC, HEAD]),
                                  ALU.mult).then_inc(state_ready, 1)
                score_mask = con[:, C_SCORE + 4 * P * b:C_SCORE + 4 * P * (b + 1)]
                for q in range(QUADS):
                    for j in range(4 * q, 4 * q + 4):
                        dve.wait_ge(score_mm, HEADS * n + j + 1)
                        dve.tensor_tensor(AM[:, j].rearrange("p e s -> p (e s)"), pS[j % 2][:, :], score_mask,
                                          ALU.mult).then_inc(score_ev, 1)
                    dve.wait_ge(score_ev, HEADS * n + 4 * q + 4)
                    heads = slice(4 * q, 4 * q + 4)
                    dve.tensor_tensor(W[:, heads, :], AM[:, heads, 0, :],
                                      con[:, C_LEVEL:C_LEVEL + P].unsqueeze(1).to_broadcast([P, 4, P]), ALU.mult).then_inc(half_done, 1)
                    dve.wait_ge(half_done, QUADS * n + q + 1)
                    dve.tensor_tensor(XT[:, heads, :], W[:, heads, :],
                                      con[:, C_ID:C_ID + P].unsqueeze(1).to_broadcast([P, 4, P]), ALU.add).then_inc(inv_ev[q], 1)
                for lev in range(1, LEVELS + 1):
                    at = C_LEVEL + P * lev
                    for q in range(QUADS):
                        dve.wait_ge(inv_mm[q], MM * n + 3 * lev - 1)
                        dve.tensor_tensor(W[:, 4 * q:4 * q + 4, :], pI[q][:, :].rearrange("p (h s) -> p h s", s=P),
                                          con[:, at:at + P].unsqueeze(1).to_broadcast([P, 4, P]), ALU.mult).then_inc(inv_ev[q], 1)
                    for q in range(QUADS):
                        dve.wait_ge(inv_mm[q], MM * n + 3 * lev)
                        into = (X if lev < LEVELS else XT)[:, 4 * q:4 * q + 4, :].rearrange("p h s -> p (h s)")
                        dve.tensor_tensor(into, into, pI[q][:, :], ALU.add).then_inc(inv_ev[q], 1)
                    if lev == 2 and not last:
                        prep(i + b, 1 - b)
                for h in range(2):
                    wait_alone(dve, pt_full[h], USES[h] * n + 5, dve_tick)
                    cols = y[:, bass.ds(chunk(i, b), 1), :].rearrange("p a (c e v) -> p (a c) e v", e=2, v=HEAD)[:, :, h, :]
                    dve.tensor_tensor(cols, cols, pT[h][:, :].rearrange("p (c v) -> p c v", v=HEAD), ALU.add).then_inc(pt_free[h], 1)
                dve.wait_ge(pt_full[0], USES[0] * (n + 1))
                dve.tensor_tensor(state[:, :, :], state[:, :, :], pT[0][:, :].rearrange("p (c v) -> p c v", v=HEAD),
                                  ALU.add).then_inc(pt_free[0], 1)
                dve.wait_ge(pt_free[0], USES[0] * (n + 1))
                dve.tensor_tensor(carry[b][:, :, :], state[:, :, :], p_end[b][:, :].unsqueeze(2).to_broadcast([P, DC, HEAD]),
                                  ALU.mult).then_inc(carried, 1)

            rolled(dve, body)


WEIGHT_BLOCKS = 6
RING = 3


def weight_block(io, expert, m):
    half = slice(D * (m // 2), D * (m // 2) + D) if m < 4 else slice(D * (m - 4), D * (m - 4) + D)
    if m < 4:
        w = io["exp_w_gate" if m % 2 == 0 else "exp_w_up"]
        return w[0, bass.ds(expert, 1), :, half].rearrange("a (c p) f -> p (a c) f", p=P)
    return io["exp_w_down"][0, bass.ds(expert, 1), half, :].rearrange("a (c p) d -> p (a c) d", p=P)


def mix_output(nc, io, scr, keep):
    con, y, res, bonus = keep["con"], keep["y"], keep["res"], keep["bonus"]
    ident = con[:, C_ID:C_ID + P]
    with ExitStack() as ctx:
        def sb(name, *shape):
            return ctx.enter_context(nc.sbuf_tensor(name, list(shape), F32))

        def sem(name):
            return ctx.enter_context(nc.semaphore(name))

        w_out = keep["ring"][:, RING - 1]
        rows = sb("rows", P, 3, D)
        g2 = sb("g2", P, D)
        w_router = sb("w_router", P, DC, EXPERTS)
        v_in = sb("v_in", P, 2, D)
        part = sb("part", P, D)
        turned_in = sb("turned_in", P, DC, P)
        h2T = sb("h2T", P, DC, P)
        head_stat = sb("head_stat", P, 4, HEADS)
        stat = sb("mo_stat", P, 4, TILES)
        prob = sb("prob", P, EXPERTS)
        soft = sb("soft", P, 4)
        affT, work = sb("affT", EXPERTS, SEQ), sb("work", EXPERTS, 2, SEQ)
        top8 = sb("top8", EXPERTS, 2, 8)
        mask = sb("mask", P, TILES, EXPERTS)
        ps = [ctx.enter_context(nc.psum_tensor(f"mo_ps{i}", [P, HALF], F32)) for i in range(8)]

        row_load, w_load, v_load = sem("mo_row_load"), sem("mo_w_load"), [sem(f"mo_v_load{k}") for k in range(2)]
        x_load = sem("mo_x_load")
        chain_s, act_step, dve_step = sem("mo_chain"), sem("act_step"), sem("dve_step")
        gate_mm, gated = sem("gate_mm"), sem("gated")
        turn1, turn1_ev, out_mm, added = sem("turn1"), sem("turn1_ev"), sem("out_mm"), sem("added")
        h2_done, turn2, turn2_ev, logit_mm, prob_done = sem("h2_done"), sem("turn2"), sem("turn2_ev"), sem("logit_mm"), sem("prob_done")
        aff_turn, mask_done, mask_turn, mask_ev, count_mm = (sem(n) for n in ("aff_turn", "mask_done", "mask_turn", "mask_ev", "count_mm"))
        bonus_done = sem("bonus_done")
        block = ctx.enter_context(nc.Block())

        @block.sync
        def _(sp):
            for t in range(TILES):
                if t >= 2:
                    sp.wait_ge(gated, 2 * (t - 1))
                sp.dma_start(v_in[:, t % 2, :], scr["v"][t]).then_inc(v_load[t % 2], 16)
                if t == 0:
                    for i, name in enumerate(("rw_lnx_g", "rw_lnx_b", "norm_ffn_g")):
                        sp.dma_start(rows[:, i, :], io[name][0].partition_broadcast(P)).then_inc(row_load, 16)
                    sp.dma_start(g2[:, :], io["rw_g2"][0]).then_inc(row_load, 16)
                    sp.dma_start(w_router[:, :, :], io["router_w"][0].rearrange("(c p) e -> p c e", p=P)).then_inc(row_load, 16)
                    sp.dma_start(res[:, :, :], io["x"].rearrange("b (t p) d -> p (b t) d", p=P)).then_inc(x_load, 16)
                    sp.dma_start(w_out, io["rw_w_out"][0].rearrange("(c p) e -> p c e", p=P)).then_inc(w_load, 16)
                    for m in range(RING - 1):
                        for half in range(2):
                            ks = slice(4 * half, 4 * half + 4)
                            sp.dma_start(keep["ring"][:, m, ks, :], weight_block(io, 0, m)[:, ks, :]).then_inc(keep["landed"][m], 16)
            sp.wait_ge(out_mm, TILES)
            for half in range(2):
                ks = slice(4 * half, 4 * half + 4)
                sp.dma_start(keep["ring"][:, 2, ks, :], weight_block(io, 0, 2)[:, ks, :]).then_inc(keep["landed"][2], 16)

        @block.gpsimd
        def _(pool):
            for t in range(TILES):
                pool.wait_ge(v_load[t % 2], 16 * (t // 2 + 1))
                v3 = v_in[:, t % 2, :].rearrange("p (h v) -> p h v", v=HEAD)
                pool.tensor_tensor(v3, v3, bonus[:, t, :].unsqueeze(2).to_broadcast([P, HEADS, HEAD]), ALU.mult).then_inc(bonus_done, 1)

        @block.scalar
        def _(act):
            steps = 0
            for t in range(TILES):
                act.wait_ge(dve_step, 4 * t + 1)
                act.activation(part[:, :], y[:, t, :], ACT.Square).then_inc(act_step, 1)
                act.wait_ge(dve_step, 4 * t + 2)
                act.activation(head_stat[:, 3, :], head_stat[:, 2, :], ACT.Sqrt).then_inc(act_step, 1)
                for g in range(2):
                    act.wait_ge(turn1, 2 * t + g + 1)
                    act.activation(turned_in[:, 4 * g:4 * g + 4, :].rearrange("p c s -> p (c s)"), ps[2 + g][:, :], ACT.Copy).then_inc(turn1_ev, 1)
                act.wait_ge(added, 2 * t + 2)
                act.activation(part[:, :], res[:, t, :], ACT.Square, accum_out=stat[:, 0, t:t + 1]).then_inc(act_step, 1)
                act.wait_ge(dve_step, 4 * t + 3)
                act.activation(stat[:, 2, t:t + 1], stat[:, 1, t:t + 1], ACT.Sqrt).then_inc(act_step, 1)
                for g in range(2):
                    act.wait_ge(turn2, 2 * t + g + 1)
                    act.activation(h2T[:, 4 * g:4 * g + 4, :].rearrange("p c s -> p (c s)"), ps[2 + g][:, :], ACT.Copy).then_inc(turn2_ev, 1)
                act.wait_ge(dve_step, 4 * t + 4)
                act.activation(prob[:, :], ps[6][:, 0:EXPERTS], ACT.Exp, bias=soft[:, 0:1], accum_out=soft[:, 1:2]).then_inc(act_step, 1)

        @block.tensor
        def _(pe):
            pe.wait_ge(row_load, 16 * 5)
            for t in range(TILES):
                for h in range(2):
                    if t:
                        pe.wait_ge(gated, 2 * (t - 1) + h + 1)
                    pe.matmul(ps[h][:, :], keep["gate_low"][:, P * t:P * t + P], g2[:, HALF * h:HALF * h + HALF],
                              start=True, stop=True).then_inc(gate_mm, 1)
                for g in range(2):
                    pe.wait_ge(gated, 2 * t + g + 1)
                    if t:
                        pe.wait_ge(turn2_ev, 2 * t)
                    for c in range(4):
                        k = 4 * g + c
                        mm = pe.transpose(ps[2 + g][:, P * c:P * c + P], y[:, t, P * k:P * k + P], ident)
                    mm.then_inc(turn1, 1)
                pe.wait_ge(turn1_ev, 2 * t + 2)
                pe.wait_ge(w_load, 16)
                if t:
                    pe.wait_ge(added, 2 * t)
                for h in range(2):
                    for c in range(DC):
                        mm = pe.matmul(ps[4 + h][:, :], turned_in[:, c, :], w_out[:, c, HALF * h:HALF * h + HALF], start=c == 0, stop=c == DC - 1)
                mm.then_inc(out_mm, 1)
                pe.wait_ge(h2_done, t + 1)
                for g in range(2):
                    for c in range(4):
                        k = 4 * g + c
                        mm = pe.transpose(ps[2 + g][:, P * c:P * c + P], y[:, t, P * k:P * k + P], ident)
                    mm.then_inc(turn2, 1)
                pe.wait_ge(turn2_ev, 2 * t + 2)
                if t:
                    pe.wait_ge(prob_done, t)
                for c in range(DC):
                    mm = pe.matmul(ps[6][:, 0:EXPERTS], h2T[:, c, :], w_router[:, c, :], start=c == 0, stop=c == DC - 1)
                mm.then_inc(logit_mm, 1)
            pe.wait_ge(prob_done, TILES)
            for t in range(TILES):
                mm = pe.transpose(ps[7][0:EXPERTS, P * t:P * t + P], keep["aff"][:, t, :], ident)
            mm.then_inc(aff_turn, 1)
            pe.wait_ge(mask_done, 1)
            for t in range(TILES):
                mm = pe.transpose(ps[6][:, EXPERTS * t:EXPERTS * t + EXPERTS], affT[:, P * t:P * t + P], ident[0:EXPERTS, 0:EXPERTS])
            mm.then_inc(mask_turn, 1)
            pe.wait_ge(mask_ev, 1)
            for t in range(TILES):
                for s in range(t + 1):
                    tri = C_TRI if s == t else C_ONES
                    mm = pe.matmul(ps[7][:, EXPERTS * t:EXPERTS * t + EXPERTS], con[:, tri:tri + P], mask[:, s, :], start=s == 0, stop=s == t)
            mm.then_inc(count_mm, 1)

        @block.vector
        def _(dve):
            chain = Chain(dve, chain_s)
            for t in range(TILES):
                yt = y[:, t, :]
                y3 = yt.rearrange("p (h v) -> p h v", v=HEAD)
                p3 = part[:, :].rearrange("p (h v) -> p h v", v=HEAD)

                def spread(i):
                    return head_stat[:, i, :].unsqueeze(2).to_broadcast([P, HEADS, HEAD])

                chain.link(dve.tensor_reduce(head_stat[:, 0, :], y3, AX_X, ALU.add))
                chain.link(dve.tensor_scalar(head_stat[:, 1, :], head_stat[:, 0, :], 1.0 / HEAD, None, ALU.mult))
                if t:
                    dve.wait_ge(act_step, 5 * t)
                dve.tensor_tensor(y3, y3, spread(1), ALU.subtract).then_inc(dve_step, 1)
                dve.wait_ge(act_step, 5 * t + 1)
                chain.link(dve.tensor_reduce(head_stat[:, 0, :], p3, AX_X, ALU.add))
                dve.tensor_scalar(head_stat[:, 2, :], head_stat[:, 0, :], 1.0 / HEAD, LNX_EPS, ALU.mult, ALU.add).then_inc(dve_step, 1)
                dve.wait_ge(act_step, 5 * t + 2)
                chain.link(dve.reciprocal(head_stat[:, 1, :], head_stat[:, 3, :]))
                chain.link(dve.tensor_tensor(y3, y3, spread(1), ALU.mult))
                if t == 0:
                    dve.wait_ge(row_load, 16 * 5)
                chain.link(dve.tensor_tensor(yt, yt, rows[:, 0, :], ALU.mult))
                chain.link(dve.tensor_tensor(yt, yt, rows[:, 1, :], ALU.add))
                dve.wait_ge(bonus_done, t + 1)
                chain.link(dve.tensor_tensor(yt, yt, v_in[:, t % 2, :], ALU.add))
                for h in range(2):
                    cols = slice(HALF * h, HALF * h + HALF)
                    dve.wait_ge(gate_mm, 2 * t + h + 1)
                    dve.tensor_tensor(y[:, t, cols], y[:, t, cols], ps[h][:, :], ALU.mult).then_inc(gated, 1)
                dve.wait_ge(out_mm, t + 1)
                if t == 0:
                    dve.wait_ge(x_load, 16)
                for h in range(2):
                    cols = slice(HALF * h, HALF * h + HALF)
                    dve.tensor_tensor(res[:, t, cols], res[:, t, cols], ps[4 + h][:, :], ALU.add).then_inc(added, 1)
                dve.wait_ge(act_step, 5 * t + 3)
                dve.tensor_scalar(stat[:, 1, t:t + 1], stat[:, 0, t:t + 1], 1.0 / D, EPS, ALU.mult, ALU.add).then_inc(dve_step, 1)
                dve.wait_ge(act_step, 5 * t + 4)
                chain.link(dve.reciprocal(stat[:, 3, t:t + 1], stat[:, 2, t:t + 1]))
                dve.scalar_tensor_tensor(out=yt, in0=res[:, t, :], scalar=stat[:, 3, t:t + 1], in1=rows[:, 2, :],
                                         op0=ALU.mult, op1=ALU.mult).then_inc(h2_done, 1)
                dve.wait_ge(logit_mm, t + 1)
                dve.tensor_reduce(soft[:, 0:1], ps[6][:, 0:EXPERTS], AX_X, ALU.max, negate=True).then_inc(dve_step, 1)
                dve.wait_ge(act_step, 5 * t + 5)
                chain.link(dve.reciprocal(soft[:, 2:3], soft[:, 1:2]))
                dve.tensor_scalar(keep["aff"][:, t, :], prob[:, :], soft[:, 2:3], None, ALU.mult).then_inc(prob_done, 1)
            dve.wait_ge(aff_turn, 1)
            chain.link(dve.tensor_copy(work[:, 0, :], ps[7][0:EXPERTS, :]))
            for r in range(CAP // 8):
                chain.link(dve.max(top8[:, r % 2, :], work[:, r % 2, :]))
                chain.link(dve.match_replace(work[:, (r + 1) % 2, :], top8[:, r % 2, :], work[:, r % 2, :], -1.0))
            dve.tensor_scalar(affT[:, :], work[:, 0, :], 0.0, None, ALU.is_lt).then_inc(mask_done, 1)
            dve.wait_ge(mask_turn, 1)
            dve.tensor_copy(mask[:, :, :].rearrange("p t e -> p (t e)"), ps[6][:, 0:TILES * EXPERTS]).then_inc(mask_ev, 1)
            dve.wait_ge(mask_ev, 1)
            dve.wait_ge(count_mm, 1)
            slot = keep["slot"][:, :, :].rearrange("p t e -> p (t e)")
            chain.link(dve.tensor_tensor(slot, ps[7][:, 0:TILES * EXPERTS], mask[:, :, :].rearrange("p t e -> p (t e)"), ALU.mult))
            chain.link(dve.tensor_scalar(slot, slot, -1.0, None, ALU.add))


def experts(nc, io, keep):
    con, h2, res, ring, landed = keep["con"], keep["y"], keep["res"], keep["ring"], keep["landed"]
    ident = con[:, C_ID:C_ID + P]
    with ExitStack() as ctx:
        def sb(name, *shape):
            return ctx.enter_context(nc.sbuf_tensor(name, list(shape), F32))

        def sem(name):
            return ctx.enter_context(nc.semaphore(name))

        pick = sb("pick", P, TILES, 2, CAP)
        gated_pick = sb("gated_pick", P, TILES, 2, CAP)
        scatter = sb("scatter", P, SEQ)
        xin = sb("xin", P, DC, 2, CAP)
        silu = sb("silu", P, HALF)
        hid = sb("hid", P, 2, HALF)
        hidT = sb("hidT", P, 2, 4, P)
        yexp = sb("yexp", P, D)
        pG, pU = (ctx.enter_context(nc.psum_tensor(n, [P, HALF], F32)) for n in ("pG", "pU"))
        pD, pX, pO = ([ctx.enter_context(nc.psum_tensor(f"{n}{i}", [P, HALF], F32)) for i in range(2)] for n in ("pD", "pX", "pO"))

        picked, gate_picked = sem("picked"), sem("gate_picked")
        gath_mm, gath_ev = sem("gath_mm"), sem("gath_ev")
        scat_turn, scat_ev = sem("scat_turn"), sem("scat_ev")
        gate_mm, up_mm, silu_done, hid_done = sem("e_gate_mm"), sem("up_mm"), sem("silu_done"), sem("e_hid_done")
        hid_turn, hid_ev = sem("hid_turn"), sem("hid_ev")
        down_mm, down_ev = sem("down_mm"), sem("down_ev")
        scat_mm, scat_add = sem("scat_mm"), sem("scat_add")
        sp_tick = sem("e_sp_tick")
        PAIRS = EXPERTS // 2
        PER = 2 * WEIGHT_BLOCKS
        TURNS = PER // RING

        block = ctx.enter_context(nc.Block())

        @block.sync
        def _(sp):
            def body(i, last):
                for m in range(RING, PER if last else PER + RING):
                    slot = m % RING
                    e = 2 * i + m // WEIGHT_BLOCKS
                    before = m - RING
                    n, kind = 2 * i + before // WEIGHT_BLOCKS, before % WEIGHT_BLOCKS
                    if kind < 4:
                        wait_alone(sp, (gate_mm, up_mm)[kind % 2], 2 * n + kind // 2 + 1, sp_tick)
                    else:
                        wait_alone(sp, down_mm, 2 * n + kind - 3, sp_tick)
                    for half in range(2):
                        ks = slice(4 * half, 4 * half + 4)
                        sp.dma_start(ring[:, slot, ks, :], weight_block(io, e, m % WEIGHT_BLOCKS)[:, ks, :]).then_inc(landed[slot], 16)

            with sp.Fori(0, PAIRS - 1) as i:
                body(i, False)
            body(PAIRS - 1, True)

        @block.tensor
        def _(pe):
            def body(i):
                def block_of(e, m):
                    n = WEIGHT_BLOCKS * e + m
                    slot = n % RING
                    pe.wait_ge(landed[slot], 32 * (TURNS * i + n // RING + 1))
                    return ring[:, slot]

                pe.wait_ge(picked, i + 1)
                for g in range(2):
                    pe.wait_ge(gath_ev, 2 * i)
                    pe.wait_ge(scat_ev, 2 * i)
                    pe.wait_ge(hid_ev, 4 * i)
                    for c in range(4):
                        k = 4 * g + c
                        for t in range(TILES):
                            mm = pe.matmul(pX[g][:, P * c:P * c + P], h2[:, t, P * k:P * k + P],
                                           pick[:, t].rearrange("p e s -> p (e s)"), start=t == 0, stop=t == TILES - 1)
                    mm.then_inc(gath_mm, 1)
                for e in range(2):
                    n = 2 * i + e

                    def up_down(which, psum, m):
                        w = block_of(e, m)
                        for k in range(DC):
                            for s in range(2):
                                mm = pe.matmul(psum[HEAD * s:HEAD * s + HEAD, :], xin[:, k, e, :], w[:, k, HALF * s:HALF * s + HALF],
                                               start=k == 0, stop=k == DC - 1)
                        mm.then_inc(which, 1)

                    def turn(j):
                        pe.wait_ge(hid_done, 2 * n + j + 1)
                        for c in range(4):
                            mm = pe.transpose(pX[j][:, P * c:P * c + P], hid[:, j, P * c:P * c + P], ident)
                        mm.then_inc(hid_turn, 1)

                    def down(j):
                        w = block_of(e, 4 + j)
                        pe.wait_ge(hid_ev, 2 * n + j + 1)
                        if j == 0:
                            pe.wait_ge(down_ev, 2 * n)
                        for c in range(4):
                            for h in range(2):
                                for s in range(2):
                                    mm = pe.matmul(pD[h][HEAD * s:HEAD * s + HEAD, :], hidT[:, j, c, HEAD * s:HEAD * s + HEAD],
                                                   w[:, 4 * s + c, HALF * h:HALF * h + HALF], start=j == 0 and c == 0, stop=j == 1 and c == 3)
                        mm.then_inc(down_mm, 1)

                    pe.wait_ge(gath_ev, 2 * i + 2)
                    pe.wait_ge(silu_done, 2 * n)
                    up_down(gate_mm, pG, 0)
                    pe.wait_ge(gate_picked, n + 1)
                    for t in range(TILES):
                        mm = pe.transpose(pX[0][:, P * t:P * t + P], gated_pick[:, t].rearrange("p e s -> p (e s)"), ident)
                    mm.then_inc(scat_turn, 1)
                    pe.wait_ge(hid_done, 2 * n)
                    up_down(up_mm, pU, 1)
                    pe.wait_ge(silu_done, 2 * n + 1)
                    up_down(gate_mm, pG, 2)
                    pe.wait_ge(scat_ev, n + 1)
                    turn(0)
                    up_down(up_mm, pU, 3)
                    down(0)
                    turn(1)
                    down(1)
                    pe.wait_ge(down_ev, 2 * n + 2)
                    for u in range(2 * TILES):
                        t, h = u // 2, u % 2
                        if u >= 2:
                            pe.wait_ge(scat_add, 2 * TILES * n + u - 1)
                        else:
                            pe.wait_ge(scat_add, 2 * TILES * n)
                        pe.matmul(pO[h][:, :], scatter[:, P * t:P * t + P], yexp[:, HALF * h:HALF * h + HALF], start=True,
                                  stop=True).then_inc(scat_mm, 1)

            with pe.Fori(0, PAIRS) as i:
                body(i)

        @block.scalar
        def _(act):
            def body(i):
                for g in range(2):
                    act.wait_ge(gath_mm, 2 * i + g + 1)
                    act.activation(xin[:, 4 * g:4 * g + 4].rearrange("p c e s -> p (c e s)"), pX[g][:, :], ACT.Copy).then_inc(gath_ev, 1)
                for e in range(2):
                    n = 2 * i + e
                    for j in range(2):
                        act.wait_ge(gate_mm, 2 * n + j + 1)
                        act.wait_ge(hid_done, 2 * n + j)
                        act.activation(silu[:, :], pG[:, :], ACT.Silu).then_inc(silu_done, 1)
                        if j == 0:
                            act.wait_ge(scat_turn, n + 1)
                            act.activation(scatter[:, :], pX[0][:, :], ACT.Copy).then_inc(scat_ev, 1)
                    for j in range(2):
                        act.wait_ge(hid_turn, 2 * n + j + 1)
                        act.activation(hidT[:, j].rearrange("p c s -> p (c s)"), pX[j][:, :], ACT.Copy).then_inc(hid_ev, 1)
                    act.wait_ge(down_mm, 2 * n + 2)
                    for h in range(2):
                        act.activation(yexp[:, HALF * h:HALF * h + HALF], pD[h][:, :], ACT.Copy).then_inc(down_ev, 1)

            with act.Fori(0, PAIRS) as i:
                body(i)

        @block.vector
        def _(dve):
            iota = con[:, C_IOTA:C_IOTA + CAP]

            def body(i):
                dve.wait_ge(gath_mm, 2 * i)
                dve.wait_ge(gate_picked, 2 * i)
                dve.tensor_tensor(pick[:, :, :, :], iota.unsqueeze(1).unsqueeze(1).to_broadcast([P, TILES, 2, CAP]),
                                  keep["slot"][:, :, bass.ds(2 * i, 2)].unsqueeze(3).to_broadcast([P, TILES, 2, CAP]),
                                  ALU.is_equal).then_inc(picked, 1)
                dve.wait_ge(picked, i + 1)
                for e in range(2):
                    n = 2 * i + e
                    dve.wait_ge(scat_turn, n)
                    dve.tensor_tensor(gated_pick[:, :, :, :], pick[:, :, e:e + 1, :].to_broadcast([P, TILES, 2, CAP]),
                                      keep["aff"][:, :, bass.ds(n, 1)].unsqueeze(3).to_broadcast([P, TILES, 2, CAP]),
                                      ALU.mult).then_inc(gate_picked, 1)
                    for j in range(2):
                        dve.wait_ge(silu_done, 2 * n + j + 1)
                        dve.wait_ge(up_mm, 2 * n + j + 1)
                        dve.wait_ge(hid_turn, 2 * n + j - 1 if j else 2 * n)
                        dve.tensor_tensor(hid[:, j, :], silu[:, :], pU[:, :], ALU.mult).then_inc(hid_done, 1)
                    for u in range(2 * TILES):
                        t, h = u // 2, u % 2
                        dve.wait_ge(scat_mm, 2 * TILES * n + u + 1)
                        cols = res[:, t, HALF * h:HALF * h + HALF]
                        dve.tensor_tensor(cols, cols, pO[h][:, :], ALU.add).then_inc(scat_add, 1)

            with dve.Fori(0, PAIRS) as i:
                body(i)


def final_norm(nc, io, keep, out):
    res = keep["res"]
    with ExitStack() as ctx:
        row = ctx.enter_context(nc.sbuf_tensor("final_row", [P, D], F32))
        part = ctx.enter_context(nc.sbuf_tensor("final_part", [P, D], F32))
        stat = ctx.enter_context(nc.sbuf_tensor("final_stat", [P, 4, TILES], F32))
        row_load, squared, mean, rooted, inverse, done, stored = (
            ctx.enter_context(nc.semaphore(f"final_{n}")) for n in ("row", "squared", "mean", "rooted", "inverse", "done", "stored"))
        block = ctx.enter_context(nc.Block())
        out_t = out.rearrange("b (t p) d -> (b t) p d", p=P)

        @block.sync
        def _(sp):
            sp.dma_start(row[:, :], io["final_norm_g"].partition_broadcast(P)).then_inc(row_load, 16)
            for t in range(TILES):
                sp.wait_ge(done, t + 1)
                sp.dma_start(out_t[t], res[:, t, :]).then_inc(stored, 16)
            sp.wait_ge(stored, 16 * TILES)

        @block.scalar
        def _(act):
            for t in range(TILES):
                act.activation(part[:, :], res[:, t, :], ACT.Square, accum_out=stat[:, 0, t:t + 1]).then_inc(squared, 1)
                act.wait_ge(squared, t + 1)
            act.wait_ge(mean, 1)
            act.activation(stat[:, 2, :], stat[:, 1, :], ACT.Sqrt).then_inc(rooted, 1)

        @block.vector
        def _(dve):
            dve.wait_ge(squared, TILES)
            dve.tensor_scalar(stat[:, 1, :], stat[:, 0, :], 1.0 / D, EPS, ALU.mult, ALU.add).then_inc(mean, 1)
            dve.wait_ge(rooted, 1)
            dve.reciprocal(stat[:, 3, :], stat[:, 2, :]).then_inc(inverse, 1)
            dve.wait_ge(inverse, 1)
            dve.wait_ge(row_load, 16)
            for t in range(TILES):
                dve.scalar_tensor_tensor(out=res[:, t, :], in0=res[:, t, :], scalar=stat[:, 3, t:t + 1], in1=row[:, :],
                                         op0=ALU.mult, op1=ALU.mult).then_inc(done, 1)


_INS = ["x", "norm_ffn_g", "router_w", "exp_w_gate", "exp_w_up", "exp_w_down", "final_norm_g", "rw_w_in", "rw_w0", "rw_w1",
        "rw_w2", "rw_a1", "rw_a2", "rw_g1", "rw_g2", "rw_lnx_g", "rw_lnx_b", "rw_w_out"]


def kernel(**inputs):
    import concourse.bacc as bacc
    from concourse.bass_utils import run_bass_kernel_spmd

    nc = bacc.Bacc("TRN2", target_bir_lowering=False, num_devices=1)
    arrays, io = {}, {}

    def give(name, a):
        a = np.ascontiguousarray(a)
        arrays[f"in_{name}"] = a
        io[name] = nc.dram_tensor(f"in_{name}", a.shape, mybir.dt.from_np(a.dtype), kind="ExternalInput").ap()

    for name in _INS:
        give(name, inputs[name])
    rows = np.concatenate([np.asarray(inputs[n]).reshape(-1, D)
                           for n in ("norm_mix_g", "rw_mu", "rw_a0", "rw_k_k", "rw_k_a", "rw_r_k")], axis=0)
    give("vectors", rows.reshape(V_END, DC, P).transpose(2, 0, 1))
    give("consts", constants())
    out = nc.dram_tensor("out", (1, SEQ, D), F32, kind="ExternalOutput").ap()
    build_trunk(nc, io, out)
    r = run_bass_kernel_spmd(nc, [arrays], core_ids=[0])
    return r.results[0]["out"]
```

```python
from contextlib import ExitStack

import numpy as np

import concourse.bass as bass
from concourse import mybir

F32 = mybir.dt.float32
ALU = mybir.AluOpType
ACT = mybir.ActivationFunctionType
AX_X = mybir.AxisListType.X

P = 128
D = 1024
SEQ = 512
TILES = SEQ // P
DC = D // P
HEAD = 64
HEADS = D // HEAD
HALF = 512
LORA = 64
EXPERTS = 16
CAP = 2 * SEQ // EXPERTS
FF = 2048
EPS = 1e-6
LNX_EPS = 64e-5
DECAY = float(np.exp(-0.5))
BASE = 16
LEVELS = 3
GIVEN = 1
QUADS = HEADS // 4

C_ID, C_CUM, C_SCORE, C_LEVEL, C_EYE, C_TRI, C_ONES, C_HEAD, C_SEL, C_IOTA, C_END = np.cumsum(
    [0, P, 4 * P, 8 * P, LEVELS * P, BASE * BASE, P, P, P, 4, CAP]).tolist()
V_NORM, V_MU, V_A0, V_KK, V_KA, V_RK, V_END = np.cumsum([0, 1, 6, 2, 1, 1, 1]).tolist()


def constants():
    s, t = np.arange(P)[:, None], np.arange(P)[None, :]
    low = (s < P // 2) * 1.0
    cum = [(s <= t) - low, (s < t) - low, (s >= t) - (1 - low), (s > t) - (1 - low)]
    score = []
    for strict, incl in ((s < t, s <= t), (s > t, s >= t)):
        score += [-1.0 * strict, 1.0 * incl, 1.0 * strict, 1.0 * incl]
    level = [(s // (2 * m) == t // (2 * m)) & (s // m != t // m) for m in (BASE, 2 * BASE, 4 * BASE)]
    eye = np.broadcast_to(np.eye(BASE).reshape(1, -1), (P, BASE * BASE))
    sel = (s // HEAD == np.arange(4)[None, :]) * 1.0
    iota = np.broadcast_to(np.arange(CAP)[None, :], (P, CAP))
    parts = [s == t, *cum, *score, *level, eye, s <= t, np.ones((P, P)), s // HEAD == t // HEAD, sel, iota]
    return np.ascontiguousarray(np.concatenate([np.asarray(a, np.float32) for a in parts], axis=1))


class Chain:

    def __init__(self, eng, sem, base=0):
        self.eng, self.sem, self.base, self.n = eng, sem, base, 0

    def link(self, ins):
        ins.then_inc(self.sem, 1)
        self.n += 1
        self.eng.wait_ge(self.sem, self.base + self.n)


def wait_alone(eng, sem, value, tick):
    eng.wait_ge(sem, value)
    eng.sem_inc(tick, 1)


def build_trunk(nc, io, out):
    scr = {
        name: nc.dram_tensor(f"scratch_{name}", shape, F32, kind="Internal").ap()
        for name, shape in {
            "r": [TILES, P, DC, P], "kk": [TILES, P, DC, P], "bz": [2, TILES, P, DC, P],
            "kd": [2, TILES, P, DC, P], "sw": [2, TILES, P, D], "v": [TILES, P, D],
            "blocks": [P // BASE, HEADS, BASE, BASE], "inverses": [P // BASE, HEADS, BASE, BASE],
        }.items()
    }
    with ExitStack() as ctx:
        keep = {
            "con": ctx.enter_context(nc.sbuf_tensor("con", [P, C_END], F32)),
            "vec": ctx.enter_context(nc.sbuf_tensor("vec", [P, V_END, DC], F32)),
            "gate_low": ctx.enter_context(nc.sbuf_tensor("gate_low", [P, SEQ], F32)),
            "bonus": ctx.enter_context(nc.sbuf_tensor("bonus", [P, TILES, HEADS], F32)),
        }
        with nc.sbuf_tensor("y", [P, TILES, D], F32) as y:
            keep["y"] = y
            mix_inputs(nc, io, scr, keep)
            recurrence(nc, io, scr, keep)
            with ExitStack() as moe:
                for name, shape in (("res", [P, TILES, D]), ("slot", [P, TILES, EXPERTS]), ("aff", [P, TILES, EXPERTS]),
                                    ("ring", [P, 3, 8, D])):
                    keep[name] = moe.enter_context(nc.sbuf_tensor(name, shape, F32))
                keep["landed"] = [moe.enter_context(nc.semaphore(f"weights_landed{k}")) for k in range(3)]
                mix_output(nc, io, scr, keep)
                experts(nc, io, keep)
                final_norm(nc, io, keep, out)


def mix_inputs(nc, io, scr, keep):
    con, vec = keep["con"], keep["vec"]
    ident = con[:, C_ID:C_ID + P]
    with ExitStack() as ctx:
        def sb(name, *shape):
            return ctx.enter_context(nc.sbuf_tensor(name, list(shape), F32))

        def sem(name):
            return ctx.enter_context(nc.semaphore(name))

        x_in = sb("x_in", P, 2, D)
        hT = sb("hT", P, DC, SEQ + 2)
        shift = sb("shift", P, DC, SEQ)
        xm = [sb("xm0", P, DC, SEQ)[:, :, :], keep["y"][:, :, :].rearrange("p t d -> p (t d)").rearrange("p (c s) -> p c s", s=SEQ)]
        w_ring = sb("w_ring", P, 2, 2, DC, 256)
        low_w = sb("low_w", P, 3, DC, P)
        up_w = sb("up_w", P, 2, D)
        w0_row = sb("w0_row", P, 2, D)
        tw, xa = sb("tw", P, 2, SEQ), sb("xa", P, 2, SEQ)
        tok = sb("tok", P, 2, D)
        kT, rT = sb("kT", P, SEQ), sb("rT", P, SEQ)
        sq, rn, kk = sb("sq", P, SEQ), sb("rn", P, SEQ), sb("kk", P, SEQ)
        aT, kd, bz = sb("aT", P, 2, SEQ), sb("kd", P, 2, SEQ), sb("bz", P, 2, SEQ)
        ts, rk = sb("ts", P, SEQ), sb("rk", P, SEQ)
        stat = sb("stat", P, 3, TILES)
        ps = [ctx.enter_context(nc.psum_tensor(f"mi_ps{i}", [P, HALF], F32)) for i in range(8)]

        x_load = [sem(f"x_load{i}") for i in range(2)]
        con_load, low_load, row_load = sem("con_load"), sem("low_load"), sem("row_load")
        sq_done, root_done, h_done = sem("sq_done"), sem("root_done"), sem("h_done")
        turned, hT_done, xm_done = sem("turned"), sem("hT_done"), sem("xm_done")
        chain_s = sem("mi_chain")
        low_mm, low_ev = sem("low_mm"), sem("low_ev")
        sw_mm, sw_sum, sw_done = sem("sw_mm"), sem("sw_sum"), sem("sw_done")
        sw_out = [sem(f"sw_out{i}") for i in range(2)]
        w_load = [sem(f"w_load{i}") for i in range(2)]
        proj_mm, kr_ev, sq_ev = sem("proj_mm"), sem("kr_ev"), sem("sq_ev")
        norm_mm, norm_max, norm_root, kk_done = sem("norm_mm"), sem("norm_max"), sem("norm_root"), sem("kk_done")
        a_mm, a_ev, keys_done, rk_done = sem("a_mm"), sem("a_ev"), sem("keys_done"), sem("rk_done")
        bonus_mm, bonus_ev, chunk_out = sem("bonus_mm"), sem("bonus_ev"), sem("chunk_out")
        low_zero = sem("low_zero")

        x_t = io["x"].rearrange("b (t p) d -> (b t) p d", p=P)
        w_in = io["rw_w_in"].rearrange("a m (c p) e -> (a m) p c e", p=P)
        LOW = (3, 4, 5)

        def bonus_products(pe, c):
            pe.wait_ge(rk_done, c + 1)
            if c:
                pe.wait_ge(bonus_ev, c)
            for t in range(TILES):
                last = pe.matmul(ps[7][:, 4 * t:4 * t + 4], rk[:, P * t:P * t + P], con[:, C_SEL:C_SEL + 4], start=True, stop=True)
            last.then_inc(bonus_mm, 1)

        def bonus_copy(dve, c):
            dve.wait_ge(bonus_mm, c + 1)
            dve.tensor_copy(keep["bonus"][:, :, 2 * c:2 * c + 2],
                            ps[7][:, 0:4 * TILES].rearrange("p (t h) -> p t h", h=4)[:, :, 0:2]).then_inc(bonus_ev, 1)

        block = ctx.enter_context(nc.Block())

        @block.sync
        def _(sp):
            for t in range(TILES):
                if t >= 2:
                    sp.wait_ge(h_done, t - 1)
                    sp.wait_ge(turned, 2 * (t - 1))
                sp.dma_start(x_in[:, t % 2, :], x_t[t]).then_inc(x_load[t % 2], 16)
            for q in range(4):
                if q >= 2:
                    sp.wait_ge(proj_mm, 4 * (q - 1))
                for m, which in enumerate((1, 0)):
                    sp.dma_start(w_ring[:, q % 2, m], w_in[which][:, :, 256 * q:256 * q + 256]).then_inc(w_load[q % 2], 16)
            for k in range(2):
                sp.wait_ge(sw_out[k], 16 * TILES)
            sp.wait_ge(chunk_out, 16 * 6 * DC)

        @block.gpsimd
        def _(pool):
            pool.dma_start(con[:, :], io["consts"]).then_inc(con_load, 16)
            pool.dma_start(vec[:, :, :], io["vectors"]).then_inc(con_load, 16)
            for i, name in enumerate(("rw_w1", "rw_a1")):
                for z in range(2):
                    pool.dma_start(low_w[:, i, :, LORA * z:LORA * z + LORA],
                                   io[name][0, z].rearrange("(c p) r -> p c r", p=P)).then_inc(low_load, 16)
            pool.dma_start(low_w[:, 2], io["rw_g1"][0].rearrange("(c p) r -> p c r", p=P)).then_inc(low_load, 16)
            for i, name in enumerate(("rw_w2", "rw_a2")):
                pool.dma_start(up_w[:, i, :], io[name].rearrange("a z r d -> (a z r) d")).then_inc(low_load, 16)
            for z in range(2):
                pool.dma_start(w0_row[:, z, :], io["rw_w0"][0, z].partition_broadcast(P)).then_inc(row_load, 16)
            for u in range(2 * TILES):
                pool.wait_ge(sw_done, u + 1)
                pool.dma_start(scr["sw"][u // TILES, u % TILES], tok[:, u % 2, :]).then_inc(sw_out[u % 2], 16)
            for c in range(DC):
                def spill(name, z, src):
                    dst = scr[name] if z is None else scr[name][z]
                    pool.dma_start(dst[:, :, c, :].rearrange("t p s -> p t s"),
                                   src.rearrange("p (t s) -> p t s", s=P)).then_inc(chunk_out, 16)
                pool.wait_ge(kr_ev, 2 * c + 2)
                spill("r", None, rT[:, :])
                pool.wait_ge(kk_done, c + 1)
                spill("kk", None, kk[:, :])
                pool.wait_ge(keys_done, c + 1)
                for z in range(2):
                    spill("bz", z, bz[:, z, :])
                    spill("kd", z, kd[:, z, :])

        @block.scalar
        def _(act):
            for t in range(TILES):
                act.wait_ge(x_load[t % 2], 16 * (t // 2 + 1))
                act.activation(shift[:, 2 * t:2 * t + 2, :].rearrange("p a b -> p (a b)"), x_in[:, t % 2, :], ACT.Square,
                               accum_out=stat[:, 0, t:t + 1]).then_inc(sq_done, 1)
                act.wait_ge(norm_max, t + 1)
                act.activation(stat[:, 1, t:t + 1], stat[:, 2, t:t + 1], ACT.Sqrt).then_inc(root_done, 1)
            act.wait_ge(low_zero, 1)
            for i, (dst, fn) in enumerate(((tw, ACT.Tanh), (xa, ACT.Copy))):
                act.wait_ge(low_mm, i + 1)
                for z in range(2):
                    rows = slice(LORA * z, LORA * z + LORA)
                    last = act.activation(dst[rows, z, :], ps[i % 2][rows, :], fn)
                last.then_inc(low_ev, 1)
            act.wait_ge(low_mm, 3)
            act.activation(keep["gate_low"][:, :], ps[0][:, :], ACT.Sigmoid).then_inc(low_ev, 1)
            for u in range(2 * TILES):
                act.wait_ge(sw_sum, 2 * u + 2)
                act.activation(tok[:, u % 2, :], tok[:, u % 2, :], ACT.Sigmoid).then_inc(sw_done, 1)
            for c in range(DC):
                act.wait_ge(proj_mm, 2 * c + 1)
                if c:
                    act.wait_ge(keys_done, c)
                act.activation(kT[:, :], ps[2][:, :], ACT.Copy).then_inc(kr_ev, 1)
                act.activation(sq[:, :], ps[2][:, :], ACT.Square, scale=vec[:, V_KK, c:c + 1]).then_inc(sq_ev, 1)
                for z in range(2):
                    act.wait_ge(a_mm, 2 * c + z + 1)
                    act.activation(aT[:, z, :], ps[4 + z][:, :], ACT.Sigmoid,
                                   bias=vec[:, V_A0 + z, c:c + 1]).then_inc(a_ev, 1)
                act.wait_ge(norm_max, TILES + c + 1)
                act.activation(rn[:, :], sq[:, :], ACT.Sqrt).then_inc(norm_root, 1)
                act.wait_ge(proj_mm, 2 * c + 2)
                if c:
                    act.wait_ge(chunk_out, 16 * 6 * c)
                    act.wait_ge(rk_done, c)
                act.activation(rT[:, :], ps[3][:, :], ACT.Copy).then_inc(kr_ev, 1)

        @block.tensor
        def _(pe):
            pe.wait_ge(con_load, 32)
            for t in range(TILES):
                pe.wait_ge(h_done, t + 1)
                for g in range(2):
                    if t:
                        pe.wait_ge(hT_done, 2 * t + g - 1)
                    for c in range(4):
                        last = pe.transpose(ps[g][:, P * c:P * c + P], x_in[:, t % 2, P * (4 * g + c):P * (4 * g + c + 1)], ident)
                    last.then_inc(turned, 1)
            pe.wait_ge(low_load, 16 * 7)
            for i in range(3):
                pe.wait_ge(xm_done, i + 1)
                if i < 2:
                    pe.wait_ge(hT_done, 2 * TILES)
                else:
                    pe.wait_ge(low_ev, 1)
                for c in range(DC):
                    last = pe.matmul(ps[i % 2][:, :], low_w[:, i, c, :], xm[i % 2][:, c, :], start=c == 0, stop=c == DC - 1)
                last.then_inc(low_mm, 1)
            for u in range(2 * TILES):
                z, t = u // TILES, u % TILES
                for h in range(2):
                    pe.wait_ge(low_ev, 3)
                    if u:
                        pe.wait_ge(sw_sum, 2 * u + h - 1)
                    pe.matmul(ps[h][:, :], tw[:, z, P * t:P * t + P], up_w[:, 0, HALF * h:HALF * h + HALF],
                              start=True, stop=True).then_inc(sw_mm, 1)
            for c in range(DC):
                q = c // 2
                pe.wait_ge(w_load[q % 2], 32 * (q // 2 + 1))
                pe.wait_ge(xm_done, 5)
                for m in range(2):
                    if c:
                        pe.wait_ge(kr_ev, 2 * (c - 1) + m + 1)
                        pe.wait_ge(sq_ev, c)
                    for k in range(DC):
                        last = pe.matmul(ps[2 + m][:, :], w_ring[:, q % 2, m, k, P * (c % 2):P * (c % 2) + P],
                                         xm[(3 + m) % 2][:, k, :], start=k == 0, stop=k == DC - 1)
                    last.then_inc(proj_mm, 1)
                    if m == 0:
                        for z in range(2):
                            if c:
                                pe.wait_ge(a_ev, 2 * (c - 1) + z + 1)
                            pe.matmul(ps[4 + z][:, :], up_w[:, 1, P * c:P * c + P], xa[:, z, :], start=True, stop=True).then_inc(a_mm, 1)
                pe.wait_ge(sq_ev, c + 1)
                if c:
                    pe.wait_ge(norm_max, TILES + c)
                pe.matmul(ps[6][:, :], con[:, C_HEAD:C_HEAD + P], sq[:, :], start=True, stop=True).then_inc(norm_mm, 1)
                if c:
                    bonus_products(pe, c - 1)
            bonus_products(pe, DC - 1)

        @block.vector
        def _(dve):
            chain = Chain(dve, chain_s)
            dve.memset(hT[:, :, 0:1], 0.0)
            dve.memset(hT[:, :, SEQ + 1:SEQ + 2], 0.0)
            for z in range(2):
                other = slice(LORA * (1 - z), LORA * (1 - z) + LORA)
                dve.memset(tw[other, z, :], 0.0)
                last = dve.memset(xa[other, z, :], 0.0)
            last.then_inc(low_zero, 1)
            for t in range(TILES):
                dve.wait_ge(sq_done, t + 1)
                dve.tensor_scalar(stat[:, 2, t:t + 1], stat[:, 0, t:t + 1], 1.0 / D, EPS, ALU.mult, ALU.add).then_inc(norm_max, 1)
                dve.wait_ge(root_done, t + 1)
                chain.link(dve.reciprocal(stat[:, 1, t:t + 1], stat[:, 1, t:t + 1]))
                dve.tensor_scalar(x_in[:, t % 2, :], x_in[:, t % 2, :], stat[:, 1, t:t + 1], None, ALU.mult).then_inc(h_done, 1)
                if t == 0:
                    dve.wait_ge(con_load, 32)
                for g in range(2):
                    dve.wait_ge(turned, 2 * t + g + 1)
                    dve.tensor_tensor(hT[:, 4 * g:4 * g + 4, 1 + P * t:1 + P * t + P], ps[g][:, :].rearrange("p (c s) -> p c s", s=P),
                                      vec[:, V_NORM, 4 * g:4 * g + 4].unsqueeze(2).to_broadcast([P, 4, P]), ALU.mult).then_inc(hT_done, 1)
            dve.wait_ge(hT_done, 2 * TILES)
            for c in range(DC):
                chain.link(dve.tensor_tensor(shift[:, c, :], hT[:, c, 0:SEQ], hT[:, c, 2:SEQ + 2], ALU.add))
                chain.link(dve.scalar_tensor_tensor(out=shift[:, c, :], in0=shift[:, c, :], scalar=0.5, in1=hT[:, c, 1:SEQ + 1],
                                                    op0=ALU.mult, op1=ALU.subtract))

            def mix(i, which):
                for c in range(DC):
                    last = dve.scalar_tensor_tensor(out=xm[i % 2][:, c, :], in0=shift[:, c, :], scalar=vec[:, V_MU + which, c:c + 1],
                                                    in1=hT[:, c, 1:SEQ + 1], op0=ALU.mult, op1=ALU.add)
                last.then_inc(xm_done, 1)

            mix(0, 3)
            mix(1, 4)
            dve.wait_ge(low_mm, 1)
            mix(2, 5)
            dve.wait_ge(low_mm, 2)
            mix(3, 1)
            dve.wait_ge(low_mm, 3)
            mix(4, 0)
            dve.wait_ge(row_load, 32)
            for u in range(2 * TILES):
                for h in range(2):
                    dve.wait_ge(sw_mm, 2 * u + h + 1)
                    if u >= 2:
                        dve.wait_ge(sw_out[u % 2], 16 * (u // 2))
                    cols = slice(HALF * h, HALF * h + HALF)
                    dve.tensor_tensor(tok[:, u % 2, cols], ps[h][:, :], w0_row[:, u // TILES, cols], ALU.add).then_inc(sw_sum, 1)
            for c in range(DC):
                dve.wait_ge(norm_mm, c + 1)
                dve.tensor_scalar(sq[:, :], ps[6][:, :], 1e-24, None, ALU.max).then_inc(norm_max, 1)
                dve.wait_ge(norm_root, c + 1)
                chain.link(dve.reciprocal(rn[:, :], rn[:, :]))
                if c:
                    dve.wait_ge(chunk_out, 16 * 6 * c)
                dve.scalar_tensor_tensor(out=kk[:, :], in0=kT[:, :], scalar=vec[:, V_KK, c:c + 1], in1=rn[:, :],
                                         op0=ALU.mult, op1=ALU.mult).then_inc(kk_done, 1)
                dve.wait_ge(kk_done, c + 1)
                for z in range(2):
                    dve.wait_ge(a_ev, 2 * c + z + 1)
                    chain.link(dve.tensor_scalar(ts[:, :], aT[:, z, :], -1.0, vec[:, V_KA, c:c + 1], ALU.add, ALU.mult))
                    chain.link(dve.scalar_tensor_tensor(out=kd[:, z, :], in0=ts[:, :], scalar=1.0, in1=kT[:, :],
                                                        op0=ALU.add, op1=ALU.mult))
                    last = dve.tensor_tensor(bz[:, z, :], kk[:, :], aT[:, z, :], ALU.mult)
                last.then_inc(keys_done, 1)
                chain.link(dve.tensor_tensor(ts[:, :], kd[:, 0, :], kd[:, 1, :], ALU.add))
                dve.wait_ge(kr_ev, 2 * c + 2)
                if c:
                    dve.wait_ge(bonus_mm, c)
                dve.scalar_tensor_tensor(out=rk[:, :], in0=rT[:, :], scalar=vec[:, V_RK, c:c + 1], in1=ts[:, :],
                                         op0=ALU.mult, op1=ALU.mult).then_inc(rk_done, 1)
                if c == DC - 1:
                    dve.wait_ge(proj_mm, 2 * DC)
                    mix(5, 2)
                if c:
                    bonus_copy(dve, c - 1)
            bonus_copy(dve, DC - 1)


def recurrence(nc, io, scr, keep):
    con, y = keep["con"], keep["y"]
    with ExitStack() as ctx:
        def sb(name, *shape):
            return ctx.enter_context(nc.sbuf_tensor(name, list(shape), F32))

        def sem(name):
            return ctx.enter_context(nc.semaphore(name))

        R_, KK_, BZ_, KD_, SW_ = range(5)
        IN = sb("streams", P, 5, D)
        V = [sb(f"V{b}", P, D) for b in range(2)]
        decay = sb("decay", P, DC, 2, P)
        grow = sb("grow", P, DC, P)
        QR = [sb(f"QR{b}", P, DC, 2, P) for b in range(2)]
        B = [sb(f"B{e}", P, DC, P) for e in range(2)]
        KH = [sb(f"KH{e}", P, DC, P) for e in range(2)]
        QB = [sb(f"QB{b}", P, HEADS, P) for b in range(2)]
        AM = sb("AM", P, HEADS, 3, P)
        X, XT, W = (sb(n, P, HEADS, P) for n in ("X", "XT", "W"))
        TK = sb("TK", P, DC, 2, 2, HEAD)
        RN, UN = sb("RN", P, 2, HALF), sb("UN", P, 2, HALF)
        carry = [sb(f"carry{b}", P, DC, HEAD) for b in range(2)]
        state = sb("state", P, DC, 2, HEAD)
        p_mid = [sb(f"p_mid{b}", P, DC) for b in range(2)]
        p_end = [sb(f"p_end{b}", P, DC) for b in range(2)]
        NB, XB, step_sum = (sb(n, P, BASE, BASE) for n in ("NB", "XB", "step_sum"))
        pS = [ctx.enter_context(nc.psum_tensor(f"pS{i}", [P, HALF], F32)) for i in range(2)]
        pI = [ctx.enter_context(nc.psum_tensor(f"pI{i}", [P, HALF], F32)) for i in range(QUADS)]
        pT = [ctx.enter_context(nc.psum_tensor(f"pT{i}", [P, HALF], F32)) for i in range(2)]
        am_flat = AM[:, :, :, :].rearrange("p h e s -> p (h e s)")
        w_v = [am_flat[:, 0:8 * HALF].rearrange("p (c e) -> p c e", e=HALF),
               am_flat[:, 8 * HALF:12 * HALF].rearrange("p (c e) -> p c e", e=HALF),
               X[:, :, :].rearrange("p h s -> p (h s)").rearrange("p (c e) -> p c e", e=HALF)]

        streams_in = sem("streams_in")
        v_in = [sem(f"v_in{b}") for b in range(2)]
        wv_load, v_mm, v_ev = sem("wv_load"), sem("v_mm"), sem("v_ev")
        v_out = [sem(f"v_out{b}") for b in range(2)]
        cleared, y_cleared, xt_cleared = sem("cleared"), sem("y_cleared"), sem("xt_cleared")
        cum_mm, exp_done = sem("cum_mm"), sem("exp_done")
        prep_dve, prep_pool = sem("prep_dve"), sem("prep_pool")
        qb_mm, qb_ev, score_mm, score_ev = sem("qb_mm"), sem("qb_ev"), sem("score_mm"), sem("score_ev")
        blocks_out, blocks_in, base_step, base_done, base_out, base_in = (
            sem(n) for n in ("blocks_out", "blocks_in", "base_step", "base_done", "base_out", "base_in"))
        inv_mm = [sem(f"inv_mm{q}") for q in range(QUADS)]
        inv_ev = [sem(f"inv_ev{q}") for q in range(QUADS)]
        pt_full = [sem(f"pt_full{k}") for k in range(2)]
        pt_free = [sem(f"pt_free{k}") for k in range(2)]
        state_ready, summed, carried = sem("state_ready"), sem("summed"), sem("carried")
        sp_tick, dve_tick, pe_tick, pool_tick = sem("sp_tick"), sem("dve_tick"), sem("pe_tick"), sem("pool_tick")
        USES = 6
        STEPS = 3 * LEVELS
        STREAM_SUM = 16 * 5

        def chunk(i, b):
            return (TILES - 1) - i if b else i

        def rolled(eng, body):
            with eng.Fori(0, TILES - 1) as i:
                for b in range(2):
                    body(i, b, False)
            for b in range(2):
                body(TILES - 1, b, True)

        block = ctx.enter_context(nc.Block())

        @block.sync
        def _(sp):
            def load_streams(i, b):
                c = chunk(i, b)
                for s, src in ((SW_, scr["sw"][b, c]), (R_, scr["r"][c]), (KK_, scr["kk"][c]), (BZ_, scr["bz"][b, c]),
                               (KD_, scr["kd"][b, c])):
                    if len(src.shape) == 3:
                        src = src.rearrange("p c s -> p (c s)")
                    sp.dma_start(IN[:, s, :], src).then_inc(streams_in, 16)

            def base_blocks(n, b):
                sp.wait_ge(qb_ev, QUADS * (n + 1))
                for k in range(P // BASE):
                    rows = slice(BASE * k, BASE * k + BASE)
                    sp.dma_start(scr["blocks"][k].rearrange("h s t -> s h t"), QB[b][rows, :, rows]).then_inc(blocks_out, 16)
                sp.wait_ge(blocks_out, P * (n + 1))
                sp.dma_start(NB[:, :, :].rearrange("p s t -> p (s t)"),
                             scr["blocks"].rearrange("k h s t -> (k h) (s t)")).then_inc(blocks_in, 16)
                sp.wait_ge(base_done, n + 1)
                sp.dma_start(scr["inverses"].rearrange("k h s t -> (k h) (s t)"),
                             XB[:, :, :].rearrange("p s t -> p (s t)")).then_inc(base_out, 16)
                sp.wait_ge(base_out, 16 * (n + 1) + GIVEN)
                sp.wait_ge(xt_cleared, n + 1)
                for k in range(P // BASE):
                    rows = slice(BASE * k, BASE * k + BASE)
                    sp.dma_start(XT[rows, :, rows], scr["inverses"][k].rearrange("h s t -> s h t")).then_inc(base_in, 16)

            load_streams(0, 0)
            for k, half, part in ((0, 0, slice(0, 8)), (1, 1, slice(0, 4)), (2, 1, slice(4, 8))):
                sp.dma_start(w_v[k], io["rw_w_in"][0, 2].rearrange("(c p) e -> p c e", p=P)[:, part, HALF * half:HALF * half + HALF])\
                  .then_inc(wv_load, 16)
            sp.wait_ge(prep_dve, 1)
            sp.wait_ge(prep_pool, 1)
            load_streams(0, 1)
            for t in range(2):
                sp.wait_ge(v_ev, 2 * t + 2)
                sp.dma_start(scr["v"][t], V[t % 2][:, :]).then_inc(v_out[t % 2], 16)
            base_blocks(0, 0)
            for t in range(2, TILES):
                sp.wait_ge(v_ev, 2 * t + 2)
                sp.dma_start(scr["v"][t], V[t % 2][:, :]).then_inc(v_out[t % 2], 16)
            for t in range(2):
                sp.wait_ge(v_out[t], 16 * TILES // 2)
            sp.dma_start(V[0][:, :], scr["v"][0]).then_inc(v_in[0], 16)

            def body(i, b, last):
                n = 2 * i + b
                if last and b == 1:
                    return
                wait_alone(sp, pt_full[1], USES * n + GIVEN, sp_tick)
                sp.dma_start(V[1 - b][:, :], scr["v"][chunk(i + b, 1 - b)]).then_inc(v_in[1 - b], 16)
                if not last:
                    sp.wait_ge(prep_dve, n + 2)
                    wait_alone(sp, prep_pool, n + 2, sp_tick)
                    load_streams(i + 1, b)
                base_blocks(n + 1, 1 - b)

            rolled(sp, body)

        @block.gpsimd
        def _(pool):
            zeroed = Chain(pool, cleared)
            for e in range(2):
                zero = slice(HEAD * (1 - e), HEAD * (1 - e) + HEAD)
                zeroed.link(pool.memset(B[e][zero, :, :], 0.0))
                zeroed.link(pool.memset(KH[e][zero, :, :], 0.0))
            for b in range(2):
                zeroed.link(pool.memset(carry[b][:, :, :], 0.0))
            zeroed.link(pool.memset(state[:, :, :, :], 0.0))
            pool.memset(XT[:, :, :], 0.0).then_inc(xt_cleared, 1)
            pool.wait_ge(xt_cleared, 1)

            def prep(n, b):
                pool.wait_ge(exp_done, 4 * n + 4)
                pool.wait_ge(streams_in, STREAM_SUM * (n + 1))
                for dst, s in ((B, BZ_), (KH, KD_)):
                    for e in range(2):
                        rows = slice(HEAD * e, HEAD * e + HEAD)
                        last = pool.tensor_tensor(dst[e][rows, :, :], IN[rows, s, :].rearrange("p (c s) -> p c s", s=P),
                                                  grow[rows, :, :], ALU.mult)
                last.then_inc(prep_pool, 1)
                wait_alone(pool, prep_pool, n + 1, pool_tick)

            def base(n, b):
                per = 2 * BASE - 1
                done = 0

                def link(ins):
                    nonlocal done
                    done += 1
                    ins.then_inc(base_step, 1)
                    pool.wait_ge(base_step, per * n + done)

                pool.wait_ge(blocks_in, 16 * (n + 1))
                wait_alone(pool, base_out, 16 * n + GIVEN, pool_tick)
                link(pool.tensor_copy(XB[:, :, :].rearrange("p s t -> p (s t)"), con[:, C_EYE:C_EYE + BASE * BASE]))
                for k in range(BASE - 1):
                    r = k if b else BASE - 1 - k
                    rows, cols = (slice(r + 1, BASE), slice(0, r + 1)) if b else (slice(0, r), slice(r, BASE))
                    h, w = BASE - 1 - k, k + 1
                    link(pool.tensor_tensor(step_sum[:, 0:h, 0:w], NB[:, rows, r:r + 1].to_broadcast([P, h, w]),
                                            XB[:, r:r + 1, cols].to_broadcast([P, h, w]), ALU.mult))
                    into = XB[:, rows, cols]
                    link(pool.tensor_tensor(into, into, step_sum[:, 0:h, 0:w], ALU.add))
                pool.sem_inc(base_done, 1)

            prep(0, 0)
            pool.wait_ge(v_mm, 2 * TILES)
            pool.memset(y[:, :, :], 0.0).then_inc(y_cleared, 1)
            base(0, 0)

            def body(i, b, last):
                n = 2 * i + b
                if last and b == 1:
                    return
                for k in range(2):
                    pool.wait_ge(pt_full[k], USES * n + 2 + GIVEN)
                prep(n + 1, 1 - b)
                base(n + 1, 1 - b)
                for k in range(2):
                    wait_alone(pool, pt_full[k], USES * n + 4 + GIVEN, pool_tick)
                pool.memset(XT[:, :, :], 0.0).then_inc(xt_cleared, 1)
                wait_alone(pool, xt_cleared, n + 2, pool_tick)

            rolled(pool, body)

        @block.scalar
        def _(act):
            def decays(n, b, first_batch=False):
                first = P - 1 if b else 0
                for u in range(4):
                    act.wait_ge(cum_mm, 4 * n + u + 1)
                    if u == 0 and not first_batch:
                        act.wait_ge(prep_dve, n)
                        act.wait_ge(prep_pool, n)
                    two = pS[u % 2][:, :].rearrange("p (c e s) -> p c e s", e=2, s=P)
                    cs = slice(2 * u, 2 * u + 2)
                    act.activation(decay[:, cs].rearrange("p c e s -> p (c e s)"), pS[u % 2][:, :], ACT.Exp, scale=-DECAY)
                    act.activation(grow[:, cs, :], two[:, :, 0, :], ACT.Exp, scale=DECAY)
                    act.activation(p_mid[b][:, cs], two[:, :, 1, first], ACT.Exp, scale=DECAY).then_inc(exp_done, 1)

            decays(0, 0, True)
            for t in range(TILES):
                if t >= 2:
                    act.wait_ge(v_out[t % 2], 16 * (t // 2))
                for h in range(2):
                    act.wait_ge(v_mm, 2 * t + h + 1)
                    act.activation(V[t % 2][:, HALF * h:HALF * h + HALF], pT[h][:, :], ACT.Copy).then_inc(v_ev, 1)

            def body(i, b, last):
                n = 2 * i + b
                for u in range(4):
                    k, cs = u % 2, slice(4 * (u // 2), 4 * (u // 2) + 4)
                    act.wait_ge(pt_full[k], USES * n + u // 2 + 1 + GIVEN)
                    act.activation(TK[:, cs, :, k, :], pT[k][:, :].rearrange("p (c e v) -> p c e v", e=2, v=HEAD),
                                   ACT.Copy).then_inc(pt_free[k], 1)
                for h in range(2):
                    act.wait_ge(pt_full[h], USES * n + 3 + GIVEN)
                    act.activation(RN[:, h, :], pT[h][:, :], ACT.Copy, scale=-1.0).then_inc(pt_free[h], 1)
                if not (last and b):
                    decays(n + 1, 1 - b)
                for lev in range(LEVELS):
                    for q in range(QUADS):
                        act.wait_ge(inv_mm[q], STEPS * n + 3 * lev + 1)
                        dst = X if lev == 0 else XT
                        act.activation(dst[:, 4 * q:4 * q + 4, :].rearrange("p h s -> p (h s)"), pI[q][:, :],
                                       ACT.Copy).then_inc(inv_ev[q], 1)
                for h in range(2):
                    act.wait_ge(pt_full[h], USES * n + 4 + GIVEN)
                    act.activation(UN[:, h, :], pT[h][:, :], ACT.Copy).then_inc(pt_free[h], 1)

            rolled(act, body)

        @block.tensor
        def _(pe):
            for k in range(2):
                pe.sem_inc(pt_full[k], GIVEN)

            def cumulate(n, b):
                pe.wait_ge(streams_in, STREAM_SUM * (n + 1))
                for u in range(4):
                    if u >= 2:
                        pe.wait_ge(exp_done, 4 * n + u - 1)
                    for c in range(2):
                        last = pe.matmul(pS[u % 2][:, 2 * P * c:2 * P * c + 2 * P], IN[:, SW_, P * (2 * u + c):P * (2 * u + c + 1)],
                                         con[:, C_CUM + 2 * P * b:C_CUM + 2 * P * (b + 1)], start=True, stop=True)
                    last.then_inc(cum_mm, 1)

            def scores_qb(n, b):
                pe.wait_ge(prep_dve, n + 1)
                pe.wait_ge(prep_pool, n + 1)
                for q in range(QUADS):
                    pe.wait_ge(exp_done, 4 * (n + 1))
                    if q >= 2:
                        pe.wait_ge(qb_ev, QUADS * n + q - 1)
                    for k in range(4):
                        j = 4 * q + k
                        mm = pe.matmul(pS[q % 2][:, P * k:P * k + P], B[j % 2][:, j // 2, :], QR[b][:, j // 2, 0, :], start=True, stop=True)
                    mm.then_inc(qb_mm, 1)

            def project_v(t):
                for h in range(2):
                    if t:
                        pe.wait_ge(v_ev, 2 * t + h - 1)
                    for k in range(DC):
                        w = w_v[0][:, k, :] if h == 0 else w_v[1 + k // 4][:, k % 4, :]
                        mm = pe.matmul(pT[h][:, :], y[:, :, :].rearrange("p t d -> p (t d)")[:, SEQ * k + P * t:SEQ * k + P * t + P], w,
                                       start=k == 0, stop=k == DC - 1)
                    mm.then_inc(v_mm, 1)

            cumulate(0, 0)
            pe.wait_ge(wv_load, 16 * 3)
            project_v(0)
            project_v(1)
            pe.wait_ge(cleared, 7)
            scores_qb(0, 0)
            project_v(2)
            project_v(3)
            pe.wait_ge(v_ev, 2 * TILES)

            def body(i, b, last):
                n = 2 * i + b
                v = V[b][:, :]
                for j in range(HEADS):
                    c, e, bank = j // 2, j % 2, pS[j % 2]
                    pe.wait_ge(*((score_ev, HEADS * n + j - 1) if j >= 2 else (qb_ev, QUADS * (n + 1))))
                    pe.matmul(bank[:, 0:P], B[e][:, c, :], QR[b][:, c, 1, :], start=True, stop=True)
                    pe.matmul(bank[:, P:3 * P], KH[e][:, c, :], QR[b][:, c].rearrange("k e s -> k (e s)"),
                              start=True, stop=True).then_inc(score_mm, 1)
                for u in range(4):
                    k = u % 2
                    wait_alone(pe, pt_free[k], USES * n + u // 2 + GIVEN, pe_tick)
                    rows = slice(HEAD * k, HEAD * k + HEAD)
                    for c in range(4):
                        for e, src in enumerate((B[k], KH[k])):
                            at = HEAD * (2 * c + e)
                            tr = pe.transpose(pT[k][:, at:at + HEAD], src[rows, 4 * (u // 2) + c, :], con[rows, C_ID + HEAD * k:C_ID + HEAD * k + HEAD])
                    tr.then_inc(pt_full[k], 1)
                pe.wait_ge(score_ev, HEADS * (n + 1))
                pe.wait_ge(state_ready, n + 1)
                pe.wait_ge(v_in[b], 16 * (i + 1))
                for h in range(2):
                    pe.wait_ge(pt_free[h], USES * n + 2 + GIVEN)
                    for c in range(DC):
                        j, at = 2 * c + h, HEAD * c
                        pe.matmul(pT[h][:, at:at + HEAD], QR[b][:, c, 0, :], state[:, c, h, :], start=True, stop=False)
                        mm = pe.matmul(pT[h][:, at:at + HEAD], AM[:, j, 1, :], v[:, HEAD * j:HEAD * j + HEAD], start=False, stop=True)
                    mm.then_inc(pt_full[h], 1)
                if not (last and b):
                    cumulate(n + 1, 1 - b)

                def per_head(q, step, lhsT, rhs):
                    pe.wait_ge(inv_ev[q], STEPS * n + step - 1 + GIVEN)
                    for k in range(4):
                        j = 4 * q + k
                        dst = pI[q][:, P * k:P * k + P]
                        if rhs is None:
                            mm = pe.transpose(dst, lhsT[:, j, :], con[:, C_ID:C_ID + P])
                        else:
                            mm = pe.matmul(dst, lhsT[:, j, :], rhs[:, j, :], start=True, stop=True)
                    mm.then_inc(inv_mm[q], 1)

                pe.wait_ge(base_in, P * (n + 1))
                for q in range(QUADS):
                    per_head(q, 1, XT, None)
                for lev in range(1, LEVELS + 1):
                    at = 3 * lev - 1
                    for q in range(QUADS):
                        per_head(q, at, QB[b], X)
                    for q in range(QUADS):
                        if lev < LEVELS:
                            per_head(q, at + 1, XT, W)
                        else:
                            per_head(q, at + 1, W, XT)
                    if lev < LEVELS:
                        for q in range(QUADS):
                            per_head(q, at + 2, X, None)
                    if lev == LEVELS - 1 and not (last and b):
                        scores_qb(n + 1, 1 - b)
                for h in range(2):
                    pe.wait_ge(pt_free[h], USES * n + 3 + GIVEN)
                    for q in range(QUADS):
                        pe.wait_ge(inv_ev[q], STEPS * (n + 1) + GIVEN)
                    for c in range(DC):
                        mm = pe.matmul(pT[h][:, HEAD * c:HEAD * c + HEAD], XT[:, 2 * c + h, :], RN[:, h, HEAD * c:HEAD * c + HEAD],
                                       start=True, stop=True)
                    mm.then_inc(pt_full[h], 1)
                for h in range(2):
                    pe.wait_ge(pt_free[h], USES * n + 4 + GIVEN)
                    for c in range(DC):
                        j, at = 2 * c + h, HEAD * c
                        dst = pT[h][:, at:at + HEAD]
                        pe.matmul(dst, QR[b][:, c, 1, :], state[:, c, h, :], start=True, stop=False)
                        pe.matmul(dst, AM[:, j, 2, :], v[:, HEAD * j:HEAD * j + HEAD], start=False, stop=False)
                        mm = pe.matmul(dst, AM[:, j, 0, :], UN[:, h, at:at + HEAD], start=False, stop=True)
                    mm.then_inc(pt_full[h], 1)
                for h in range(2):
                    pe.wait_ge(pt_free[h], USES * n + 5 + GIVEN)
                    for k in range(4):
                        c = 4 * h + k
                        dst = pT[h][:, P * k:P * k + P]
                        pe.matmul(dst, TK[:, c, 1].rearrange("p e v -> p (e v)"), v[:, P * c:P * c + P], start=True, stop=False)
                        mm = pe.matmul(dst, TK[:, c, 0].rearrange("p e v -> p (e v)"), UN[:, :, HEAD * c:HEAD * c + HEAD],
                                       start=False, stop=True)
                    mm.then_inc(pt_full[h], 1)

            rolled(pe, body)

        @block.vector
        def _(dve):
            for k in range(2):
                dve.sem_inc(pt_free[k], GIVEN)
            for q in range(QUADS):
                dve.sem_inc(inv_ev[q], GIVEN)
            dve.sem_inc(base_out, GIVEN)
            dve.sem_inc(carried, GIVEN)

            def prep(n, b):
                last_col = 0 if b else P - 1
                dve.wait_ge(exp_done, 4 * n + 4)
                dve.wait_ge(streams_in, STREAM_SUM * (n + 1))
                dve.tensor_tensor(QR[b][:, :, 0, :], IN[:, KK_, :].rearrange("p (c s) -> p c s", s=P), decay[:, :, 1, :], ALU.mult)
                dve.tensor_tensor(QR[b][:, :, 1, :], IN[:, R_, :].rearrange("p (c s) -> p c s", s=P), decay[:, :, 0, :], ALU.mult)
                dve.tensor_copy(p_end[b][:, :], decay[:, :, 0, last_col]).then_inc(prep_dve, 1)

            def mask_qb(n, b):
                at = C_SCORE + 4 * P * b
                for q in range(QUADS):
                    dve.wait_ge(qb_mm, QUADS * n + q + 1)
                    dve.tensor_tensor(QB[b][:, 4 * q:4 * q + 4, :], pS[q % 2][:, :].rearrange("p (h s) -> p h s", s=P),
                                      con[:, at:at + P].unsqueeze(1).to_broadcast([P, 4, P]), ALU.mult).then_inc(qb_ev, 1)

            prep(0, 0)
            mask_qb(0, 0)
            dve.wait_ge(cleared, 7)
            dve.wait_ge(y_cleared, 1)

            def body(i, b, last):
                n = 2 * i + b
                dve.wait_ge(carried, n + GIVEN)
                for e in range(2):
                    rows = slice(HEAD * e, HEAD * e + HEAD)
                    ins = dve.tensor_tensor(state[rows, :, e, :], carry[b][rows, :, :],
                                            p_mid[b][rows, :].unsqueeze(2).to_broadcast([HEAD, DC, HEAD]), ALU.mult)
                ins.then_inc(state_ready, 1)
                at = C_SCORE + 4 * P * b + P
                for j in range(HEADS):
                    dve.wait_ge(score_mm, HEADS * n + j + 1)
                    dve.tensor_tensor(AM[:, j].rearrange("p e s -> p (e s)"), pS[j % 2][:, 0:3 * P], con[:, at:at + 3 * P],
                                      ALU.mult).then_inc(score_ev, 1)
                for lev in range(1, LEVELS + 1):
                    at = C_LEVEL + P * (lev - 1)
                    for q in range(QUADS):
                        dve.wait_ge(inv_mm[q], STEPS * n + 3 * lev - 1)
                        dve.tensor_tensor(W[:, 4 * q:4 * q + 4, :], pI[q][:, :].rearrange("p (h s) -> p h s", s=P),
                                          con[:, at:at + P].unsqueeze(1).to_broadcast([P, 4, P]), ALU.mult).then_inc(inv_ev[q], 1)
                    for q in range(QUADS):
                        dve.wait_ge(inv_mm[q], STEPS * n + 3 * lev)
                        into = (X if lev < LEVELS else XT)[:, 4 * q:4 * q + 4, :].rearrange("p h s -> p (h s)")
                        dve.tensor_tensor(into, into, pI[q][:, :], ALU.add).then_inc(inv_ev[q], 1)
                    if not (last and b):
                        if lev == LEVELS - 2:
                            prep(n + 1, 1 - b)
                        if lev == LEVELS - 1:
                            mask_qb(n + 1, 1 - b)
                for h in range(2):
                    wait_alone(dve, pt_full[h], USES * n + 5 + GIVEN, dve_tick)
                    cols = y[:, bass.ds(chunk(i, b), 1), :].rearrange("p a (c e v) -> p (a c) e v", e=2, v=HEAD)[:, :, h, :]
                    dve.tensor_tensor(cols, cols, pT[h][:, :].rearrange("p (c v) -> p c v", v=HEAD), ALU.add).then_inc(pt_free[h], 1)
                for h in range(2):
                    dve.wait_ge(pt_full[h], USES * (n + 1) + GIVEN)
                    for e in range(2):
                        rows, cs = slice(HEAD * e, HEAD * e + HEAD), slice(4 * h, 4 * h + 4)
                        ins = dve.tensor_tensor(carry[b][rows, cs, :], state[rows, cs, e, :],
                                                pT[h][rows, :].rearrange("p (c e v) -> p c e v", e=2, v=HEAD)[:, :, e, :], ALU.add)
                    ins.then_inc(pt_free[h], 1)
                for h in range(2):
                    dve.wait_ge(pt_free[h], USES * (n + 1) + GIVEN)
                dve.tensor_tensor(carry[b][:, :, :], carry[b][:, :, :], p_end[b][:, :].unsqueeze(2).to_broadcast([P, DC, HEAD]),
                                  ALU.mult).then_inc(carried, 1)

            rolled(dve, body)


WEIGHT_BLOCKS = 6
RING = 3


def weight_block(io, expert, m):
    half = slice(D * (m // 2), D * (m // 2) + D) if m < 4 else slice(D * (m - 4), D * (m - 4) + D)
    if m < 4:
        w = io["exp_w_gate" if m % 2 == 0 else "exp_w_up"]
        return w[0, bass.ds(expert, 1), :, half].rearrange("a (c p) f -> p (a c) f", p=P)
    return io["exp_w_down"][0, bass.ds(expert, 1), half, :].rearrange("a (c p) d -> p (a c) d", p=P)


def mix_output(nc, io, scr, keep):
    con, y, res, bonus = keep["con"], keep["y"], keep["res"], keep["bonus"]
    ident = con[:, C_ID:C_ID + P]
    with ExitStack() as ctx:
        def sb(name, *shape):
            return ctx.enter_context(nc.sbuf_tensor(name, list(shape), F32))

        def sem(name):
            return ctx.enter_context(nc.semaphore(name))

        w_out = keep["ring"][:, RING - 1]
        rows = sb("rows", P, 3, D)
        g2 = sb("g2", P, D)
        w_router = sb("w_router", P, DC, EXPERTS)
        v_in = sb("v_in", P, 2, D)
        part = sb("part", P, D)
        turned_in = sb("turned_in", P, DC, P)
        h2T = sb("h2T", P, DC, P)
        head_stat = sb("head_stat", P, 4, HEADS)
        stat = sb("mo_stat", P, 4, TILES)
        prob = sb("prob", P, EXPERTS)
        soft = sb("soft", P, 4)
        affT, work = sb("affT", EXPERTS, SEQ), sb("work", EXPERTS, 2, SEQ)
        top8 = sb("top8", EXPERTS, 2, 8)
        mask = sb("mask", P, TILES, EXPERTS)
        ps = [ctx.enter_context(nc.psum_tensor(f"mo_ps{i}", [P, HALF], F32)) for i in range(8)]

        row_load, w_load, v_load = sem("mo_row_load"), sem("mo_w_load"), [sem(f"mo_v_load{k}") for k in range(2)]
        x_load = sem("mo_x_load")
        chain_s, act_step, dve_step = sem("mo_chain"), sem("act_step"), sem("dve_step")
        gate_mm, gated = sem("gate_mm"), sem("gated")
        turn1, turn1_ev, out_mm, added = sem("turn1"), sem("turn1_ev"), sem("out_mm"), sem("added")
        h2_done, turn2, turn2_ev, logit_mm, prob_done = sem("h2_done"), sem("turn2"), sem("turn2_ev"), sem("logit_mm"), sem("prob_done")
        aff_turn, mask_done, mask_turn, mask_ev, count_mm = (sem(n) for n in ("aff_turn", "mask_done", "mask_turn", "mask_ev", "count_mm"))
        bonus_done = sem("bonus_done")
        block = ctx.enter_context(nc.Block())

        @block.sync
        def _(sp):
            for t in range(TILES):
                if t >= 2:
                    sp.wait_ge(gated, 2 * (t - 1))
                sp.dma_start(v_in[:, t % 2, :], scr["v"][t]).then_inc(v_load[t % 2], 16)
                if t == 0:
                    for i, name in enumerate(("rw_lnx_g", "rw_lnx_b", "norm_ffn_g")):
                        sp.dma_start(rows[:, i, :], io[name][0].partition_broadcast(P)).then_inc(row_load, 16)
                    sp.dma_start(g2[:, :], io["rw_g2"][0]).then_inc(row_load, 16)
                    sp.dma_start(w_router[:, :, :], io["router_w"][0].rearrange("(c p) e -> p c e", p=P)).then_inc(row_load, 16)
                    sp.dma_start(res[:, :, :], io["x"].rearrange("b (t p) d -> p (b t) d", p=P)).then_inc(x_load, 16)
                    sp.dma_start(w_out, io["rw_w_out"][0].rearrange("(c p) e -> p c e", p=P)).then_inc(w_load, 16)
                    for m in range(RING - 1):
                        for half in range(2):
                            ks = slice(4 * half, 4 * half + 4)
                            sp.dma_start(keep["ring"][:, m, ks, :], weight_block(io, 0, m)[:, ks, :]).then_inc(keep["landed"][m], 16)
            sp.wait_ge(out_mm, TILES)
            for half in range(2):
                ks = slice(4 * half, 4 * half + 4)
                sp.dma_start(keep["ring"][:, 2, ks, :], weight_block(io, 0, 2)[:, ks, :]).then_inc(keep["landed"][2], 16)

        @block.gpsimd
        def _(pool):
            for t in range(TILES):
                pool.wait_ge(v_load[t % 2], 16 * (t // 2 + 1))
                v3 = v_in[:, t % 2, :].rearrange("p (h v) -> p h v", v=HEAD)
                pool.tensor_tensor(v3, v3, bonus[:, t, :].unsqueeze(2).to_broadcast([P, HEADS, HEAD]), ALU.mult).then_inc(bonus_done, 1)

        @block.scalar
        def _(act):
            steps = 0
            for t in range(TILES):
                act.wait_ge(dve_step, 4 * t + 1)
                act.activation(part[:, :], y[:, t, :], ACT.Square).then_inc(act_step, 1)
                act.wait_ge(dve_step, 4 * t + 2)
                act.activation(head_stat[:, 3, :], head_stat[:, 2, :], ACT.Sqrt).then_inc(act_step, 1)
                for g in range(2):
                    act.wait_ge(turn1, 2 * t + g + 1)
                    act.activation(turned_in[:, 4 * g:4 * g + 4, :].rearrange("p c s -> p (c s)"), ps[2 + g][:, :], ACT.Copy).then_inc(turn1_ev, 1)
                act.wait_ge(added, 2 * t + 2)
                act.activation(part[:, :], res[:, t, :], ACT.Square, accum_out=stat[:, 0, t:t + 1]).then_inc(act_step, 1)
                act.wait_ge(dve_step, 4 * t + 3)
                act.activation(stat[:, 2, t:t + 1], stat[:, 1, t:t + 1], ACT.Sqrt).then_inc(act_step, 1)
                for g in range(2):
                    act.wait_ge(turn2, 2 * t + g + 1)
                    act.activation(h2T[:, 4 * g:4 * g + 4, :].rearrange("p c s -> p (c s)"), ps[2 + g][:, :], ACT.Copy).then_inc(turn2_ev, 1)
                act.wait_ge(dve_step, 4 * t + 4)
                act.activation(prob[:, :], ps[6][:, 0:EXPERTS], ACT.Exp, bias=soft[:, 0:1], accum_out=soft[:, 1:2]).then_inc(act_step, 1)

        @block.tensor
        def _(pe):
            pe.wait_ge(row_load, 16 * 5)
            for t in range(TILES):
                for h in range(2):
                    if t:
                        pe.wait_ge(gated, 2 * (t - 1) + h + 1)
                    pe.matmul(ps[h][:, :], keep["gate_low"][:, P * t:P * t + P], g2[:, HALF * h:HALF * h + HALF],
                              start=True, stop=True).then_inc(gate_mm, 1)
                for g in range(2):
                    pe.wait_ge(gated, 2 * t + g + 1)
                    if t:
                        pe.wait_ge(turn2_ev, 2 * t)
                    for c in range(4):
                        k = 4 * g + c
                        mm = pe.transpose(ps[2 + g][:, P * c:P * c + P], y[:, t, P * k:P * k + P], ident)
                    mm.then_inc(turn1, 1)
                pe.wait_ge(turn1_ev, 2 * t + 2)
                pe.wait_ge(w_load, 16)
                if t:
                    pe.wait_ge(added, 2 * t)
                for h in range(2):
                    for c in range(DC):
                        mm = pe.matmul(ps[4 + h][:, :], turned_in[:, c, :], w_out[:, c, HALF * h:HALF * h + HALF], start=c == 0, stop=c == DC - 1)
                mm.then_inc(out_mm, 1)
                pe.wait_ge(h2_done, t + 1)
                for g in range(2):
                    for c in range(4):
                        k = 4 * g + c
                        mm = pe.transpose(ps[2 + g][:, P * c:P * c + P], y[:, t, P * k:P * k + P], ident)
                    mm.then_inc(turn2, 1)
                pe.wait_ge(turn2_ev, 2 * t + 2)
                if t:
                    pe.wait_ge(prob_done, t)
                for c in range(DC):
                    mm = pe.matmul(ps[6][:, 0:EXPERTS], h2T[:, c, :], w_router[:, c, :], start=c == 0, stop=c == DC - 1)
                mm.then_inc(logit_mm, 1)
            pe.wait_ge(prob_done, TILES)
            for t in range(TILES):
                mm = pe.transpose(ps[7][0:EXPERTS, P * t:P * t + P], keep["aff"][:, t, :], ident)
            mm.then_inc(aff_turn, 1)
            pe.wait_ge(mask_done, 1)
            for t in range(TILES):
                mm = pe.transpose(ps[6][:, EXPERTS * t:EXPERTS * t + EXPERTS], affT[:, P * t:P * t + P], ident[0:EXPERTS, 0:EXPERTS])
            mm.then_inc(mask_turn, 1)
            pe.wait_ge(mask_ev, 1)
            for t in range(TILES):
                for s in range(t + 1):
                    tri = C_TRI if s == t else C_ONES
                    mm = pe.matmul(ps[7][:, EXPERTS * t:EXPERTS * t + EXPERTS], con[:, tri:tri + P], mask[:, s, :], start=s == 0, stop=s == t)
            mm.then_inc(count_mm, 1)

        @block.vector
        def _(dve):
            chain = Chain(dve, chain_s)
            for t in range(TILES):
                yt = y[:, t, :]
                y3 = yt.rearrange("p (h v) -> p h v", v=HEAD)
                p3 = part[:, :].rearrange("p (h v) -> p h v", v=HEAD)

                def spread(i):
                    return head_stat[:, i, :].unsqueeze(2).to_broadcast([P, HEADS, HEAD])

                chain.link(dve.tensor_reduce(head_stat[:, 0, :], y3, AX_X, ALU.add))
                chain.link(dve.tensor_scalar(head_stat[:, 1, :], head_stat[:, 0, :], 1.0 / HEAD, None, ALU.mult))
                if t:
                    dve.wait_ge(act_step, 5 * t)
                dve.tensor_tensor(y3, y3, spread(1), ALU.subtract).then_inc(dve_step, 1)
                dve.wait_ge(act_step, 5 * t + 1)
                chain.link(dve.tensor_reduce(head_stat[:, 0, :], p3, AX_X, ALU.add))
                dve.tensor_scalar(head_stat[:, 2, :], head_stat[:, 0, :], 1.0 / HEAD, LNX_EPS, ALU.mult, ALU.add).then_inc(dve_step, 1)
                dve.wait_ge(act_step, 5 * t + 2)
                chain.link(dve.reciprocal(head_stat[:, 1, :], head_stat[:, 3, :]))
                chain.link(dve.tensor_tensor(y3, y3, spread(1), ALU.mult))
                if t == 0:
                    dve.wait_ge(row_load, 16 * 5)
                chain.link(dve.tensor_tensor(yt, yt, rows[:, 0, :], ALU.mult))
                chain.link(dve.tensor_tensor(yt, yt, rows[:, 1, :], ALU.add))
                dve.wait_ge(bonus_done, t + 1)
                chain.link(dve.tensor_tensor(yt, yt, v_in[:, t % 2, :], ALU.add))
                for h in range(2):
                    cols = slice(HALF * h, HALF * h + HALF)
                    dve.wait_ge(gate_mm, 2 * t + h + 1)
                    dve.tensor_tensor(y[:, t, cols], y[:, t, cols], ps[h][:, :], ALU.mult).then_inc(gated, 1)
                dve.wait_ge(out_mm, t + 1)
                if t == 0:
                    dve.wait_ge(x_load, 16)
                for h in range(2):
                    cols = slice(HALF * h, HALF * h + HALF)
                    dve.tensor_tensor(res[:, t, cols], res[:, t, cols], ps[4 + h][:, :], ALU.add).then_inc(added, 1)
                dve.wait_ge(act_step, 5 * t + 3)
                dve.tensor_scalar(stat[:, 1, t:t + 1], stat[:, 0, t:t + 1], 1.0 / D, EPS, ALU.mult, ALU.add).then_inc(dve_step, 1)
                dve.wait_ge(act_step, 5 * t + 4)
                chain.link(dve.reciprocal(stat[:, 3, t:t + 1], stat[:, 2, t:t + 1]))
                dve.scalar_tensor_tensor(out=yt, in0=res[:, t, :], scalar=stat[:, 3, t:t + 1], in1=rows[:, 2, :],
                                         op0=ALU.mult, op1=ALU.mult).then_inc(h2_done, 1)
                dve.wait_ge(logit_mm, t + 1)
                dve.tensor_reduce(soft[:, 0:1], ps[6][:, 0:EXPERTS], AX_X, ALU.max, negate=True).then_inc(dve_step, 1)
                dve.wait_ge(act_step, 5 * t + 5)
                chain.link(dve.reciprocal(soft[:, 2:3], soft[:, 1:2]))
                dve.tensor_scalar(keep["aff"][:, t, :], prob[:, :], soft[:, 2:3], None, ALU.mult).then_inc(prob_done, 1)
            dve.wait_ge(aff_turn, 1)
            chain.link(dve.tensor_copy(work[:, 0, :], ps[7][0:EXPERTS, :]))
            for r in range(CAP // 8):
                chain.link(dve.max(top8[:, r % 2, :], work[:, r % 2, :]))
                chain.link(dve.match_replace(work[:, (r + 1) % 2, :], top8[:, r % 2, :], work[:, r % 2, :], -1.0))
            dve.tensor_scalar(affT[:, :], work[:, 0, :], 0.0, None, ALU.is_lt).then_inc(mask_done, 1)
            dve.wait_ge(mask_turn, 1)
            dve.tensor_copy(mask[:, :, :].rearrange("p t e -> p (t e)"), ps[6][:, 0:TILES * EXPERTS]).then_inc(mask_ev, 1)
            dve.wait_ge(mask_ev, 1)
            dve.wait_ge(count_mm, 1)
            slot = keep["slot"][:, :, :].rearrange("p t e -> p (t e)")
            chain.link(dve.tensor_tensor(slot, ps[7][:, 0:TILES * EXPERTS], mask[:, :, :].rearrange("p t e -> p (t e)"), ALU.mult))
            chain.link(dve.tensor_scalar(slot, slot, -1.0, None, ALU.add))


def experts(nc, io, keep):
    con, h2, res, ring, landed = keep["con"], keep["y"], keep["res"], keep["ring"], keep["landed"]
    ident = con[:, C_ID:C_ID + P]
    with ExitStack() as ctx:
        def sb(name, *shape):
            return ctx.enter_context(nc.sbuf_tensor(name, list(shape), F32))

        def sem(name):
            return ctx.enter_context(nc.semaphore(name))

        pick = sb("pick", P, TILES, 2, CAP)
        gated_pick = sb("gated_pick", P, TILES, 2, CAP)
        scatter = sb("scatter", P, SEQ)
        xin = sb("xin", P, DC, 2, CAP)
        silu = sb("silu", P, HALF)
        hid = sb("hid", P, 2, HALF)
        hidT = sb("hidT", P, 2, 4, P)
        yexp = sb("yexp", P, D)
        pG, pU = (ctx.enter_context(nc.psum_tensor(n, [P, HALF], F32)) for n in ("pG", "pU"))
        pD, pX, pO = ([ctx.enter_context(nc.psum_tensor(f"{n}{i}", [P, HALF], F32)) for i in range(2)] for n in ("pD", "pX", "pO"))

        picked, gate_picked = sem("picked"), sem("gate_picked")
        gath_mm, gath_ev = sem("gath_mm"), sem("gath_ev")
        scat_turn, scat_ev = sem("scat_turn"), sem("scat_ev")
        gate_mm, up_mm, silu_done, hid_done = sem("e_gate_mm"), sem("up_mm"), sem("silu_done"), sem("e_hid_done")
        hid_turn, hid_ev = sem("hid_turn"), sem("hid_ev")
        down_mm, down_ev = sem("down_mm"), sem("down_ev")
        scat_mm, scat_add = sem("scat_mm"), sem("scat_add")
        sp_tick = sem("e_sp_tick")
        PAIRS = EXPERTS // 2
        PER = 2 * WEIGHT_BLOCKS
        TURNS = PER // RING

        block = ctx.enter_context(nc.Block())

        @block.sync
        def _(sp):
            def body(i, last):
                for m in range(RING, PER if last else PER + RING):
                    slot = m % RING
                    e = 2 * i + m // WEIGHT_BLOCKS
                    before = m - RING
                    n, kind = 2 * i + before // WEIGHT_BLOCKS, before % WEIGHT_BLOCKS
                    if kind < 4:
                        wait_alone(sp, (gate_mm, up_mm)[kind % 2], 2 * n + kind // 2 + 1, sp_tick)
                    else:
                        wait_alone(sp, down_mm, 2 * n + kind - 3, sp_tick)
                    for half in range(2):
                        ks = slice(4 * half, 4 * half + 4)
                        sp.dma_start(ring[:, slot, ks, :], weight_block(io, e, m % WEIGHT_BLOCKS)[:, ks, :]).then_inc(landed[slot], 16)

            with sp.Fori(0, PAIRS - 1) as i:
                body(i, False)
            body(PAIRS - 1, True)

        @block.tensor
        def _(pe):
            for given in (gath_mm, scat_turn, hid_turn):
                pe.sem_inc(given, GIVEN)

            def body(i):
                def block_of(e, m):
                    n = WEIGHT_BLOCKS * e + m
                    slot = n % RING
                    pe.wait_ge(landed[slot], 32 * (TURNS * i + n // RING + 1))
                    return ring[:, slot]

                pe.wait_ge(picked, i + 1)
                for g in range(2):
                    pe.wait_ge(gath_ev, 2 * i + GIVEN)
                    pe.wait_ge(scat_ev, 2 * i + GIVEN)
                    pe.wait_ge(hid_ev, 4 * i + GIVEN)
                    for c in range(4):
                        k = 4 * g + c
                        for t in range(TILES):
                            mm = pe.matmul(pX[g][:, P * c:P * c + P], h2[:, t, P * k:P * k + P],
                                           pick[:, t].rearrange("p e s -> p (e s)"), start=t == 0, stop=t == TILES - 1)
                    mm.then_inc(gath_mm, 1)
                for e in range(2):
                    n = 2 * i + e

                    def up_down(which, psum, m):
                        w = block_of(e, m)
                        for k in range(DC):
                            for s in range(2):
                                mm = pe.matmul(psum[HEAD * s:HEAD * s + HEAD, :], xin[:, k, e, :], w[:, k, HALF * s:HALF * s + HALF],
                                               start=k == 0, stop=k == DC - 1)
                        mm.then_inc(which, 1)

                    def turn(j):
                        pe.wait_ge(hid_done, 2 * n + j + 1 + GIVEN)
                        for c in range(4):
                            mm = pe.transpose(pX[j][:, P * c:P * c + P], hid[:, j, P * c:P * c + P], ident)
                        mm.then_inc(hid_turn, 1)

                    def down(j):
                        w = block_of(e, 4 + j)
                        pe.wait_ge(hid_ev, 2 * n + j + 1 + GIVEN)
                        if j == 0:
                            pe.wait_ge(down_ev, 2 * n + GIVEN)
                        for c in range(4):
                            for h in range(2):
                                for s in range(2):
                                    mm = pe.matmul(pD[h][HEAD * s:HEAD * s + HEAD, :], hidT[:, j, c, HEAD * s:HEAD * s + HEAD],
                                                   w[:, 4 * s + c, HALF * h:HALF * h + HALF], start=j == 0 and c == 0, stop=j == 1 and c == 3)
                        mm.then_inc(down_mm, 1)

                    pe.wait_ge(gath_ev, 2 * i + 2 + GIVEN)
                    pe.wait_ge(silu_done, 2 * n + GIVEN)
                    up_down(gate_mm, pG, 0)
                    pe.wait_ge(gate_picked, n + 1 + GIVEN)
                    for t in range(TILES):
                        mm = pe.transpose(pX[0][:, P * t:P * t + P], gated_pick[:, t].rearrange("p e s -> p (e s)"), ident)
                    mm.then_inc(scat_turn, 1)
                    pe.wait_ge(hid_done, 2 * n + GIVEN)
                    up_down(up_mm, pU, 1)
                    pe.wait_ge(silu_done, 2 * n + 1 + GIVEN)
                    up_down(gate_mm, pG, 2)
                    pe.wait_ge(scat_ev, n + 1 + GIVEN)
                    turn(0)
                    up_down(up_mm, pU, 3)
                    down(0)
                    turn(1)
                    down(1)
                    pe.wait_ge(down_ev, 2 * n + 2 + GIVEN)
                    for u in range(2 * TILES):
                        t, h = u // 2, u % 2
                        if u >= 2:
                            pe.wait_ge(scat_add, 2 * TILES * n + u - 1 + GIVEN)
                        else:
                            pe.wait_ge(scat_add, 2 * TILES * n + GIVEN)
                        pe.matmul(pO[h][:, :], scatter[:, P * t:P * t + P], yexp[:, HALF * h:HALF * h + HALF], start=True,
                                  stop=True).then_inc(scat_mm, 1)

            with pe.Fori(0, PAIRS) as i:
                body(i)

        @block.scalar
        def _(act):
            for given in (gath_ev, scat_ev, hid_ev, silu_done, down_ev):
                act.sem_inc(given, GIVEN)

            def body(i):
                for g in range(2):
                    act.wait_ge(gath_mm, 2 * i + g + 1 + GIVEN)
                    act.activation(xin[:, 4 * g:4 * g + 4].rearrange("p c e s -> p (c e s)"), pX[g][:, :], ACT.Copy).then_inc(gath_ev, 1)
                for e in range(2):
                    n = 2 * i + e
                    for j in range(2):
                        act.wait_ge(gate_mm, 2 * n + j + 1)
                        act.wait_ge(hid_done, 2 * n + j + GIVEN)
                        act.activation(silu[:, :], pG[:, :], ACT.Silu).then_inc(silu_done, 1)
                        if j == 0:
                            act.wait_ge(scat_turn, n + 1 + GIVEN)
                            act.activation(scatter[:, :], pX[0][:, :], ACT.Copy).then_inc(scat_ev, 1)
                    for j in range(2):
                        act.wait_ge(hid_turn, 2 * n + j + 1 + GIVEN)
                        act.activation(hidT[:, j].rearrange("p c s -> p (c s)"), pX[j][:, :], ACT.Copy).then_inc(hid_ev, 1)
                    act.wait_ge(down_mm, 2 * n + 2)
                    for h in range(2):
                        act.activation(yexp[:, HALF * h:HALF * h + HALF], pD[h][:, :], ACT.Copy).then_inc(down_ev, 1)

            with act.Fori(0, PAIRS) as i:
                body(i)

        @block.vector
        def _(dve):
            for given in (hid_done, scat_add, gate_picked):
                dve.sem_inc(given, GIVEN)

            iota = con[:, C_IOTA:C_IOTA + CAP]

            def body(i):
                dve.wait_ge(gath_mm, 2 * i + GIVEN)
                dve.wait_ge(gate_picked, 2 * i + GIVEN)
                dve.tensor_tensor(pick[:, :, :, :], iota.unsqueeze(1).unsqueeze(1).to_broadcast([P, TILES, 2, CAP]),
                                  keep["slot"][:, :, bass.ds(2 * i, 2)].unsqueeze(3).to_broadcast([P, TILES, 2, CAP]),
                                  ALU.is_equal).then_inc(picked, 1)
                dve.wait_ge(picked, i + 1)
                for e in range(2):
                    n = 2 * i + e
                    dve.wait_ge(scat_turn, n + GIVEN)
                    dve.tensor_tensor(gated_pick[:, :, :, :], pick[:, :, e:e + 1, :].to_broadcast([P, TILES, 2, CAP]),
                                      keep["aff"][:, :, bass.ds(n, 1)].unsqueeze(3).to_broadcast([P, TILES, 2, CAP]),
                                      ALU.mult).then_inc(gate_picked, 1)
                    for j in range(2):
                        dve.wait_ge(silu_done, 2 * n + j + 1 + GIVEN)
                        dve.wait_ge(up_mm, 2 * n + j + 1)
                        dve.wait_ge(hid_turn, 2 * n + GIVEN)
                        dve.tensor_tensor(hid[:, j, :], silu[:, :], pU[:, :], ALU.mult).then_inc(hid_done, 1)
                    for u in range(2 * TILES):
                        t, h = u // 2, u % 2
                        dve.wait_ge(scat_mm, 2 * TILES * n + u + 1)
                        cols = res[:, t, HALF * h:HALF * h + HALF]
                        dve.tensor_tensor(cols, cols, pO[h][:, :], ALU.add).then_inc(scat_add, 1)

            with dve.Fori(0, PAIRS) as i:
                body(i)


def final_norm(nc, io, keep, out):
    res = keep["res"]
    with ExitStack() as ctx:
        row = ctx.enter_context(nc.sbuf_tensor("final_row", [P, D], F32))
        part = ctx.enter_context(nc.sbuf_tensor("final_part", [P, D], F32))
        stat = ctx.enter_context(nc.sbuf_tensor("final_stat", [P, 4, TILES], F32))
        row_load, squared, mean, rooted, inverse, done, stored = (
            ctx.enter_context(nc.semaphore(f"final_{n}")) for n in ("row", "squared", "mean", "rooted", "inverse", "done", "stored"))
        block = ctx.enter_context(nc.Block())
        out_t = out.rearrange("b (t p) d -> (b t) p d", p=P)

        @block.sync
        def _(sp):
            sp.dma_start(row[:, :], io["final_norm_g"].partition_broadcast(P)).then_inc(row_load, 16)
            for t in range(TILES):
                sp.wait_ge(done, t + 1)
                sp.dma_start(out_t[t], res[:, t, :]).then_inc(stored, 16)
            sp.wait_ge(stored, 16 * TILES)

        @block.scalar
        def _(act):
            for t in range(TILES):
                act.activation(part[:, :], res[:, t, :], ACT.Square, accum_out=stat[:, 0, t:t + 1]).then_inc(squared, 1)
                act.wait_ge(squared, t + 1)
            act.wait_ge(mean, 1)
            act.activation(stat[:, 2, :], stat[:, 1, :], ACT.Sqrt).then_inc(rooted, 1)

        @block.vector
        def _(dve):
            dve.wait_ge(squared, TILES)
            dve.tensor_scalar(stat[:, 1, :], stat[:, 0, :], 1.0 / D, EPS, ALU.mult, ALU.add).then_inc(mean, 1)
            dve.wait_ge(rooted, 1)
            dve.reciprocal(stat[:, 3, :], stat[:, 2, :]).then_inc(inverse, 1)
            dve.wait_ge(inverse, 1)
            dve.wait_ge(row_load, 16)
            for t in range(TILES):
                dve.scalar_tensor_tensor(out=res[:, t, :], in0=res[:, t, :], scalar=stat[:, 3, t:t + 1], in1=row[:, :],
                                         op0=ALU.mult, op1=ALU.mult).then_inc(done, 1)


_INS = ["x", "norm_ffn_g", "router_w", "exp_w_gate", "exp_w_up", "exp_w_down", "final_norm_g", "rw_w_in", "rw_w0", "rw_w1",
        "rw_w2", "rw_a1", "rw_a2", "rw_g1", "rw_g2", "rw_lnx_g", "rw_lnx_b", "rw_w_out"]


def kernel(**inputs):
    import concourse.bacc as bacc
    from concourse.bass_utils import run_bass_kernel_spmd

    nc = bacc.Bacc("TRN2", target_bir_lowering=False, num_devices=1)
    arrays, io = {}, {}

    def give(name, a):
        a = np.ascontiguousarray(a)
        arrays[f"in_{name}"] = a
        io[name] = nc.dram_tensor(f"in_{name}", a.shape, mybir.dt.from_np(a.dtype), kind="ExternalInput").ap()

    for name in _INS:
        give(name, inputs[name])
    rows = np.concatenate([np.asarray(inputs[n]).reshape(-1, D)
                           for n in ("norm_mix_g", "rw_mu", "rw_a0", "rw_k_k", "rw_k_a", "rw_r_k")], axis=0)
    give("vectors", rows.reshape(V_END, DC, P).transpose(2, 0, 1))
    give("consts", constants())
    out = nc.dram_tensor("out", (1, SEQ, D), F32, kind="ExternalOutput").ap()
    build_trunk(nc, io, out)
    r = run_bass_kernel_spmd(nc, [arrays], core_ids=[0])
    return r.results[0]["out"]
```

```python
from contextlib import ExitStack

import numpy as np

import concourse.bass as bass
from concourse import mybir

F32 = mybir.dt.float32
ALU = mybir.AluOpType
ACT = mybir.ActivationFunctionType
AX_X = mybir.AxisListType.X

P = 128
D = 1024
SEQ = 512
TILES = SEQ // P
DC = D // P
HEAD = 64
HEADS = D // HEAD
HALF = 512
LORA = 64
EXPERTS = 16
CAP = 2 * SEQ // EXPERTS
FF = 2048
EPS = 1e-6
LNX_EPS = 64e-5
DECAY = float(np.exp(-0.5))
BASE = 16
LEVELS = 2
GIVEN = 1
QUADS = HEADS // 4
R_, KK_, BZ_, KD_, SW_ = range(5)

C_ID, C_CUM, C_SCORE, C_LEVEL, C_EYE, C_TRI, C_ONES, C_HEAD, C_SEL, C_IOTA, C_END = np.cumsum(
    [0, P, 2 * (P + 1), 8 * P, LEVELS * P, BASE * BASE, P, P, P, 4, CAP]).tolist()
V_NORM, V_MU, V_A0, V_KK, V_KA, V_RK, V_END = np.cumsum([0, 1, 6, 2, 1, 1, 1]).tolist()


def constants():
    s, t = np.arange(P)[:, None], np.arange(P)[None, :]
    low = (s < P // 2) * 1.0
    edge = np.arange(P + 1)[None, :]
    cum = [(s < edge) - low, (s >= edge) - (1 - low)]
    score = []
    for strict, incl in ((s < t, s <= t), (s > t, s >= t)):
        score += [-1.0 * strict, 1.0 * incl, 1.0 * strict, 1.0 * incl]
    level = [(s // (2 * m) == t // (2 * m)) & (s // m != t // m) for m in (BASE << k for k in range(LEVELS))]
    eye = np.broadcast_to(np.eye(BASE).reshape(1, -1), (P, BASE * BASE))
    sel = (s // HEAD == np.arange(4)[None, :]) * 1.0
    iota = np.broadcast_to(1 + np.arange(CAP)[None, :], (P, CAP))
    parts = [s == t, *cum, *score, *level, eye, s <= t, np.ones((P, P)), s // HEAD == t // HEAD, sel, iota]
    return np.ascontiguousarray(np.concatenate([np.asarray(a, np.float32) for a in parts], axis=1))


class Chain:

    def __init__(self, eng, sem):
        self.eng, self.sem, self.n = eng, sem, 0

    def link(self, ins):
        ins.then_inc(self.sem, 1)
        self.n += 1
        self.eng.wait_ge(self.sem, self.n)


def wait_alone(eng, sem, value, tick):
    eng.wait_ge(sem, value)
    eng.sem_inc(tick, 1)


TILE_ORDER = (TILES - 1, *range(TILES - 1))


def add_bonus(pool, keep, t, v):
    v3 = v.rearrange("p (h v) -> p h v", v=HEAD)
    pool.tensor_tensor(v3, v3, keep["bonus"][:, TILE_ORDER[t], :].unsqueeze(2).to_broadcast([P, HEADS, HEAD]),
                       ALU.mult).then_inc(keep["bonus_step"], 1)
    pool.wait_ge(keep["bonus_step"], t + 1)
    pool.wait_ge(keep["lnx_load"], 32 * (1 if t == 0 else 2))
    pool.tensor_tensor(v, v, keep["lnx_b"], ALU.add).then_inc(keep["bonus_done"], 1)


def head_norm(dve, keep, t):
    chain, head_stat = keep["chain"], keep["head_stat"]
    y3 = keep["y"][:, TILE_ORDER[t], :].rearrange("p (h v) -> p h v", v=HEAD)

    def spread(i):
        return head_stat[:, i, :].unsqueeze(2).to_broadcast([P, HEADS, HEAD])

    chain.link(dve.tensor_reduce(head_stat[:, 0, :], y3, AX_X, ALU.add))
    chain.link(dve.tensor_scalar(head_stat[:, 1, :], head_stat[:, 0, :], 1.0 / HEAD, None, ALU.mult))
    dve.tensor_tensor(y3, y3, spread(1), ALU.subtract).then_inc(keep["centred"], 1)
    dve.wait_ge(keep["squared"], t + 1)
    chain.link(dve.tensor_reduce(head_stat[:, 0, :], keep["squares"].rearrange("p (h v) -> p h v", v=HEAD), AX_X, ALU.add))
    dve.tensor_scalar(head_stat[:, 2, :], head_stat[:, 0, :], 1.0 / HEAD, LNX_EPS, ALU.mult, ALU.add).then_inc(keep["spread_ready"], 1)
    dve.wait_ge(keep["head_root"], t + 1)
    chain.link(dve.reciprocal(head_stat[:, 1, :], head_stat[:, 3, :]))
    chain.link(dve.tensor_tensor(y3, y3, spread(1), ALU.mult))


def scale_and_add(dve, keep, t, v):
    chain, yt = keep["chain"], keep["y"][:, TILE_ORDER[t], :]
    dve.wait_ge(keep["lnx_load"], 32 * (1 if t == 0 else 2))
    chain.link(dve.tensor_tensor(yt, yt, keep["lnx_g"], ALU.mult))
    dve.wait_ge(keep["bonus_done"], t + 1)
    chain.link(dve.tensor_tensor(yt, yt, v, ALU.add))


def head_norm_roots(act, keep, t):
    act.wait_ge(keep["centred"], t + 1)
    act.activation(keep["squares"], keep["y"][:, TILE_ORDER[t], :], ACT.Square).then_inc(keep["squared"], 1)
    act.wait_ge(keep["spread_ready"], t + 1)
    act.activation(keep["head_stat"][:, 3, :], keep["head_stat"][:, 2, :], ACT.Sqrt).then_inc(keep["head_root"], 1)


def build_trunk(nc, io, out):
    scr = {
        name: nc.dram_tensor(f"scratch_{name}", shape, F32, kind="Internal").ap()
        for name, shape in {
            "r": [TILES, P, DC, P], "kk": [TILES, P, DC, P], "bz": [2, TILES, P, DC, P],
            "kd": [2, TILES, P, DC, P], "sw": [2, TILES, P, D], "v": [TILES, P, D],
            "blocks": [P // BASE, HEADS, BASE, BASE], "inverses": [2, P // BASE, HEADS, BASE, BASE],
        }.items()
    }
    with ExitStack() as ctx:
        keep = {
            "con": ctx.enter_context(nc.sbuf_tensor("con", [P, C_END], F32)),
            "vec": ctx.enter_context(nc.sbuf_tensor("vec", [P, V_END, DC], F32)),
            "gate_low": ctx.enter_context(nc.sbuf_tensor("gate_low", [P, SEQ], F32)),
            "bonus": ctx.enter_context(nc.sbuf_tensor("bonus", [P, TILES, HEADS], F32)),
            "lent": ctx.enter_context(nc.sbuf_tensor("lent_slot", [P, DC, D], F32)),
            "w_out_load": ctx.enter_context(nc.semaphore("w_out_load")),
            "decays_in": ctx.enter_context(nc.semaphore("decays_in")),
            "sp_tick": ctx.enter_context(nc.semaphore("sp_tick")),
            "g2": ctx.enter_context(nc.sbuf_tensor("g2", [P, D], F32)),
            "g2_load": ctx.enter_context(nc.semaphore("g2_load")),
            "head_stat": ctx.enter_context(nc.sbuf_tensor("head_stat", [P, 4, HEADS], F32)),
            **{name: ctx.enter_context(nc.semaphore(name)) for name in ("centred", "squared", "spread_ready", "head_root", "bonus_step", "bonus_done", "lnx_load")},
            "chain": Chain(nc.vector, ctx.enter_context(nc.semaphore("dve_chain"))),
        }
        with nc.sbuf_tensor("y", [P, TILES, D], F32) as y:
            keep["y"] = y
            mix_inputs(nc, io, scr, keep)
            recurrence(nc, io, scr, keep)
            with ExitStack() as moe:
                for name, shape in (("res", [P, TILES, D]), ("slot", [P, TILES, EXPERTS]), ("aff", [P, TILES, EXPERTS])):
                    keep[name] = moe.enter_context(nc.sbuf_tensor(name, shape, F32))
                ring = [moe.enter_context(nc.sbuf_tensor(f"ring{k}", [P, DC, D], F32)) for k in range(RING - 1)]
                keep["ring"] = [*ring[:2], keep["lent"], ring[2]]
                keep["landed"] = [[moe.enter_context(nc.semaphore(f"weights_landed{k}_{half}")) for half in range(2)] for k in range(RING)]
                mix_output(nc, io, scr, keep)
                experts(nc, io, keep, out)


def mix_inputs(nc, io, scr, keep):
    con, vec = keep["con"], keep["vec"]
    ident = con[:, C_ID:C_ID + P]
    with ExitStack() as ctx:
        def sb(name, *shape):
            return ctx.enter_context(nc.sbuf_tensor(name, list(shape), F32))

        def sem(name):
            return ctx.enter_context(nc.semaphore(name))

        x_in = sb("x_in", P, TILES, D)
        hT = sb("hT", P, DC, SEQ + 2)
        shift = sb("shift", P, DC, SEQ)
        xm = [sb("xm0", P, DC, SEQ)[:, :, :], keep["y"][:, :, :].rearrange("p t d -> p (t d)").rearrange("p (c s) -> p c s", s=SEQ)]
        w_ring = keep["lent"][:, :, :].rearrange("p k d -> p (k d)").rearrange("p (q m c e) -> p q m c e", q=2, m=2, e=256)
        low_w = sb("low_w", P, 3, DC, P)
        up_w = sb("up_w", P, 2, D)
        w0_row = sb("w0_row", P, 2, D)
        tw, xa = sb("tw", P, 2, SEQ), sb("xa", P, 2, SEQ)
        tok = sb("tok", P, 2, D)
        kT, rT = sb("kT", P, SEQ), sb("rT", P, SEQ)
        sq, rn, kk = sb("sq", P, SEQ), sb("rn", P, SEQ), sb("kk", P, SEQ)
        aT, kd, bz = sb("aT", P, 2, SEQ), sb("kd", P, 2, SEQ), sb("bz", P, 2, SEQ)
        ts, rk = sb("ts", P, SEQ), sb("rk", P, SEQ)
        stat = sb("stat", P, 3, TILES)
        ps = [ctx.enter_context(nc.psum_tensor(f"mi_ps{i}", [P, HALF], F32)) for i in range(8)]

        x_load = [sem(f"x_load{t}") for t in range(TILES)]
        ident_load, con_load, row_load = sem("ident_load"), sem("con_load"), sem("row_load")
        low_load, up_load = sem("low_load"), sem("up_load")
        sq_done, root_done, h_done = sem("sq_done"), sem("root_done"), sem("h_done")
        turned, hT_done, xm_done = sem("turned"), sem("hT_done"), sem("xm_done")
        low_mm, low_ev = sem("low_mm"), sem("low_ev")
        sw_mm, sw_sum, sw_done = sem("sw_mm"), sem("sw_sum"), sem("sw_done")
        sw_out = [sem(f"sw_out{i}") for i in range(2)]
        w_load = [sem(f"w_load{i}") for i in range(2)]
        proj_mm, kr_ev, sq_ev = sem("proj_mm"), sem("kr_ev"), sem("sq_ev")
        norm_mm, norm_max, norm_root, kk_done = sem("norm_mm"), sem("norm_max"), sem("norm_root"), sem("kk_done")
        a_mm, a_ev, keys_done, rk_done = sem("a_mm"), sem("a_ev"), sem("keys_done"), sem("rk_done")
        bonus_mm, bonus_ev, chunk_out = sem("bonus_mm"), sem("bonus_ev"), sem("chunk_out")
        low_zero, neighbours = sem("low_zero"), sem("neighbours")
        wv_load, v_scaled, v_mixed, v_mm, v_ev, v_out = (sem(f"first_{n}") for n in ("wv_load", "v_scaled", "v_mixed", "v_mm", "v_ev", "v_out"))

        x_t = io["x"].rearrange("b (t p) d -> (b t) p d", p=P)
        w_in = io["rw_w_in"].rearrange("a m (c p) e -> (a m) p c e", p=P)
        MIXES = (3, 4, 5, 1, 0)
        w_v = w_ring[:, 0].rearrange("p m c e -> p (m c e)").rearrange("p (c e) -> p c e", e=HALF)

        def scaled(k):
            return x_in[:, :, :].rearrange("p t d -> p (t d)")[:, SEQ * k:SEQ * k + SEQ]

        def bonus_products(pe, c):
            pe.wait_ge(rk_done, c + 1)
            if c:
                pe.wait_ge(bonus_ev, c)
            for t in range(TILES):
                last = pe.matmul(ps[7][:, 4 * t:4 * t + 4], rk[:, P * t:P * t + P], con[:, C_SEL:C_SEL + 4], start=True, stop=True)
            last.then_inc(bonus_mm, 1)

        def bonus_copy(dve, c):
            dve.wait_ge(bonus_mm, c + 1)
            dve.tensor_copy(keep["bonus"][:, :, 2 * c:2 * c + 2],
                            ps[7][:, 0:4 * TILES].rearrange("p (t h) -> p t h", h=4)[:, :, 0:2]).then_inc(bonus_ev, 1)

        block = ctx.enter_context(nc.Block())

        @block.sync
        def _(sp):
            for t in range(TILES):
                sp.dma_start(x_in[:, t, :], x_t[t]).then_inc(x_load[t], 16)
            for i, name in enumerate(("rw_w1", "rw_a1")):
                for z in range(2):
                    sp.dma_start(low_w[:, i, :, LORA * z:LORA * z + LORA],
                                 io[name][0, z].rearrange("(c p) r -> p c r", p=P)).then_inc(low_load, 16)
            sp.dma_start(low_w[:, 2], io["rw_g1"][0].rearrange("(c p) r -> p c r", p=P)).then_inc(low_load, 16)
            for q in range(4):
                if q >= 2:
                    sp.wait_ge(proj_mm, 4 * (q - 1))
                for m, which in enumerate((1, 0)):
                    sp.dma_start(w_ring[:, q % 2, m], w_in[which][:, :, 256 * q:256 * q + 256]).then_inc(w_load[q % 2], 16)
            sp.wait_ge(proj_mm, 4 * 3)
            sp.dma_start(w_v, w_in[2][:, :, 0:HALF]).then_inc(wv_load, 16)
            sp.wait_ge(proj_mm, 2 * DC)
            sp.wait_ge(sw_out[0], 16 * TILES)
            sp.dma_start(keep["lent"][:, SW_, :], scr["sw"][0, 0]).then_inc(keep["decays_in"], 16)
            for t in range(2):
                sp.wait_ge(v_ev, t + 1)
                sp.dma_start(scr["v"][t][:, 0:HALF], tok[:, t, 0:HALF]).then_inc(v_out, 16)
            for k in range(2):
                sp.wait_ge(sw_out[k], 16 * TILES)
            sp.wait_ge(chunk_out, 16 * 6 * DC)
            sp.wait_ge(v_out, 32)

        @block.gpsimd
        def _(pool):
            pool.dma_start(con[:, C_ID:C_ID + P], io["consts"][:, C_ID:C_ID + P]).then_inc(ident_load, 16)
            pool.dma_start(vec[:, :, :], io["vectors"]).then_inc(ident_load, 16)
            pool.wait_ge(x_load[TILES - 1], 16)
            pool.wait_ge(turned, 2)
            pool.dma_start(con[:, C_ID + P:C_END], io["consts"][:, C_ID + P:C_END]).then_inc(con_load, 16)
            for i, name in enumerate(("rw_w2", "rw_a2")):
                pool.dma_start(up_w[:, i, :], io[name].rearrange("a z r d -> (a z r) d")).then_inc(up_load, 16)
            for z in range(2):
                pool.dma_start(w0_row[:, z, :], io["rw_w0"][0, z].partition_broadcast(P)).then_inc(row_load, 16)
            pool.wait_ge(sq_done, TILES)
            pool.wait_ge(hT_done, 2 * TILES)
            for c in range(DC):
                pool.tensor_tensor(shift[:, c, :], hT[:, c, 0:SEQ], hT[:, c, 2:SEQ + 2], ALU.add).then_inc(neighbours, 1)
            for k in range(DC):
                pool.wait_ge(xm_done, k + 1)
                pool.tensor_tensor(scaled(k), shift[:, k, :], vec[:, V_MU + 2, k:k + 1].to_broadcast([P, SEQ]), ALU.mult).then_inc(v_scaled, 1)
            for c in range(DC):
                pool.wait_ge(sw_done, c + 1)
                pool.dma_start(scr["sw"][c // TILES, c % TILES], tok[:, c % 2, :]).then_inc(sw_out[c % 2], 16)
                def spill(name, z, src):
                    dst = scr[name] if z is None else scr[name][z]
                    pool.dma_start(dst[:, :, c, :].rearrange("t p s -> p t s"),
                                   src.rearrange("p (t s) -> p t s", s=P)).then_inc(chunk_out, 16)
                if c == DC - 1:
                    pool.wait_ge(proj_mm, 2 * DC - 1)
                    pool.wait_ge(v_scaled, DC)
                    for k in range(DC):
                        pool.tensor_tensor(xm[1][:, k, :], scaled(k), hT[:, k, 1:SEQ + 1], ALU.add).then_inc(v_mixed, 1)
                pool.wait_ge(kr_ev, 2 * c + 2)
                spill("r", None, rT[:, :])
                pool.wait_ge(kk_done, c + 1)
                spill("kk", None, kk[:, :])
                pool.wait_ge(keys_done, c + 1)
                for z in range(2):
                    spill("bz", z, bz[:, z, :])
                    spill("kd", z, kd[:, z, :])

        @block.scalar
        def _(act):
            for t in range(TILES):
                act.wait_ge(x_load[t], 16)
                act.activation(shift[:, 2 * t:2 * t + 2, :].rearrange("p a b -> p (a b)"), x_in[:, t, :], ACT.Square,
                               accum_out=stat[:, 0, t:t + 1]).then_inc(sq_done, 1)
                act.wait_ge(norm_max, t + 1)
                act.activation(stat[:, 1, t:t + 1], stat[:, 2, t:t + 1], ACT.Sqrt).then_inc(root_done, 1)
            act.wait_ge(low_zero, 1)
            for i, (dst, fn) in enumerate(((tw, ACT.Tanh), (xa, ACT.Copy))):
                act.wait_ge(low_mm, i + 1)
                for z in range(2):
                    rows = slice(LORA * z, LORA * z + LORA)
                    last = act.activation(dst[rows, z, :], ps[i % 2][rows, :], fn)
                last.then_inc(low_ev, 1)
            act.wait_ge(low_mm, 3)
            act.activation(keep["gate_low"][:, :], ps[0][:, :], ACT.Sigmoid).then_inc(low_ev, 1)
            for c in range(DC):
                act.wait_ge(sw_sum, 2 * c + 2)
                act.activation(tok[:, c % 2, :], tok[:, c % 2, :], ACT.Sigmoid).then_inc(sw_done, 1)
                act.wait_ge(proj_mm, 2 * c + 1)
                if c:
                    act.wait_ge(keys_done, c)
                act.activation(kT[:, :], ps[2][:, :], ACT.Copy).then_inc(kr_ev, 1)
                act.activation(sq[:, :], ps[2][:, :], ACT.Square, scale=vec[:, V_KK, c:c + 1]).then_inc(sq_ev, 1)
                for z in range(2):
                    act.wait_ge(a_mm, 2 * c + z + 1)
                    act.activation(aT[:, z, :], ps[4 + z][:, :], ACT.Sigmoid,
                                   bias=vec[:, V_A0 + z, c:c + 1]).then_inc(a_ev, 1)
                act.wait_ge(norm_max, TILES + c + 1)
                act.activation(rn[:, :], sq[:, :], ACT.Sqrt).then_inc(norm_root, 1)
                act.wait_ge(proj_mm, 2 * c + 2)
                if c:
                    act.wait_ge(chunk_out, 16 * 6 * c)
                    act.wait_ge(rk_done, c)
                act.activation(rT[:, :], ps[3][:, :], ACT.Copy).then_inc(kr_ev, 1)
            for k in range(2):
                act.wait_ge(sw_out[k], 16 * TILES)
            for t in range(2):
                act.wait_ge(v_mm, t + 1)
                act.activation(tok[:, t, 0:HALF], ps[t][:, :], ACT.Copy).then_inc(v_ev, 1)

        @block.tensor
        def _(pe):
            pe.wait_ge(ident_load, 32)
            for t in range(TILES):
                pe.wait_ge(h_done, t + 1)
                for g in range(2):
                    for c in range(4):
                        last = pe.transpose(ps[2 * t + g][:, P * c:P * c + P], x_in[:, t, P * (4 * g + c):P * (4 * g + c + 1)], ident)
                    last.then_inc(turned, 1)
            pe.wait_ge(low_load, 16 * 5)
            pe.wait_ge(hT_done, 2 * TILES)
            for i in range(3):
                if i == 2:
                    pe.wait_ge(low_ev, 1)
                for c in range(DC):
                    pe.wait_ge(xm_done, DC * i + c + 1)
                    last = pe.matmul(ps[i % 2][:, :], low_w[:, i, c, :], xm[i % 2][:, c, :], start=c == 0, stop=c == DC - 1)
                last.then_inc(low_mm, 1)
            for c in range(DC):
                q = c // 2
                z, t = c // TILES, c % TILES
                if c == 0:
                    pe.wait_ge(up_load, 32)
                for h in range(2):
                    pe.wait_ge(low_ev, 3)
                    if c:
                        pe.wait_ge(sw_sum, 2 * c + h - 1)
                    pe.matmul(ps[h][:, :], tw[:, z, P * t:P * t + P], up_w[:, 0, HALF * h:HALF * h + HALF],
                              start=True, stop=True).then_inc(sw_mm, 1)
                pe.wait_ge(w_load[q % 2], 32 * (q // 2 + 1))
                for m in range(2):
                    if c:
                        pe.wait_ge(kr_ev, 2 * (c - 1) + m + 1)
                        pe.wait_ge(sq_ev, c)
                    for k in range(DC):
                        if c == 0:
                            pe.wait_ge(xm_done, DC * (3 + m) + k + 1)
                        last = pe.matmul(ps[2 + m][:, :], w_ring[:, q % 2, m, k, P * (c % 2):P * (c % 2) + P],
                                         xm[(3 + m) % 2][:, k, :], start=k == 0, stop=k == DC - 1)
                    last.then_inc(proj_mm, 1)
                    if m == 0:
                        if c == 0:
                            pe.wait_ge(con_load, 16)
                        for z in range(2):
                            if c:
                                pe.wait_ge(a_ev, 2 * (c - 1) + z + 1)
                            pe.matmul(ps[4 + z][:, :], up_w[:, 1, P * c:P * c + P], xa[:, z, :], start=True, stop=True).then_inc(a_mm, 1)
                        pe.wait_ge(sq_ev, c + 1)
                        if c:
                            pe.wait_ge(norm_max, TILES + c)
                        pe.matmul(ps[6][:, :], con[:, C_HEAD:C_HEAD + P], sq[:, :], start=True, stop=True).then_inc(norm_mm, 1)
                if c:
                    bonus_products(pe, c - 1)
            pe.wait_ge(wv_load, 16)
            for t in range(2):
                for k in range(DC):
                    pe.wait_ge(v_mixed, k + 1)
                    last = pe.matmul(ps[t][:, :], xm[1][:, k, P * t:P * t + P], w_v[:, k, :], start=k == 0, stop=k == DC - 1)
                last.then_inc(v_mm, 1)
            bonus_products(pe, DC - 1)

        @block.vector
        def _(dve):
            chain = keep["chain"]
            dve.memset(hT[:, :, 0:1], 0.0)
            dve.memset(hT[:, :, SEQ + 1:SEQ + 2], 0.0)
            for z in range(2):
                other = slice(LORA * (1 - z), LORA * (1 - z) + LORA)
                dve.memset(tw[other, z, :], 0.0)
                last = dve.memset(xa[other, z, :], 0.0)
            last.then_inc(low_zero, 1)
            for t in range(TILES):
                dve.wait_ge(sq_done, t + 1)
                dve.tensor_scalar(stat[:, 2, t:t + 1], stat[:, 0, t:t + 1], 1.0 / D, EPS, ALU.mult, ALU.add).then_inc(norm_max, 1)
                dve.wait_ge(root_done, t + 1)
                chain.link(dve.reciprocal(stat[:, 1, t:t + 1], stat[:, 1, t:t + 1]))
                dve.tensor_scalar(x_in[:, t, :], x_in[:, t, :], stat[:, 1, t:t + 1], None, ALU.mult).then_inc(h_done, 1)
            dve.wait_ge(ident_load, 32)
            for t in range(TILES):
                for g in range(2):
                    dve.wait_ge(turned, 2 * t + g + 1)
                    dve.tensor_tensor(hT[:, 4 * g:4 * g + 4, 1 + P * t:1 + P * t + P], ps[2 * t + g][:, :].rearrange("p (c s) -> p c s", s=P),
                                      vec[:, V_NORM, 4 * g:4 * g + 4].unsqueeze(2).to_broadcast([P, 4, P]), ALU.mult).then_inc(hT_done, 1)
            dve.wait_ge(hT_done, 2 * TILES)

            def mix(i, c):
                dve.scalar_tensor_tensor(out=xm[i % 2][:, c, :], in0=shift[:, c, :], scalar=vec[:, V_MU + MIXES[i], c:c + 1],
                                         in1=hT[:, c, 1:SEQ + 1], op0=ALU.mult, op1=ALU.add).then_inc(xm_done, 1)

            for c in range(DC):
                dve.wait_ge(neighbours, c + 1)
                chain.link(dve.scalar_tensor_tensor(out=shift[:, c, :], in0=shift[:, c, :], scalar=0.5, in1=hT[:, c, 1:SEQ + 1],
                                                    op0=ALU.mult, op1=ALU.subtract))
                mix(0, c)
            for i in range(1, len(MIXES)):
                if i >= 2:
                    dve.wait_ge(low_mm, i - 1)
                for c in range(DC):
                    mix(i, c)
            dve.wait_ge(row_load, 32)
            for c in range(DC):
                for h in range(2):
                    dve.wait_ge(sw_mm, 2 * c + h + 1)
                    if c >= 2:
                        dve.wait_ge(sw_out[c % 2], 16 * (c // 2))
                    cols = slice(HALF * h, HALF * h + HALF)
                    dve.tensor_tensor(tok[:, c % 2, cols], ps[h][:, :], w0_row[:, c // TILES, cols], ALU.add).then_inc(sw_sum, 1)
                dve.wait_ge(norm_mm, c + 1)
                dve.tensor_scalar(sq[:, :], ps[6][:, :], 1e-24, None, ALU.max).then_inc(norm_max, 1)
                dve.wait_ge(norm_root, c + 1)
                chain.link(dve.reciprocal(rn[:, :], rn[:, :]))
                if c:
                    dve.wait_ge(chunk_out, 16 * 6 * c)
                dve.scalar_tensor_tensor(out=kk[:, :], in0=kT[:, :], scalar=vec[:, V_KK, c:c + 1], in1=rn[:, :],
                                         op0=ALU.mult, op1=ALU.mult).then_inc(kk_done, 1)
                dve.wait_ge(kk_done, c + 1)
                for z in range(2):
                    dve.wait_ge(a_ev, 2 * c + z + 1)
                    chain.link(dve.tensor_scalar(ts[:, :], aT[:, z, :], -1.0, vec[:, V_KA, c:c + 1], ALU.add, ALU.mult))
                    chain.link(dve.scalar_tensor_tensor(out=kd[:, z, :], in0=ts[:, :], scalar=1.0, in1=kT[:, :],
                                                        op0=ALU.add, op1=ALU.mult))
                    last = dve.tensor_tensor(bz[:, z, :], kk[:, :], aT[:, z, :], ALU.mult)
                last.then_inc(keys_done, 1)
                chain.link(dve.tensor_tensor(ts[:, :], kd[:, 0, :], kd[:, 1, :], ALU.add))
                dve.wait_ge(kr_ev, 2 * c + 2)
                if c:
                    dve.wait_ge(bonus_mm, c)
                dve.scalar_tensor_tensor(out=rk[:, :], in0=rT[:, :], scalar=vec[:, V_RK, c:c + 1], in1=ts[:, :],
                                         op0=ALU.mult, op1=ALU.mult).then_inc(rk_done, 1)
                if c:
                    bonus_copy(dve, c - 1)
            bonus_copy(dve, DC - 1)


def recurrence(nc, io, scr, keep):
    con, y = keep["con"], keep["y"]
    with ExitStack() as ctx:
        def sb(name, *shape):
            return ctx.enter_context(nc.sbuf_tensor(name, list(shape), F32))

        def sem(name):
            return ctx.enter_context(nc.semaphore(name))

        lent = keep["lent"][:, :, :].rearrange("p k d -> p (k d)")
        IN = lent[:, 0:5 * D].rearrange("p (s d) -> p s d", d=D)
        grow = lent[:, 5 * D:6 * D].rearrange("p (c s) -> p c s", s=P)
        QR = [lent[:, 6 * D:8 * D].rearrange("p (c e s) -> p c e s", e=2, s=P), sb("QR1", P, DC, 2, P)]
        V = [sb(f"V{b}", P, D) for b in range(2)]
        decay = sb("decay", P, DC, P + 1)
        B = [sb(f"B{e}", P, DC, P) for e in range(2)]
        KH = [sb(f"KH{e}", P, DC, P) for e in range(2)]
        QB = [sb(f"QB{b}", P, HEADS, P) for b in range(2)]
        AM = sb("AM", P, HEADS, 3, P)
        X, XT, W = (sb(n, P, HEADS, P) for n in ("X", "XT", "W"))
        TK = sb("TK", P, DC, 2, 2, HEAD)
        RN, UN = sb("RN", P, 2, HALF), sb("UN", P, 2, HALF)
        UH = [sb(f"UH{b}", P, 2, HALF) for b in range(2)]
        carry = [sb(f"carry{b}", P, DC, HEAD) for b in range(2)]
        state = sb("state", P, DC, 2, HEAD)
        p_mid = [sb(f"p_mid{b}", P, DC) for b in range(2)]
        p_end = [sb(f"p_end{b}", P, DC) for b in range(2)]
        NB, XB, step_sum = sb("NB", P, BASE, BASE), sb("XB", P, 2, BASE, BASE), sb("step_sum", P, BASE, BASE)
        WITH, BEFORE = (slice(1, P + 1), slice(0, P)), (slice(0, P), slice(1, P + 1))
        pS = [ctx.enter_context(nc.psum_tensor(f"pS{i}", [P, HALF], F32)) for i in range(2)]
        pI = [ctx.enter_context(nc.psum_tensor(f"pI{i}", [P, HALF], F32)) for i in range(QUADS)]
        pT = [ctx.enter_context(nc.psum_tensor(f"pT{i}", [P, HALF], F32)) for i in range(2)]
        am_flat = AM[:, :, :, :].rearrange("p h e s -> p (h e s)")
        w_v = [am_flat[:, 0:8 * HALF].rearrange("p (c e) -> p c e", e=HALF),
               am_flat[:, 8 * HALF:12 * HALF].rearrange("p (c e) -> p c e", e=HALF),
               X[:, :, :].rearrange("p h s -> p (h s)").rearrange("p (c e) -> p c e", e=HALF)]

        decays_in, streams_in = keep["decays_in"], sem("streams_in")
        v_in = [sem(f"v_in{b}") for b in range(2)]
        wv_load = [sem(f"wv_load{h}") for h in range(2)]
        v_mm, v_ev = sem("v_mm"), sem("v_ev")
        v_out = [sem(f"v_out{b}") for b in range(2)]
        cleared, y_cleared, x_cleared = sem("cleared"), sem("y_cleared"), sem("x_cleared")
        cum_mm, exp_done = sem("cum_mm"), sem("exp_done")
        prep_dve, prep_b, prep_pool = sem("prep_dve"), sem("prep_b"), sem("prep_pool")
        qb_mm, qb_ev, score_mm, score_ev = sem("qb_mm"), sem("qb_ev"), sem("score_mm"), sem("score_ev")
        blocks_out, blocks_in, base_step, base_done, base_out, base_in = (
            sem(n) for n in ("blocks_out", "blocks_in", "base_step", "base_done", "base_out", "base_in"))
        inv_mm = [sem(f"inv_mm{q}") for q in range(QUADS)]
        inv_ev = [sem(f"inv_ev{q}") for q in range(QUADS)]
        pt_full = [sem(f"pt_full{k}") for k in range(2)]
        pt_free = [sem(f"pt_free{k}") for k in range(2)]
        state_ready, carried = sem("state_ready"), sem("carried")
        sp_tick, dve_tick, pe_tick, pool_tick = keep["sp_tick"], sem("dve_tick"), sem("pe_tick"), sem("pool_tick")
        TURN, R_SUM, U_FIRST, U_CROSS, U_ALL, Y_SUM, S_SUM, USES = 1, 3, 4, 5, 6, 7, 8, 8
        STEPS = 3 * LEVELS - 1
        STREAM_SUM = 16 * 4
        V_PIECES = [(0, 1), (1, 1), (2, 1), (3, 1), (2, 0), (3, 0)]
        V_SECOND = 4

        keep["squares"] = QB[0][:, 0:DC, :].rearrange("p h s -> p (h s)")
        keep["lnx_g"] = decay[:, :, :].rearrange("p c s -> p (c s)")[:, 0:D]
        keep["lnx_b"] = UH[0][:, :, :].rearrange("p h s -> p (h s)")

        def chunk(i, b):
            return (TILES - 1) - i if b else i

        def used(n, b, last, step):
            return USES * n + (step - (2 if step >= R_SUM - 1 else 0) - (3 if b else 0) if last else step) + GIVEN

        def rolled(eng, body):
            with eng.Fori(0, TILES - 1) as i:
                for b in range(2):
                    body(i, b, False)
            for b in range(2):
                body(TILES - 1, b, True)

        block = ctx.enter_context(nc.Block())

        @block.sync
        def _(sp):
            def load_decays(i, b):
                sp.dma_start(IN[:, SW_, :], scr["sw"][b, chunk(i, b)]).then_inc(decays_in, 16)

            def load_streams(i, b):
                c = chunk(i, b)
                for s, src in ((R_, scr["r"][c]), (KK_, scr["kk"][c]), (BZ_, scr["bz"][b, c]),
                               (KD_, scr["kd"][b, c])):
                    if len(src.shape) == 3:
                        src = src.rearrange("p c s -> p (c s)")
                    sp.dma_start(IN[:, s, :], src).then_inc(streams_in, 16)

            def base_blocks(n, b):
                sp.wait_ge(qb_ev, QUADS * (n + 1))
                for k in range(P // BASE):
                    rows = slice(BASE * k, BASE * k + BASE)
                    sp.dma_start(scr["blocks"][k].rearrange("h s t -> s h t"), QB[b][rows, :, rows]).then_inc(blocks_out, 16)
                sp.wait_ge(blocks_out, P * (n + 1))
                sp.dma_start(NB[:, :, :].rearrange("p s t -> p (s t)"),
                             scr["blocks"].rearrange("k h s t -> (k h) (s t)")).then_inc(blocks_in, 16)
                sp.wait_ge(base_done, n + 1)
                sp.dma_start(scr["inverses"].rearrange("a k h s t -> (k h) a (s t)"),
                             XB[:, :, :, :].rearrange("p a s t -> p a (s t)")).then_inc(base_out, 16)
                wait_alone(sp, base_out, 16 * (n + 1) + GIVEN, sp_tick)
                wait_alone(sp, x_cleared, 2 * (n + 1), sp_tick)
                for k in range(P // BASE):
                    rows = slice(BASE * k, BASE * k + BASE)
                    for a, dst in enumerate((XT, X)):
                        sp.dma_start(dst[rows, :, rows], scr["inverses"][a, k].rearrange("h s t -> s h t")).then_inc(base_in, 16)

            def load_w_v(k, half, part):
                sp.dma_start(w_v[k], io["rw_w_in"][0, 2].rearrange("(c p) e -> p c e", p=P)[:, part, HALF * half:HALF * half + HALF])\
                  .then_inc(wv_load[half], 16)

            load_w_v(1, 1, slice(0, 4))
            load_w_v(2, 1, slice(4, 8))
            load_streams(0, 0)
            load_w_v(0, 0, slice(0, 8))
            sp.wait_ge(prep_dve, 1)
            sp.wait_ge(prep_pool, 1)
            load_decays(0, 1)
            load_streams(0, 1)
            for t in range(2):
                sp.wait_ge(v_ev, t + 1)
                sp.dma_start(scr["v"][t][:, HALF:D], V[t % 2][:, HALF:D]).then_inc(v_out[t % 2], 16)
            base_blocks(0, 0)
            for t in range(2, TILES):
                sp.wait_ge(v_ev, V_SECOND + t - 1)
                sp.dma_start(scr["v"][t], V[t % 2][:, :]).then_inc(v_out[t % 2], 16)
            for t in range(2):
                sp.wait_ge(v_out[t], 16 * TILES // 2)
            sp.dma_start(V[0][:, :], scr["v"][0]).then_inc(v_in[0], 16)

            def body(i, b, last):
                n = 2 * i + b
                if last and b == 1:
                    for k in range(2):
                        sp.wait_ge(pt_full[k], used(n, b, last, 0))
                    for name in ("lnx_g", "lnx_b"):
                        sp.dma_start(keep[name], io[f"rw_{name}"][0].partition_broadcast(P)).then_inc(keep["lnx_load"], 16)
                    sp.dma_start(keep["g2"][:, :], io["rw_g2"][0]).then_inc(keep["g2_load"], 16)
                    sp.dma_start(keep["lent"][:, :, :], io["rw_w_out"][0].rearrange("(c p) e -> p c e", p=P)).then_inc(keep["w_out_load"], 16)
                    return
                wait_alone(sp, pt_full[1], used(n, b, last, 0), sp_tick)
                sp.dma_start(V[1 - b][:, :], scr["v"][chunk(i + b, 1 - b)]).then_inc(v_in[1 - b], 16)
                if not last:
                    sp.wait_ge(prep_dve, n + 2)
                    wait_alone(sp, prep_pool, n + 2, sp_tick)
                    load_decays(i + 1, b)
                    load_streams(i + 1, b)
                base_blocks(n + 1, 1 - b)

            rolled(sp, body)

        @block.gpsimd
        def _(pool):
            zeroed = Chain(pool, cleared)
            for e in range(2):
                zero = slice(HEAD * (1 - e), HEAD * (1 - e) + HEAD)
                zeroed.link(pool.memset(B[e][zero, :, :], 0.0))
                zeroed.link(pool.memset(KH[e][zero, :, :], 0.0))
            for b in range(2):
                zeroed.link(pool.memset(carry[b][:, :, :], 0.0))
                zeroed.link(pool.memset(UH[b][:, :, :], 0.0))
            zeroed.link(pool.memset(state[:, :, :, :], 0.0))
            pool.memset(XT[:, :, :], 0.0).then_inc(x_cleared, 1)
            pool.wait_ge(x_cleared, 1)

            def prep(n, b):
                pool.wait_ge(exp_done, 4 * n + 4)
                pool.wait_ge(streams_in, STREAM_SUM * (n + 1))
                for dst, s in ((B, BZ_), (KH, KD_)):
                    for e in range(2):
                        rows = slice(HEAD * e, HEAD * e + HEAD)
                        last = pool.tensor_tensor(dst[e][rows, :, :], IN[rows, s, :].rearrange("p (c s) -> p c s", s=P),
                                                  grow[rows, :, :], ALU.mult)
                    last.then_inc(prep_b if dst is B else prep_pool, 1)
                wait_alone(pool, prep_pool, n + 1, pool_tick)

            def base(n, b):
                per = 2 * BASE
                done = 0

                def link(ins, alone=False):
                    nonlocal done
                    done += 1
                    ins.then_inc(base_step, 1)
                    if alone:
                        wait_alone(pool, base_step, per * n + done, pool_tick)
                    else:
                        pool.wait_ge(base_step, per * n + done)

                pool.wait_ge(blocks_in, 16 * (n + 1))
                wait_alone(pool, base_out, 16 * n + GIVEN, pool_tick)
                link(pool.tensor_copy(XB[:, 0].rearrange("p s t -> p (s t)"), con[:, C_EYE:C_EYE + BASE * BASE]))
                for k in range(BASE - 1):
                    r = k if b else BASE - 1 - k
                    rows, cols = (slice(r + 1, BASE), slice(0, r + 1)) if b else (slice(0, r), slice(r, BASE))
                    h, w = BASE - 1 - k, k + 1
                    link(pool.tensor_tensor(step_sum[:, 0:h, 0:w], NB[:, rows, r:r + 1].to_broadcast([P, h, w]),
                                            XB[:, 0, r:r + 1, cols].to_broadcast([P, h, w]), ALU.mult))
                    into = XB[:, 0, rows, cols]
                    link(pool.tensor_tensor(into, into, step_sum[:, 0:h, 0:w], ALU.add), alone=k == BASE - 2)
                link(pool.tensor_copy(XB[:, 1], XB[:, 0].rearrange("p s t -> p t s")))
                pool.sem_inc(base_done, 1)

            prep(0, 0)
            base(0, 0)
            pool.wait_ge(v_mm, V_SECOND)
            pool.memset(X[:, :, :], 0.0).then_inc(x_cleared, 1)
            pool.wait_ge(v_mm, len(V_PIECES))
            pool.memset(y[:, :, :], 0.0).then_inc(y_cleared, 1)
            pool.wait_ge(y_cleared, 1)
            pool.wait_ge(x_cleared, 2)

            def body(i, b, last):
                n = 2 * i + b
                if last and b == 1:
                    for k in range(2):
                        pool.wait_ge(pt_full[k], used(n, b, last, 0))
                    add_bonus(pool, keep, 0, V[0][:, :])
                    return
                if last:
                    pool.wait_ge(score_mm, HEADS * (n + 1))
                else:
                    for k in range(2):
                        pool.wait_ge(pt_full[k], used(n, b, last, TURN + 1))
                prep(n + 1, 1 - b)
                for k in range(2):
                    wait_alone(pool, pt_full[k], used(n, b, last, U_ALL), pool_tick)
                pool.memset(XT[:, :, :], 0.0).then_inc(x_cleared, 1)
                pool.memset(X[:, :, :], 0.0).then_inc(x_cleared, 1)
                wait_alone(pool, x_cleared, 2 * (n + 2), pool_tick)
                base(n + 1, 1 - b)

            rolled(pool, body)

        @block.scalar
        def _(act):
            def decays(n, b, quarters=range(4), first_batch=False):
                first = P if b else 0
                for u in quarters:
                    act.wait_ge(cum_mm, 4 * n + u + 1)
                    if u == 0 and not first_batch:
                        act.wait_ge(prep_dve, n)
                        act.wait_ge(prep_pool, n)
                    two = pS[u % 2][:, 0:2 * (P + 1)].rearrange("p (c s) -> p c s", s=P + 1)
                    cs = slice(2 * u, 2 * u + 2)
                    act.activation(decay[:, cs, :], two, ACT.Exp, scale=-DECAY)
                    act.activation(grow[:, cs, :], two[:, :, WITH[b]], ACT.Exp, scale=DECAY)
                    act.activation(p_mid[b][:, cs], two[:, :, first], ACT.Exp, scale=DECAY).then_inc(exp_done, 1)

            decays(0, 0, first_batch=True)
            for k, (t, h) in enumerate(V_PIECES):
                if t >= 2:
                    act.wait_ge(v_out[t % 2], 16)
                act.wait_ge(v_mm, k + 1)
                act.activation(V[t % 2][:, HALF * h:HALF * h + HALF], pT[k % 2][:, :], ACT.Copy).then_inc(v_ev, 1)

            def body(i, b, last):
                n = 2 * i + b
                for u in range(0 if last else 4):
                    k, cs = u % 2, slice(4 * (u // 2), 4 * (u // 2) + 4)
                    act.wait_ge(pt_full[k], used(n, b, last, TURN + u // 2))
                    act.activation(TK[:, cs, :, k, :], pT[k][:, :].rearrange("p (c e v) -> p c e v", e=2, v=HEAD),
                                   ACT.Copy).then_inc(pt_free[k], 1)
                if last and b:
                    head_norm_roots(act, keep, 0)
                for h in range(2):
                    act.wait_ge(pt_full[h], used(n, b, last, R_SUM))
                    act.activation(RN[:, h, :], pT[h][:, :], ACT.Copy, scale=-1.0).then_inc(pt_free[h], 1)
                    if h == 0 and not (last and b):
                        decays(n + 1, 1 - b, (0, 1))
                if not (last and b):
                    decays(n + 1, 1 - b, (2, 3))
                for lev in range(1, LEVELS):
                    for q in range(QUADS):
                        act.wait_ge(inv_mm[q], STEPS * n + 3 * lev)
                        act.activation(XT[:, 4 * q:4 * q + 4, :].rearrange("p h s -> p (h s)"), pI[q][:, :],
                                       ACT.Copy).then_inc(inv_ev[q], 1)
                rows = slice(HEAD * b, HEAD * b + HEAD)
                for h in range(2):
                    act.wait_ge(pt_full[h], used(n, b, last, U_FIRST))
                    act.activation(UH[b][rows, h, :], pT[h][rows, :], ACT.Copy).then_inc(pt_free[h], 1)
                for h in range(2):
                    act.wait_ge(pt_full[h], used(n, b, last, U_ALL))
                    act.activation(UN[:, h, :], pT[h][:, :], ACT.Copy).then_inc(pt_free[h], 1)

            rolled(act, body)

        @block.tensor
        def _(pe):
            for k in range(2):
                pe.sem_inc(pt_full[k], GIVEN)

            def cumulate(n, b, quarters=range(4), first_batch=False):
                pe.wait_ge(decays_in, 16 * (n + 1))
                for u in quarters:
                    if not first_batch:
                        pe.wait_ge(qb_ev, QUADS * n)
                    if u >= 2:
                        pe.wait_ge(exp_done, 4 * n + u - 1)
                    for c in range(2):
                        last = pe.matmul(pS[u % 2][:, (P + 1) * c:(P + 1) * (c + 1)], IN[:, SW_, P * (2 * u + c):P * (2 * u + c + 1)],
                                         con[:, C_CUM + (P + 1) * b:C_CUM + (P + 1) * (b + 1)], start=True, stop=True)
                    last.then_inc(cum_mm, 1)

            def scores_qb(n, b):
                pe.wait_ge(prep_dve, n + 1)
                pe.wait_ge(prep_b, n + 1)
                for q in range(QUADS):
                    pe.wait_ge(exp_done, 4 * (n + 1))
                    if q >= 2:
                        pe.wait_ge(qb_ev, QUADS * n + q - 1)
                    for k in range(4):
                        j = 4 * q + k
                        mm = pe.matmul(pS[q % 2][:, P * k:P * k + P], B[j % 2][:, j // 2, :], QR[b][:, j // 2, 0, :], start=True, stop=True)
                    mm.then_inc(qb_mm, 1)

            def project_v(pieces):
                for i in pieces:
                    t, h = V_PIECES[i]
                    if i >= 2:
                        pe.wait_ge(v_ev, i - 1)
                    for k in range(DC):
                        w = w_v[0][:, k, :] if h == 0 else w_v[1 + k // 4][:, k % 4, :]
                        mm = pe.matmul(pT[i % 2][:, :], y[:, :, :].rearrange("p t d -> p (t d)")[:, SEQ * k + P * t:SEQ * k + P * t + P], w,
                                       start=k == 0, stop=k == DC - 1)
                    mm.then_inc(v_mm, 1)

            cumulate(0, 0, first_batch=True)
            pe.wait_ge(wv_load[1], 16 * 2)
            project_v(range(2))
            pe.wait_ge(cleared, 9)
            scores_qb(0, 0)
            project_v(range(2, V_SECOND))
            pe.wait_ge(wv_load[0], 16)
            project_v(range(V_SECOND, len(V_PIECES)))
            pe.wait_ge(v_ev, len(V_PIECES))

            def body(i, b, last):
                n = 2 * i + b
                v = V[b][:, :]

                def turn_keys(part):
                    for k in range(2):
                        wait_alone(pe, pt_free[k], used(n, b, last, TURN - 1 + part), pe_tick)
                        rows = slice(HEAD * k, HEAD * k + HEAD)
                        for c in range(4):
                            for e, src in enumerate((B[k], KH[k])):
                                at = HEAD * (2 * c + e)
                                tr = pe.transpose(pT[k][:, at:at + HEAD], src[rows, 4 * part + c, :], con[rows, C_ID + HEAD * k:C_ID + HEAD * k + HEAD])
                        tr.then_inc(pt_full[k], 1)

                pe.wait_ge(prep_pool, n + 1)
                for j in range(HEADS):
                    c, e, bank = j // 2, j % 2, pI[j % QUADS]
                    if j >= QUADS:
                        pe.wait_ge(score_ev, HEADS * n + j - QUADS + 1)
                    pe.matmul(bank[:, 0:P], B[e][:, c, :], QR[b][:, c, 1, :], start=True, stop=True)
                    pe.matmul(bank[:, P:3 * P], KH[e][:, c, :], QR[b][:, c].rearrange("k e s -> k (e s)"),
                              start=True, stop=True).then_inc(score_mm, 1)
                    if j in (5, 11) and not last:
                        turn_keys(j // 6)
                pe.wait_ge(state_ready, n + 1)
                pe.wait_ge(v_in[b], 16 * (i + 1))
                for h in range(2):
                    pe.wait_ge(pt_free[h], used(n, b, last, R_SUM - 1))
                    for c in range(DC):
                        j, at = 2 * c + h, HEAD * c
                        pe.wait_ge(score_ev, HEADS * n + j + 1)
                        pe.matmul(pT[h][:, at:at + HEAD], QR[b][:, c, 0, :], state[:, c, h, :], start=True, stop=False)
                        mm = pe.matmul(pT[h][:, at:at + HEAD], AM[:, j, 1, :], v[:, HEAD * j:HEAD * j + HEAD], start=False, stop=True)
                    mm.then_inc(pt_full[h], 1)
                    if h == 0 and not (last and b):
                        cumulate(n + 1, 1 - b, (0, 1))

                def per_head(q, step, lhsT, rhs):
                    pe.wait_ge(inv_ev[q], STEPS * n + step - 1 + GIVEN)
                    for k in range(4):
                        j = 4 * q + k
                        dst = pI[q][:, P * k:P * k + P]
                        if rhs is None:
                            mm = pe.transpose(dst, lhsT[:, j, :], con[:, C_ID:C_ID + P])
                        else:
                            mm = pe.matmul(dst, lhsT[:, j, :], rhs[:, j, :], start=True, stop=True)
                    mm.then_inc(inv_mm[q], 1)

                pe.wait_ge(base_in, 2 * P * (n + 1))
                for lev in range(1, LEVELS + 1):
                    at = 3 * lev - 2
                    for q in range(QUADS):
                        per_head(q, at, QB[b], X)
                    for q in range(QUADS):
                        if lev < LEVELS:
                            per_head(q, at + 1, XT, W)
                        else:
                            per_head(q, at + 1, W, XT)
                    if not (last and b):
                        if lev == 1:
                            cumulate(n + 1, 1 - b, (2, 3))
                        if lev == LEVELS:
                            scores_qb(n + 1, 1 - b)
                    if lev < LEVELS:
                        for q in range(QUADS):
                            per_head(q, at + 2, X, None)

                def product(use, lhsT, rhs):
                    for quads in ((0, 1, 2), (3,)) if use == U_FIRST else ((0, 1, 2, 3),):
                        for h in range(2):
                            if 0 in quads:
                                pe.wait_ge(pt_free[h], used(n, b, last, use - 1))
                            for q in quads:
                                if use == U_FIRST:
                                    pe.wait_ge(inv_ev[q], STEPS * (n + 1) + GIVEN)
                                for c in (2 * q, 2 * q + 1):
                                    mm = pe.matmul(pT[h][:, HEAD * c:HEAD * c + HEAD], lhsT[:, 2 * c + h, :],
                                                   rhs[:, h, HEAD * c:HEAD * c + HEAD], start=True, stop=True)
                            if 3 in quads:
                                mm.then_inc(pt_full[h], 1)

                product(U_FIRST, XT, RN)
                product(U_CROSS, QB[b], UH[b])
                product(U_ALL, XT, RN)
                for h in range(2):
                    pe.wait_ge(pt_free[h], used(n, b, last, Y_SUM - 1))
                    for c in range(DC):
                        j, at = 2 * c + h, HEAD * c
                        dst = pT[h][:, at:at + HEAD]
                        pe.matmul(dst, QR[b][:, c, 1, :], state[:, c, h, :], start=True, stop=False)
                        pe.matmul(dst, AM[:, j, 2, :], v[:, HEAD * j:HEAD * j + HEAD], start=False, stop=False)
                        mm = pe.matmul(dst, AM[:, j, 0, :], UN[:, h, at:at + HEAD], start=False, stop=True)
                    mm.then_inc(pt_full[h], 1)
                if last:
                    return
                for h in range(2):
                    pe.wait_ge(pt_free[h], used(n, b, last, S_SUM - 1))
                    for k in range(4):
                        c = 4 * h + k
                        dst = pT[h][:, P * k:P * k + P]
                        pe.matmul(dst, TK[:, c, 1].rearrange("p e v -> p (e v)"), v[:, P * c:P * c + P], start=True, stop=False)
                        mm = pe.matmul(dst, TK[:, c, 0].rearrange("p e v -> p (e v)"), UN[:, :, HEAD * c:HEAD * c + HEAD],
                                       start=False, stop=True)
                    mm.then_inc(pt_full[h], 1)

            rolled(pe, body)

        @block.vector
        def _(dve):
            for k in range(2):
                dve.sem_inc(pt_free[k], GIVEN)
            for q in range(QUADS):
                dve.sem_inc(inv_ev[q], GIVEN)
            dve.sem_inc(base_out, GIVEN)
            dve.sem_inc(carried, GIVEN)

            def prep(n, b):
                last_col = 0 if b else P
                dve.wait_ge(exp_done, 4 * n + 4)
                dve.wait_ge(streams_in, STREAM_SUM * (n + 1))
                dve.tensor_tensor(QR[b][:, :, 0, :], IN[:, KK_, :].rearrange("p (c s) -> p c s", s=P), decay[:, :, BEFORE[b]], ALU.mult)
                dve.tensor_tensor(QR[b][:, :, 1, :], IN[:, R_, :].rearrange("p (c s) -> p c s", s=P), decay[:, :, WITH[b]], ALU.mult)
                dve.tensor_copy(p_end[b][:, :], decay[:, :, last_col]).then_inc(prep_dve, 1)

            def mask_qb(n, b):
                at = C_SCORE + 4 * P * b
                for q in range(QUADS):
                    dve.wait_ge(qb_mm, QUADS * n + q + 1)
                    dve.tensor_tensor(QB[b][:, 4 * q:4 * q + 4, :], pS[q % 2][:, :].rearrange("p (h s) -> p h s", s=P),
                                      con[:, at:at + P].unsqueeze(1).to_broadcast([P, 4, P]), ALU.mult).then_inc(qb_ev, 1)

            prep(0, 0)
            mask_qb(0, 0)
            dve.wait_ge(cleared, 9)

            def body(i, b, last):
                n = 2 * i + b
                at = C_SCORE + 4 * P * b + P
                for j in range(HEADS):
                    dve.wait_ge(score_mm, HEADS * n + j + 1)
                    dve.tensor_tensor(AM[:, j].rearrange("p e s -> p (e s)"), pI[j % QUADS][:, 0:3 * P], con[:, at:at + 3 * P],
                                      ALU.mult).then_inc(score_ev, 1)
                    if j == QUADS - 1:
                        dve.wait_ge(carried, n - (1 if last and b else 0) + GIVEN)
                        for e in range(2):
                            rows = slice(HEAD * e, HEAD * e + HEAD)
                            ins = dve.tensor_tensor(state[rows, :, e, :], carry[b][rows, :, :],
                                                    p_mid[b][rows, :].unsqueeze(2).to_broadcast([HEAD, DC, HEAD]), ALU.mult)
                        ins.then_inc(state_ready, 1)
                if last and b:
                    head_norm(dve, keep, 0)
                for lev in range(1, LEVELS + 1):
                    at = C_LEVEL + P * (lev - 1)
                    for q in range(QUADS):
                        dve.wait_ge(inv_mm[q], STEPS * n + 3 * lev - 2)
                        dve.tensor_tensor(W[:, 4 * q:4 * q + 4, :], pI[q][:, :].rearrange("p (h s) -> p h s", s=P),
                                          con[:, at:at + P].unsqueeze(1).to_broadcast([P, 4, P]), ALU.mult).then_inc(inv_ev[q], 1)
                    for q in range(QUADS):
                        dve.wait_ge(inv_mm[q], STEPS * n + 3 * lev - 1)
                        into = (X if lev < LEVELS else XT)[:, 4 * q:4 * q + 4, :].rearrange("p h s -> p (h s)")
                        dve.tensor_tensor(into, into, pI[q][:, :], ALU.add).then_inc(inv_ev[q], 1)
                    if not (last and b):
                        if lev == 1:
                            prep(n + 1, 1 - b)
                        if lev == LEVELS:
                            mask_qb(n + 1, 1 - b)
                if last and b:
                    scale_and_add(dve, keep, 0, V[0][:, :])
                rows = slice(HEAD * (1 - b), HEAD * (1 - b) + HEAD)
                for h in range(2):
                    dve.wait_ge(pt_full[h], used(n, b, last, U_CROSS))
                    dve.tensor_tensor(RN[rows, h, :], RN[rows, h, :], pT[h][rows, :], ALU.add).then_inc(pt_free[h], 1)
                dve.wait_ge(y_cleared, 1)
                for h in range(2):
                    wait_alone(dve, pt_full[h], used(n, b, last, Y_SUM), dve_tick)
                    cols = y[:, bass.ds(chunk(i, b), 1), :].rearrange("p a (c e v) -> p (a c) e v", e=2, v=HEAD)[:, :, h, :]
                    dve.tensor_tensor(cols, cols, pT[h][:, :].rearrange("p (c v) -> p c v", v=HEAD), ALU.add).then_inc(pt_free[h], 1)
                if last:
                    return
                for h in range(2):
                    dve.wait_ge(pt_full[h], USES * (n + 1) + GIVEN)
                    for e in range(2):
                        rows, cs = slice(HEAD * e, HEAD * e + HEAD), slice(4 * h, 4 * h + 4)
                        ins = dve.tensor_tensor(carry[b][rows, cs, :], state[rows, cs, e, :],
                                                pT[h][rows, :].rearrange("p (c e v) -> p c e v", e=2, v=HEAD)[:, :, e, :], ALU.add)
                    ins.then_inc(pt_free[h], 1)
                for h in range(2):
                    dve.wait_ge(pt_free[h], USES * (n + 1) + GIVEN)
                dve.tensor_tensor(carry[b][:, :, :], carry[b][:, :, :], p_end[b][:, :].unsqueeze(2).to_broadcast([P, DC, HEAD]),
                                  ALU.mult).then_inc(carried, 1)

            rolled(dve, body)


WEIGHT_BLOCKS = 6
RING = 4


def weight_block(io, expert, m):
    half = slice(D * (m // 2), D * (m // 2) + D) if m < 4 else slice(D * (m - 4), D * (m - 4) + D)
    if m < 4:
        w = io["exp_w_gate" if m % 2 == 0 else "exp_w_up"]
        return w[0, bass.ds(expert, 1), :, half].rearrange("a (c p) f -> p (a c) f", p=P)
    return io["exp_w_down"][0, bass.ds(expert, 1), half, :].rearrange("a (c p) d -> p (a c) d", p=P)


def load_half_block(sp, io, keep, expert, m, slot, half):
    ks = slice(DC // 2 * half, DC // 2 * half + DC // 2)
    sp.dma_start(keep["ring"][slot][:, ks, :], weight_block(io, expert, m)[:, ks, :]).then_inc(keep["landed"][slot][half], 16)


def mix_output(nc, io, scr, keep):
    con, y, res, bonus = keep["con"], keep["y"], keep["res"], keep["bonus"]
    ident = con[:, C_ID:C_ID + P]
    with ExitStack() as ctx:
        def sb(name, *shape):
            return ctx.enter_context(nc.sbuf_tensor(name, list(shape), F32))

        def sem(name):
            return ctx.enter_context(nc.semaphore(name))

        w_out = keep["ring"][2]
        lent = keep["ring"][3]
        rows = lent[:, 0:3, :]
        g2, v_in, unread = keep["g2"], lent[:, 4:6, :], lent[:, 7, :]
        keep["squares"], keep["lnx_g"], keep["lnx_b"] = lent[:, 6, :], rows[:, 0, :], rows[:, 1, :]
        w_router = sb("w_router", P, DC, EXPERTS)
        turned_in = sb("turned_in", P, DC, P)
        h2T = sb("h2T", P, DC, P)
        stat = sb("mo_stat", P, 4, TILES)
        prob = sb("prob", P, TILES, EXPERTS)
        soft = sb("soft", P, 3, TILES)
        affT, work = sb("affT", EXPERTS, SEQ), sb("work", EXPERTS, 2, SEQ)
        top8 = sb("top8", EXPERTS, 2, 8)
        mask = sb("mask", P, TILES, EXPERTS)
        ps = [ctx.enter_context(nc.psum_tensor(f"mo_ps{i}", [P, HALF], F32)) for i in range(8)]

        v_load = [sem(f"mo_v_load{k}") for k in range(2)]
        router_load, x_load = sem("router_load"), sem("mo_x_load")
        gate_mm, gated = sem("gate_mm"), sem("gated")
        turn1, turn1_ev, out_mm, added = sem("turn1"), sem("turn1_ev"), sem("out_mm"), sem("added")
        res_squared, res_mean, res_root = sem("res_squared"), sem("res_mean"), sem("res_root")
        h2_done, turn2, turn2_ev, logit_mm = sem("h2_done"), sem("turn2"), sem("turn2_ev"), sem("logit_mm")
        shifted, exped, prob_done = sem("shifted"), sem("exped"), sem("prob_done")
        aff_turn, mask_done, mask_turn, mask_ev, count_mm = (sem(n) for n in ("aff_turn", "mask_done", "mask_turn", "mask_ev", "count_mm"))
        block = ctx.enter_context(nc.Block())

        @block.sync
        def _(sp):
            def load_block(m):
                for half in range(2):
                    load_half_block(sp, io, keep, 0, m, m, half)

            def load_v(t):
                if t >= 3:
                    sp.wait_ge(gated, 2 * (t - 1))
                sp.dma_start(v_in[:, t % 2, :], scr["v"][TILE_ORDER[t]]).then_inc(v_load[t % 2], 16)

            load_v(1)
            for name in ("lnx_g", "lnx_b"):
                sp.dma_start(keep[name], io[f"rw_{name}"][0].partition_broadcast(P)).then_inc(keep["lnx_load"], 16)
            sp.dma_start(rows[:, 2, :], io["norm_ffn_g"][0].partition_broadcast(P)).then_inc(x_load, 16)
            sp.dma_start(res[:, :, :], io["x"].rearrange("b (t p) d -> p (b t) d", p=P)).then_inc(x_load, 16)
            sp.dma_start(w_router[:, :, :], io["router_w"][0].rearrange("(c p) e -> p c e", p=P)).then_inc(router_load, 16)
            load_v(2)
            load_block(0)
            load_v(3)
            load_block(1)
            sp.wait_ge(out_mm, 2 * TILES)
            load_block(2)
            sp.wait_ge(h2_done, TILES)
            load_block(3)

        @block.gpsimd
        def _(pool):
            for t in range(1, TILES):
                pool.wait_ge(v_load[t % 2], 16 * ((t + 1) // 2))
                add_bonus(pool, keep, t, v_in[:, t % 2, :])

        @block.scalar
        def _(act):
            def first(t):
                if t:
                    head_norm_roots(act, keep, t)
                    act.wait_ge(out_mm, 2 * t)
                for g in range(2):
                    act.wait_ge(turn1, 2 * t + g + 1)
                    act.activation(turned_in[:, 4 * g:4 * g + 4, :].rearrange("p c s -> p (c s)"), ps[2 + g][:, :], ACT.Copy).then_inc(turn1_ev, 1)

            def second(t):
                act.wait_ge(added, 2 * t + 2)
                act.activation(unread, res[:, TILE_ORDER[t], :], ACT.Square, accum_out=stat[:, 0, t:t + 1]).then_inc(res_squared, 1)
                act.wait_ge(res_mean, t + 1)
                act.activation(stat[:, 2, t:t + 1], stat[:, 1, t:t + 1], ACT.Sqrt).then_inc(res_root, 1)
                if t:
                    act.wait_ge(logit_mm, t)
                for g in range(2):
                    act.wait_ge(turn2, 2 * t + g + 1)
                    act.activation(h2T[:, 4 * g:4 * g + 4, :].rearrange("p c s -> p (c s)"), ps[2 + g][:, :], ACT.Copy).then_inc(turn2_ev, 1)

            first(0)
            for t in range(1, TILES):
                first(t)
                second(t - 1)
            second(TILES - 1)
            act.wait_ge(shifted, 1)
            flat = prob[:, :, :].rearrange("p t e -> p (t e)")
            act.activation(flat, flat, ACT.Exp).then_inc(exped, 1)

        @block.tensor
        def _(pe):
            def gate(t):
                for h in range(2):
                    if t:
                        pe.wait_ge(gated, 2 * (t - 1) + h + 1)
                    pe.matmul(ps[h][:, :], keep["gate_low"][:, P * TILE_ORDER[t]:P * TILE_ORDER[t] + P], g2[:, HALF * h:HALF * h + HALF],
                              start=True, stop=True).then_inc(gate_mm, 1)

            def turn(t, turned):
                for g in range(2):
                    for c in range(4):
                        k = 4 * g + c
                        mm = pe.transpose(ps[2 + g][:, P * c:P * c + P], y[:, TILE_ORDER[t], P * k:P * k + P], ident)
                    mm.then_inc(turned, 1)

            def project(t, h):
                if t:
                    pe.wait_ge(added, 2 * (t - 1) + h + 1)
                for c in range(DC):
                    mm = pe.matmul(ps[4 + h][:, :], turned_in[:, c, :], w_out[:, c, HALF * h:HALF * h + HALF], start=c == 0, stop=c == DC - 1)
                mm.then_inc(out_mm, 1)

            def turn_h2(t):
                pe.wait_ge(h2_done, t + 1)
                turn(t, turn2)

            def logits(t):
                pe.wait_ge(turn2_ev, 2 * t + 2)
                for c in range(DC):
                    mm = pe.matmul(ps[6][:, EXPERTS * TILE_ORDER[t]:EXPERTS * TILE_ORDER[t] + EXPERTS], h2T[:, c, :], w_router[:, c, :], start=c == 0, stop=c == DC - 1)
                mm.then_inc(logit_mm, 1)

            pe.wait_ge(keep["g2_load"], 16)
            gate(0)
            for t in range(TILES):
                pe.wait_ge(gated, 2 * t + 2)
                if t >= 2:
                    pe.wait_ge(turn2_ev, 2 * (t - 1))
                turn(t, turn1)
                if t + 1 < TILES:
                    gate(t + 1)
                pe.wait_ge(turn1_ev, 2 * t + 2)
                if t == 0:
                    pe.wait_ge(keep["w_out_load"], 16)
                project(t, 0)
                if t:
                    turn_h2(t - 1)
                project(t, 1)
                if t:
                    if t == 1:
                        pe.wait_ge(router_load, 16)
                    logits(t - 1)
            turn_h2(TILES - 1)
            logits(TILES - 1)
            pe.wait_ge(prob_done, 1)
            for t in range(TILES):
                mm = pe.transpose(ps[7][0:EXPERTS, P * t:P * t + P], keep["aff"][:, t, :], ident)
            mm.then_inc(aff_turn, 1)
            pe.wait_ge(mask_done, 1)
            for t in range(TILES):
                mm = pe.transpose(ps[6][:, EXPERTS * t:EXPERTS * t + EXPERTS], affT[:, P * t:P * t + P], ident[0:EXPERTS, 0:EXPERTS])
            mm.then_inc(mask_turn, 1)
            pe.wait_ge(mask_ev, 1)
            pe.matmul(ps[7][:, 0:TILES * EXPERTS], con[:, C_TRI:C_TRI + P], mask[:, :, :].rearrange("p t e -> p (t e)"), start=True, stop=False)
            for t in range(TILES - 1):
                later = ps[7][:, EXPERTS * (t + 1):EXPERTS * TILES].rearrange("p (t e) -> p t e", e=EXPERTS)
                mm = pe.matmul(later, con[:, C_ONES:C_ONES + P], mask[:, t:t + 1, :].to_broadcast([P, TILES - 1 - t, EXPERTS]),
                               start=False, stop=t == TILES - 2)
            mm.then_inc(count_mm, 1)

        @block.vector
        def _(dve):
            chain = keep["chain"]

            def first(t):
                yt = y[:, TILE_ORDER[t], :]
                if t:
                    head_norm(dve, keep, t)
                    scale_and_add(dve, keep, t, v_in[:, t % 2, :])
                for h in range(2):
                    cols = slice(HALF * h, HALF * h + HALF)
                    dve.wait_ge(gate_mm, 2 * t + h + 1)
                    dve.tensor_tensor(yt[:, cols], yt[:, cols], ps[h][:, :], ALU.mult).then_inc(gated, 1)

            def second(t):
                rest = res[:, TILE_ORDER[t], :]
                if t == 0:
                    dve.wait_ge(x_load, 16 * 2)
                for h in range(2):
                    cols = slice(HALF * h, HALF * h + HALF)
                    dve.wait_ge(out_mm, 2 * t + h + 1)
                    dve.tensor_tensor(rest[:, cols], rest[:, cols], ps[4 + h][:, :], ALU.add).then_inc(added, 1)
                dve.wait_ge(res_squared, t + 1)
                dve.tensor_scalar(stat[:, 1, t:t + 1], stat[:, 0, t:t + 1], 1.0 / D, EPS, ALU.mult, ALU.add).then_inc(res_mean, 1)
                dve.wait_ge(res_root, t + 1)
                chain.link(dve.reciprocal(stat[:, 3, t:t + 1], stat[:, 2, t:t + 1]))
                dve.scalar_tensor_tensor(out=y[:, TILE_ORDER[t], :], in0=rest, scalar=stat[:, 3, t:t + 1], in1=rows[:, 2, :],
                                         op0=ALU.mult, op1=ALU.mult).then_inc(h2_done, 1)

            def spread_soft(i):
                return soft[:, i, :].unsqueeze(2).to_broadcast([P, TILES, EXPERTS])

            first(0)
            for t in range(1, TILES):
                first(t)
                second(t - 1)
            second(TILES - 1)
            dve.wait_ge(logit_mm, TILES)
            logits = ps[6][:, 0:TILES * EXPERTS].rearrange("p (t e) -> p t e", e=EXPERTS)
            chain.link(dve.tensor_reduce(soft[:, 0, :], logits, AX_X, ALU.max))
            dve.tensor_tensor(prob[:, :, :], logits, spread_soft(0), ALU.subtract).then_inc(shifted, 1)
            dve.wait_ge(exped, 1)
            chain.link(dve.tensor_reduce(soft[:, 1, :], prob[:, :, :], AX_X, ALU.add))
            chain.link(dve.reciprocal(soft[:, 2, :], soft[:, 1, :]))
            dve.tensor_tensor(keep["aff"][:, :, :], prob[:, :, :], spread_soft(2), ALU.mult).then_inc(prob_done, 1)
            dve.wait_ge(aff_turn, 1)
            chain.link(dve.tensor_copy(work[:, 0, :], ps[7][0:EXPERTS, :]))
            for r in range(CAP // 8):
                chain.link(dve.max(top8[:, r % 2, :], work[:, r % 2, :]))
                chain.link(dve.match_replace(work[:, (r + 1) % 2, :], top8[:, r % 2, :], work[:, r % 2, :], -1.0))
            dve.tensor_scalar(affT[:, :], work[:, 0, :], 0.0, None, ALU.is_lt).then_inc(mask_done, 1)
            dve.wait_ge(mask_turn, 1)
            dve.tensor_copy(mask[:, :, :].rearrange("p t e -> p (t e)"), ps[6][:, 0:TILES * EXPERTS]).then_inc(mask_ev, 1)
            dve.wait_ge(mask_ev, 1)
            dve.wait_ge(count_mm, 1)
            slot = keep["slot"][:, :, :].rearrange("p t e -> p (t e)")
            chain.link(dve.tensor_tensor(slot, ps[7][:, 0:TILES * EXPERTS], mask[:, :, :].rearrange("p t e -> p (t e)"), ALU.mult))


def experts(nc, io, keep, out):
    con, h2, res, ring, landed = keep["con"], keep["y"], keep["res"], keep["ring"], keep["landed"]
    ident = con[:, C_ID:C_ID + P]
    with ExitStack() as ctx:
        def sb(name, *shape):
            return ctx.enter_context(nc.sbuf_tensor(name, list(shape), F32))

        def sem(name):
            return ctx.enter_context(nc.semaphore(name))

        pick = sb("pick", P, TILES, 2, CAP)
        gated_pick = sb("gated_pick", P, TILES, 2, CAP)
        scatter = sb("scatter", P, SEQ)
        xin = sb("xin", P, DC, 2, CAP)
        silu = sb("silu", P, HALF)
        hid = sb("hid", P, 2, HALF)
        hidT = sb("hidT", P, 2, 4, P)
        yexp = sb("yexp", P, D)
        pG, pU = (ctx.enter_context(nc.psum_tensor(n, [P, HALF], F32)) for n in ("pG", "pU"))
        pD, pX, pO = ([ctx.enter_context(nc.psum_tensor(f"{n}{i}", [P, HALF], F32)) for i in range(2)] for n in ("pD", "pX", "pO"))

        picked, gate_picked = sem("picked"), sem("gate_picked")
        gath_mm, gath_ev = sem("gath_mm"), sem("gath_ev")
        scat_turn, scat_ev = sem("scat_turn"), sem("scat_ev")
        gate_mm, up_mm, silu_done, hid_done = sem("e_gate_mm"), sem("up_mm"), sem("silu_done"), sem("e_hid_done")
        hid_turn, hid_ev = sem("hid_turn"), sem("hid_ev")
        down_mm, down_ev = sem("down_mm"), sem("down_ev")
        scat_mm, scat_add = sem("scat_mm"), sem("scat_add")
        row_load, norm_squared, norm_mean, norm_root, normed, stored = (
            sem(f"final_{n}") for n in ("row_load", "squared", "mean", "root", "normed", "stored"))
        sp_tick = keep["sp_tick"]
        norm_row = hid[:, :, :].rearrange("p j f -> p (j f)")
        unread = xin[:, :, :, :].rearrange("p c e s -> p (c e s)")
        DONE = 2 * TILES * (EXPERTS - 1) + GIVEN
        EARLY = slice(0, TILES - 1)
        norm_stat = sb("norm_stat", P, 4, TILES)
        out_t = out.rearrange("b (t p) d -> (b t) p d", p=P)
        PAIRS = EXPERTS // 2
        PER = 2 * WEIGHT_BLOCKS
        TURNS = PER // RING

        block = ctx.enter_context(nc.Block())

        @block.sync
        def _(sp):
            def body(i, last):
                for m in range(RING, PER if last else PER + RING):
                    slot = m % RING
                    e = 2 * i + m // WEIGHT_BLOCKS
                    before = m - RING
                    n, kind = 2 * i + before // WEIGHT_BLOCKS, before % WEIGHT_BLOCKS
                    for half in range(2):
                        if kind < 4:
                            wait_alone(sp, (gate_mm, up_mm)[kind % 2], 4 * n + 2 * (kind // 2) + half + 1, sp_tick)
                        else:
                            wait_alone(sp, down_mm, 4 * n + 2 * (kind - 4) + half + 1, sp_tick)
                        load_half_block(sp, io, keep, e, m % WEIGHT_BLOCKS, slot, half)

            with sp.Fori(0, PAIRS - 1) as i:
                body(i, False)
            body(PAIRS - 1, True)
            sp.wait_ge(hid_turn, 2 * EXPERTS + GIVEN)
            sp.dma_start(norm_row, io["final_norm_g"].partition_broadcast(P)).then_inc(row_load, 16)
            for t in range(TILES):
                sp.wait_ge(normed, t + 1)
                sp.dma_start(out_t[t], res[:, t, :]).then_inc(stored, 16)
            sp.wait_ge(stored, 16 * TILES)

        @block.tensor
        def _(pe):
            for given in (gath_mm, scat_turn, hid_turn):
                pe.sem_inc(given, GIVEN)

            def body(i):
                def half_block(e, m, half):
                    n = WEIGHT_BLOCKS * e + m
                    slot = n % RING
                    pe.wait_ge(landed[slot][half], 16 * (TURNS * i + n // RING + 1))
                    return ring[slot]

                def gather(g):
                    pe.wait_ge(gath_ev, 2 * i + GIVEN)
                    pe.wait_ge(scat_ev, 2 * i + GIVEN)
                    pe.wait_ge(hid_ev, 4 * i + GIVEN)
                    for c in range(4):
                        k = 4 * g + c
                        for t in range(TILES):
                            mm = pe.matmul(pX[g][:, P * c:P * c + P], h2[:, t, P * k:P * k + P],
                                           pick[:, t].rearrange("p e s -> p (e s)"), start=t == 0, stop=t == TILES - 1)
                    mm.then_inc(gath_mm, 1)

                pe.wait_ge(picked, i + 1)
                gather(0)
                for e in range(2):
                    n = 2 * i + e

                    def up_down(which, psum, m):
                        for half in range(2):
                            w = half_block(e, m, half)
                            if e == 0 and m == 0:
                                if half == 1:
                                    gather(1)
                                pe.wait_ge(gath_ev, 2 * i + half + 1 + GIVEN)
                            for k in range(DC // 2 * half, DC // 2 * half + DC // 2):
                                for s in range(2):
                                    mm = pe.matmul(psum[HEAD * s:HEAD * s + HEAD, :], xin[:, k, e, :], w[:, k, :].rearrange("p (c s f) -> p c s f", s=2, f=P)[:, :, s, :],
                                                   start=k == 0, stop=k == DC - 1)
                            mm.then_inc(which, 1)

                    def turn(j):
                        pe.wait_ge(hid_done, 2 * n + j + 1 + GIVEN)
                        for c in range(4):
                            mm = pe.transpose(pX[j][:, P * c:P * c + P], hid[:, j, P * c:P * c + P], ident)
                        mm.then_inc(hid_turn, 1)

                    def down(j):
                        pe.wait_ge(hid_ev, 2 * n + j + 1 + GIVEN)
                        if j == 0:
                            pe.wait_ge(down_ev, 2 * n + GIVEN)
                        for half in range(2):
                            w = half_block(e, 4 + j, half)
                            for c in (2 * half, 2 * half + 1):
                                for h in range(2):
                                    for s in range(2):
                                        mm = pe.matmul(pD[h][HEAD * s:HEAD * s + HEAD, :], hidT[:, j, c, HEAD * s:HEAD * s + HEAD],
                                                       w[:, 2 * c + s, HALF * h:HALF * h + HALF], start=j == 0 and c == 0, stop=j == 1 and c == 3)
                            mm.then_inc(down_mm, 1)

                    pe.wait_ge(silu_done, 2 * n + GIVEN)
                    up_down(gate_mm, pG, 0)
                    pe.wait_ge(gate_picked, n + 1 + GIVEN)
                    for t in range(TILES):
                        mm = pe.transpose(pX[0][:, P * t:P * t + P], gated_pick[:, t].rearrange("p e s -> p (e s)"), ident)
                    mm.then_inc(scat_turn, 1)
                    pe.wait_ge(hid_done, 2 * n + GIVEN)
                    up_down(up_mm, pU, 1)
                    pe.wait_ge(silu_done, 2 * n + 1 + GIVEN)
                    up_down(gate_mm, pG, 2)
                    pe.wait_ge(scat_ev, n + 1 + GIVEN)
                    turn(0)
                    up_down(up_mm, pU, 3)
                    down(0)
                    turn(1)
                    down(1)
                    pe.wait_ge(down_ev, 2 * n + 2 + GIVEN)
                    for u in range(2 * TILES):
                        t, h = u // 2, u % 2
                        if u >= 2:
                            pe.wait_ge(scat_add, 2 * TILES * n + u - 1 + GIVEN)
                        else:
                            pe.wait_ge(scat_add, 2 * TILES * n + GIVEN)
                        pe.matmul(pO[h][:, :], scatter[:, P * t:P * t + P], yexp[:, HALF * h:HALF * h + HALF], start=True,
                                  stop=True).then_inc(scat_mm, 1)

            with pe.Fori(0, PAIRS) as i:
                body(i)

        @block.scalar
        def _(act):
            for given in (gath_ev, scat_ev, hid_ev, silu_done, down_ev):
                act.sem_inc(given, GIVEN)

            def body(i):
                for g in range(2):
                    act.wait_ge(gath_mm, 2 * i + g + 1 + GIVEN)
                    act.activation(xin[:, 4 * g:4 * g + 4].rearrange("p c e s -> p (c e s)"), pX[g][:, :], ACT.Copy).then_inc(gath_ev, 1)
                for e in range(2):
                    n = 2 * i + e
                    for j in range(2):
                        act.wait_ge(gate_mm, 4 * n + 2 * j + 2)
                        act.wait_ge(hid_done, 2 * n + j + GIVEN)
                        act.activation(silu[:, :], pG[:, :], ACT.Silu).then_inc(silu_done, 1)
                        if j == 0:
                            act.wait_ge(scat_turn, n + 1 + GIVEN)
                            act.activation(scatter[:, :], pX[0][:, :], ACT.Copy).then_inc(scat_ev, 1)
                    for j in range(2):
                        act.wait_ge(hid_turn, 2 * n + j + 1 + GIVEN)
                        act.activation(hidT[:, j].rearrange("p c s -> p (c s)"), pX[j][:, :], ACT.Copy).then_inc(hid_ev, 1)
                    act.wait_ge(down_mm, 4 * n + 4)
                    for h in range(2):
                        act.activation(yexp[:, HALF * h:HALF * h + HALF], pD[h][:, :], ACT.Copy).then_inc(down_ev, 1)

            with act.Fori(0, PAIRS) as i:
                body(i)

            for t in range(TILES):
                act.wait_ge(scat_add, DONE + 2 * t + 2)
                if t:
                    act.wait_ge(norm_squared, t)
                act.activation(unread, res[:, t, :], ACT.Square, accum_out=norm_stat[:, 0, t:t + 1]).then_inc(norm_squared, 1)
                if t == TILES - 2:
                    act.wait_ge(norm_mean, 1)
                    act.activation(norm_stat[:, 2, EARLY], norm_stat[:, 1, EARLY], ACT.Sqrt).then_inc(norm_root, 1)
            act.wait_ge(norm_mean, 2)
            act.activation(norm_stat[:, 2, TILES - 1:TILES], norm_stat[:, 1, TILES - 1:TILES], ACT.Sqrt).then_inc(norm_root, 1)

        @block.vector
        def _(dve):
            for given in (hid_done, scat_add, gate_picked):
                dve.sem_inc(given, GIVEN)

            iota = con[:, C_IOTA:C_IOTA + CAP]

            def body(i):
                dve.wait_ge(gath_mm, 2 * i + GIVEN)
                dve.wait_ge(gate_picked, 2 * i + GIVEN)
                dve.tensor_tensor(pick[:, :, :, :], iota.unsqueeze(1).unsqueeze(1).to_broadcast([P, TILES, 2, CAP]),
                                  keep["slot"][:, :, bass.ds(2 * i, 2)].unsqueeze(3).to_broadcast([P, TILES, 2, CAP]),
                                  ALU.is_equal).then_inc(picked, 1)
                dve.wait_ge(picked, i + 1)
                for e in range(2):
                    n = 2 * i + e
                    dve.wait_ge(scat_turn, n + GIVEN)
                    dve.tensor_tensor(gated_pick[:, :, :, :], pick[:, :, e:e + 1, :].to_broadcast([P, TILES, 2, CAP]),
                                      keep["aff"][:, :, bass.ds(n, 1)].unsqueeze(3).to_broadcast([P, TILES, 2, CAP]),
                                      ALU.mult).then_inc(gate_picked, 1)
                    for j in range(2):
                        dve.wait_ge(silu_done, 2 * n + j + 1 + GIVEN)
                        dve.wait_ge(up_mm, 4 * n + 2 * j + 2)
                        dve.wait_ge(hid_turn, 2 * n + GIVEN)
                        dve.tensor_tensor(hid[:, j, :], silu[:, :], pU[:, :], ALU.mult).then_inc(hid_done, 1)
                    for u in range(2 * TILES):
                        t, h = u // 2, u % 2
                        dve.wait_ge(scat_mm, 2 * TILES * n + u + 1)
                        cols = res[:, t, HALF * h:HALF * h + HALF]
                        dve.tensor_tensor(cols, cols, pO[h][:, :], ALU.add).then_inc(scat_add, 1)

            with dve.Fori(0, PAIRS) as i:
                body(i)

            for k, (ts, tiles) in enumerate(((EARLY, range(TILES - 1)), (slice(TILES - 1, TILES), (TILES - 1,)))):
                dve.wait_ge(norm_squared, tiles[-1] + 1)
                dve.tensor_scalar(norm_stat[:, 1, ts], norm_stat[:, 0, ts], 1.0 / D, EPS, ALU.mult, ALU.add).then_inc(norm_mean, 1)
                dve.wait_ge(norm_root, k + 1)
                keep["chain"].link(dve.reciprocal(norm_stat[:, 3, ts], norm_stat[:, 2, ts]))
                dve.wait_ge(row_load, 16)
                for t in tiles:
                    dve.scalar_tensor_tensor(out=res[:, t, :], in0=res[:, t, :], scalar=norm_stat[:, 3, t:t + 1], in1=norm_row,
                                             op0=ALU.mult, op1=ALU.mult).then_inc(normed, 1)


_INS = ["x", "norm_ffn_g", "router_w", "exp_w_gate", "exp_w_up", "exp_w_down", "final_norm_g", "rw_w_in", "rw_w0", "rw_w1",
        "rw_w2", "rw_a1", "rw_a2", "rw_g1", "rw_g2", "rw_lnx_g", "rw_lnx_b", "rw_w_out"]


def kernel(**inputs):
    import concourse.bacc as bacc
    from concourse.bass_utils import run_bass_kernel_spmd

    nc = bacc.Bacc("TRN2", target_bir_lowering=False, num_devices=1)
    arrays, io = {}, {}

    def give(name, a):
        a = np.ascontiguousarray(a)
        arrays[f"in_{name}"] = a
        io[name] = nc.dram_tensor(f"in_{name}", a.shape, mybir.dt.from_np(a.dtype), kind="ExternalInput").ap()

    for name in _INS:
        give(name, inputs[name])
    rows = np.concatenate([np.asarray(inputs[n]).reshape(-1, D)
                           for n in ("norm_mix_g", "rw_mu", "rw_a0", "rw_k_k", "rw_k_a", "rw_r_k")], axis=0)
    give("vectors", rows.reshape(V_END, DC, P).transpose(2, 0, 1))
    give("consts", constants())
    out = nc.dram_tensor("out", (1, SEQ, D), F32, kind="ExternalOutput").ap()
    build_trunk(nc, io, out)
    r = run_bass_kernel_spmd(nc, [arrays], core_ids=[0])
    return r.results[0]["out"]
```
